# Optimizing a Trainium2 kernel written in Bass

```python
import math
import jax, jax.numpy as jnp
from jax import lax
import numpy as np

D_MODEL = 1024
BATCH = 1
SEQ = 1024
DEPTH = 2
DEC_BATCH = 8
DEC_SEQ = 1
PAST_LEN = 1024
PAGE_SIZE = 128

S5_WIDTH = D_MODEL // 2
S5_GROUP = 16
S5_GROUPS = S5_WIDTH // S5_GROUP
S5_STATE = 64
MLSTM_WIDTH = D_MODEL - S5_WIDTH
MLSTM_HEAD_DIM = 128
MLSTM_HEADS = MLSTM_WIDTH // MLSTM_HEAD_DIM
MLSTM_CHUNK = 64
ATT_HEAD_DIM = 128
ATT_HEADS = D_MODEL // ATT_HEAD_DIM
ATT_KV_HEADS = 2
ATT_GROUP = ATT_HEADS // ATT_KV_HEADS
ATT_WIDTH = ATT_HEADS * ATT_HEAD_DIM
IDX_HEADS = 8
IDX_DIM = 64
TOPK_MAX = 256
Q_BLOCK = 128
D_FF = 4 * D_MODEL
EPS = 1e-6

IN0_SIZES = (S5_WIDTH, MLSTM_WIDTH, MLSTM_WIDTH, MLSTM_WIDTH, MLSTM_WIDTH, MLSTM_HEADS, MLSTM_HEADS)
IN1_SIZES = (ATT_WIDTH, ATT_KV_HEADS * ATT_HEAD_DIM, ATT_KV_HEADS * ATT_HEAD_DIM, IDX_HEADS * IDX_DIM, IDX_DIM, IDX_HEADS)
IN0_WIDTH = sum(IN0_SIZES)
IN1_WIDTH = sum(IN1_SIZES)

kernel_name = "hybrid_s5_mlstm_dsa_decoder_step"

def split_cols(z, sizes):
    out, start = [], 0
    for s in sizes:
        out.append(z[..., start:start + s])
        start += s
    return out

def rms_norm(x, g):
    xf = x.astype(jnp.float32)
    y = xf * lax.rsqrt(jnp.mean(xf * xf, axis=-1, keepdims=True) + EPS)
    return (y * g.astype(jnp.float32)).astype(x.dtype)

def sq_relu_mlp(x, w_up, w_down):
    h = jax.nn.relu(x @ w_up)
    return (h * h) @ w_down

def s5_scan(u, h_re, h_im, lam_re, lam_im, log_dt, b_re, b_im, c_re, c_im, d_skip, w_glu, b_glu):
    f32 = jnp.float32
    bsz, t, _ = u.shape
    uf = u.astype(f32)
    lam = lax.complex(lam_re.astype(f32), lam_im.astype(f32))
    dt = jnp.exp(log_dt.astype(f32))[:, None]
    lam_bar = jnp.exp(lam * dt)
    b_bar = ((lam_bar - 1.0) / lam)[..., None] * lax.complex(b_re.astype(f32), b_im.astype(f32))
    ug = uf.reshape(bsz, t, S5_GROUPS, S5_GROUP).astype(jnp.complex64)
    bu = jnp.einsum('gpc,btgc->btgp', b_bar, ug)
    h0 = lax.complex(h_re.astype(f32), h_im.astype(f32))
    bu = bu.at[:, 0].add(lam_bar * h0)
    a = jnp.broadcast_to(lam_bar, bu.shape)

    def combine(l, r):
        a_l, b_l = l
        a_r, b_r = r
        return a_l * a_r, a_r * b_l + b_r

    _, hs = lax.associative_scan(combine, (a, bu), axis=1)
    c = lax.complex(c_re.astype(f32), c_im.astype(f32))
    y = jnp.einsum('gcp,btgp->btgc', c, hs).real.reshape(bsz, t, S5_WIDTH) + d_skip.astype(f32) * uf
    y = jax.nn.gelu(y)
    y = y * jax.nn.sigmoid(y @ w_glu.astype(f32) + b_glu.astype(f32))
    h_last = hs[:, -1]
    return y.astype(u.dtype), jnp.real(h_last).astype(h_re.dtype), jnp.imag(h_last).astype(h_im.dtype)

def mlstm_chunkwise(q, k, v, i_pre, f_pre, c0, n0, m0):
    f32 = jnp.float32
    bsz, t, nh, dh = q.shape
    ch = MLSTM_CHUNK if t % MLSTM_CHUNK == 0 else t
    nc = t // ch

    def to_chunks(z):
        z = z.astype(f32).reshape((bsz, nc, ch) + z.shape[2:])
        return jnp.swapaxes(jnp.moveaxis(z, 1, 0), 2, 3)

    qc, kc, vc = to_chunks(q), to_chunks(k) * (dh ** -0.5), to_chunks(v)
    ic = to_chunks(i_pre)
    lfc = jax.nn.log_sigmoid(to_chunks(f_pre))
    causal = jnp.tril(jnp.ones((ch, ch), dtype=bool))

    def step(carry, inp):
        c, n, m = carry
        qj, kj, vj, ij, lfj = inp
        b = jnp.cumsum(lfj, axis=-1)
        dmat = jnp.where(causal, b[..., :, None] - b[..., None, :] + ij[..., None, :], -jnp.inf)
        a = b + m[..., None]
        mj = jnp.maximum(a, jnp.max(dmat, axis=-1))
        w_intra = jnp.exp(dmat - mj[..., None])
        w_inter = jnp.exp(a - mj)
        s = jnp.einsum('bhtd,bhsd->bhts', qj, kj) * w_intra
        num = jnp.einsum('bhts,bhsd->bhtd', s, vj) + w_inter[..., None] * jnp.einsum('bhtk,bhkv->bhtv', qj, c)
        den = jnp.sum(s, axis=-1) + w_inter * jnp.einsum('bhtk,bhk->bht', qj, n)
        h = num / jnp.maximum(jnp.abs(den), jnp.exp(-mj))[..., None]
        m_new = mj[..., -1]
        w_end = jnp.exp(b[..., -1:] - b + ij - m_new[..., None])
        decay = jnp.exp(b[..., -1] + m - m_new)
        c_new = decay[..., None, None] * c + jnp.einsum('bhs,bhsk,bhsv->bhkv', w_end, kj, vj)
        n_new = decay[..., None] * n + jnp.einsum('bhs,bhsk->bhk', w_end, kj)
        return (c_new, n_new, m_new), h

    (c_f, n_f, m_f), hs = lax.scan(step, (c0.astype(f32), n0.astype(f32), m0.astype(f32)), (qc, kc, vc, ic, lfc))
    hs = jnp.swapaxes(jnp.moveaxis(hs, 0, 1), 2, 3).reshape(bsz, t, nh, dh)
    return hs, c_f.astype(c0.dtype), n_f.astype(n0.dtype), m_f.astype(m0.dtype)

def s5_mlstm_mixer(xn, h_re, h_im, c0, n0, m0, w_in, lam_re, lam_im, log_dt, b_re, b_im, c_re, c_im,
                   d_skip, w_glu, b_glu, b_igate, b_fgate, w_out):
    bsz, t, _ = xn.shape
    u, q, k, v, o, ig, fg = split_cols(xn @ w_in, IN0_SIZES)
    y_s5, h_re_new, h_im_new = s5_scan(u, h_re, h_im, lam_re, lam_im, log_dt, b_re, b_im, c_re, c_im,
                                       d_skip, w_glu, b_glu)
    heads = lambda z: z.reshape(bsz, t, MLSTM_HEADS, MLSTM_HEAD_DIM)
    h, c_new, n_new, m_new = mlstm_chunkwise(heads(q), heads(k), heads(v), ig + b_igate, fg + b_fgate, c0, n0, m0)
    y_ml = (jax.nn.sigmoid(o.astype(jnp.float32)) * h.reshape(bsz, t, MLSTM_WIDTH)).astype(xn.dtype)
    y = jnp.concatenate([y_s5, y_ml], axis=-1) @ w_out
    return y, (h_re_new, h_im_new, c_new, n_new, m_new)

def dsa_project(xn, w_in):
    bsz, t, _ = xn.shape
    q, k, v, qi, ki, wi = split_cols(xn @ w_in, IN1_SIZES)
    q = q.reshape(bsz, t, ATT_HEADS, ATT_HEAD_DIM)
    k = k.reshape(bsz, t, ATT_KV_HEADS, ATT_HEAD_DIM)
    v = v.reshape(bsz, t, ATT_KV_HEADS, ATT_HEAD_DIM)
    qi = qi.reshape(bsz, t, IDX_HEADS, IDX_DIM)
    return q, k, v, qi, ki, wi

def dsa_block(q, qi, wi, qpos, ki_all, gather_kv):
    f32 = jnp.float32
    bsz, nq = q.shape[0], q.shape[1]
    s_len = ki_all.shape[1]
    topk = min(TOPK_MAX, s_len // 4)
    logits = jnp.einsum('bqhd,bsd->bqhs', qi.astype(f32), ki_all.astype(f32)) * (IDX_DIM ** -0.5)
    score = jnp.einsum('bqhs,bqh->bqs', jax.nn.relu(logits), wi.astype(f32) * (IDX_HEADS ** -0.5))
    visible = jnp.arange(s_len)[None, :] <= qpos[:, None]
    score = jnp.where(visible[None], score, -jnp.inf)
    _, idx = lax.top_k(score, topk)
    valid = idx <= qpos[None, :, None]
    k_sel, v_sel = gather_kv(idx)
    qg = q.reshape(bsz, nq, ATT_KV_HEADS, ATT_GROUP, ATT_HEAD_DIM).astype(f32)
    att = jnp.einsum('bqgrd,bqkgd->bqgrk', qg, k_sel.astype(f32)) * (ATT_HEAD_DIM ** -0.5)
    att = jnp.where(valid[:, :, None, None, :], att, -jnp.inf)
    p = jax.nn.softmax(att, axis=-1)
    o = jnp.einsum('bqgrk,bqkgd->bqgrd', p, v_sel.astype(f32))
    return o.reshape(bsz, nq, ATT_WIDTH).astype(q.dtype)

def dsa_attend(q, qi, wi, qpos, ki_all, gather_kv, w_out):
    bsz, t = q.shape[0], q.shape[1]
    fn = lambda qb, qib, wib, pb: dsa_block(qb, qib, wib, pb, ki_all, gather_kv)
    if t % Q_BLOCK != 0 or t <= Q_BLOCK:
        out = fn(q, qi, wi, qpos)
    else:
        nb = t // Q_BLOCK
        split = lambda z: jnp.moveaxis(z.reshape((bsz, nb, Q_BLOCK) + z.shape[2:]), 1, 0)
        out = lax.map(lambda a: fn(*a), (split(q), split(qi), split(wi), qpos.reshape(nb, Q_BLOCK)))
        out = jnp.moveaxis(out, 0, 1).reshape(bsz, t, ATT_WIDTH)
    return out @ w_out

def gather_rows(rows, idx):
    return jax.vmap(lambda r, i: r[i])(rows, idx)

def gather_paged(pool, page_table, new_rows, idx):
    past_len = page_table.shape[1] * PAGE_SIZE
    in_past = idx < past_len
    pidx = jnp.minimum(idx, past_len - 1)
    phys = jax.vmap(lambda pt, i: pt[i])(page_table, pidx // PAGE_SIZE)
    from_past = pool[phys, pidx % PAGE_SIZE]
    from_new = gather_rows(new_rows, jnp.clip(idx - past_len, 0, new_rows.shape[1] - 1))
    mask = in_past.reshape(in_past.shape + (1,) * (from_past.ndim - in_past.ndim))
    return jnp.where(mask, from_past, from_new.astype(from_past.dtype))

def setup_inputs(seed: int = 0) -> dict:
    key = jax.random.key(seed)
    ks = iter(jax.random.split(key, 48))
    f32 = jnp.float32
    nrm = lambda shape, scale: jax.random.normal(next(ks), shape, f32) * scale
    n_pages = PAST_LEN // PAGE_SIZE
    n_used = DEC_BATCH * n_pages
    n_phys = n_used + max(1, n_used // 4)
    page_table = jax.random.permutation(next(ks), n_phys)[:n_used].reshape(DEC_BATCH, n_pages).astype(jnp.int32)
    return {
        "x_prompt": nrm((BATCH, SEQ, D_MODEL), 1.0),
        "x_sample": nrm((DEC_BATCH, DEC_SEQ, D_MODEL), 1.0),
        "state_s5_re": nrm((DEC_BATCH, S5_GROUPS, S5_STATE), 0.1),
        "state_s5_im": nrm((DEC_BATCH, S5_GROUPS, S5_STATE), 0.1),
        "state_mlstm_c": nrm((DEC_BATCH, MLSTM_HEADS, MLSTM_HEAD_DIM, MLSTM_HEAD_DIM), MLSTM_HEAD_DIM ** -0.5),
        "state_mlstm_n": nrm((DEC_BATCH, MLSTM_HEADS, MLSTM_HEAD_DIM), MLSTM_HEAD_DIM ** -0.5),
        "state_mlstm_m": nrm((DEC_BATCH, MLSTM_HEADS), 0.5),
        "cache_k": nrm((n_phys, PAGE_SIZE, ATT_KV_HEADS, ATT_HEAD_DIM), 1.0),
        "cache_v": nrm((n_phys, PAGE_SIZE, ATT_KV_HEADS, ATT_HEAD_DIM), 1.0),
        "cache_kidx": nrm((n_phys, PAGE_SIZE, IDX_DIM), 1.0),
        "page_table": page_table,
        "norm_mix": 1.0 + nrm((DEPTH, D_MODEL), 0.01),
        "norm_mlp": 1.0 + nrm((DEPTH, D_MODEL), 0.01),
        "norm_final": 1.0 + nrm((D_MODEL,), 0.01),
        "w_in0": nrm((D_MODEL, IN0_WIDTH), D_MODEL ** -0.5),
        "s5_lam_re": -0.5 + nrm((S5_GROUPS, S5_STATE), 0.01),
        "s5_lam_im": math.pi * jnp.arange(S5_STATE, dtype=f32)[None, :] + nrm((S5_GROUPS, S5_STATE), 0.01),
        "s5_log_dt": jax.random.uniform(next(ks), (S5_GROUPS,), f32, math.log(1e-3), math.log(1e-1)),
        "s5_b_re": nrm((S5_GROUPS, S5_STATE, S5_GROUP), (2 * S5_GROUP) ** -0.5),
        "s5_b_im": nrm((S5_GROUPS, S5_STATE, S5_GROUP), (2 * S5_GROUP) ** -0.5),
        "s5_c_re": nrm((S5_GROUPS, S5_GROUP, S5_STATE), (2 * S5_STATE) ** -0.5),
        "s5_c_im": nrm((S5_GROUPS, S5_GROUP, S5_STATE), (2 * S5_STATE) ** -0.5),
        "s5_d": nrm((S5_WIDTH,), 1.0),
        "w_glu": nrm((S5_WIDTH, S5_WIDTH), S5_WIDTH ** -0.5),
        "b_glu": nrm((S5_WIDTH,), 0.01),
        "b_igate": nrm((MLSTM_HEADS,), 0.1),
        "b_fgate": jnp.linspace(3.0, 6.0, MLSTM_HEADS, dtype=f32) + nrm((MLSTM_HEADS,), 0.01),
        "w_out0": nrm((S5_WIDTH + MLSTM_WIDTH, D_MODEL), (S5_WIDTH + MLSTM_WIDTH) ** -0.5),
        "w_in1": nrm((D_MODEL, IN1_WIDTH), D_MODEL ** -0.5),
        "w_out1": nrm((ATT_WIDTH, D_MODEL), ATT_WIDTH ** -0.5),
        "w_up": nrm((DEPTH, D_MODEL, D_FF), D_MODEL ** -0.5),
        "w_down": nrm((DEPTH, D_FF, D_MODEL), D_FF ** -0.5),
    }

def reference(x_prompt, x_sample, state_s5_re, state_s5_im, state_mlstm_c, state_mlstm_n, state_mlstm_m,
              cache_k, cache_v, cache_kidx, page_table, norm_mix, norm_mlp, norm_final, w_in0, s5_lam_re,
              s5_lam_im, s5_log_dt, s5_b_re, s5_b_im, s5_c_re, s5_c_im, s5_d, w_glu, b_glu, b_igate, b_fgate,
              w_out0, w_in1, w_out1, w_up, w_down):
    bp, tp, _ = x_prompt.shape
    db, ts, _ = x_sample.shape
    past_len = page_table.shape[1] * PAGE_SIZE
    zeros = lambda *shape: jnp.zeros(shape, x_prompt.dtype)
    even_w = (w_in0, s5_lam_re, s5_lam_im, s5_log_dt, s5_b_re, s5_b_im, s5_c_re, s5_c_im, s5_d, w_glu, b_glu,
              b_igate, b_fgate, w_out0)
    hp, hs = x_prompt, x_sample
    for layer in range(DEPTH):
        xp = rms_norm(hp, norm_mix[layer])
        xs = rms_norm(hs, norm_mix[layer])
        if layer % 2 == 0:
            yp, (p_s5_re, p_s5_im, p_c, p_n, p_m) = s5_mlstm_mixer(
                xp, zeros(bp, S5_GROUPS, S5_STATE), zeros(bp, S5_GROUPS, S5_STATE),
                zeros(bp, MLSTM_HEADS, MLSTM_HEAD_DIM, MLSTM_HEAD_DIM), zeros(bp, MLSTM_HEADS, MLSTM_HEAD_DIM),
                zeros(bp, MLSTM_HEADS), *even_w)
            ys, (s_s5_re, s_s5_im, s_c, s_n, s_m) = s5_mlstm_mixer(
                xs, state_s5_re, state_s5_im, state_mlstm_c, state_mlstm_n, state_mlstm_m, *even_w)
        else:
            q, p_k, p_v, qi, p_kidx, wi = dsa_project(xp, w_in1)
            yp = dsa_attend(q, qi, wi, jnp.arange(tp), p_kidx,
                            lambda idx: (gather_rows(p_k, idx), gather_rows(p_v, idx)), w_out1)
            q, s_k, s_v, qi, s_kidx, wi = dsa_project(xs, w_in1)
            ki_past = cache_kidx[page_table].reshape(db, past_len, IDX_DIM)
            ki_all = jnp.concatenate([ki_past, s_kidx.astype(ki_past.dtype)], axis=1)
            ys = dsa_attend(q, qi, wi, past_len + jnp.arange(ts), ki_all,
                            lambda idx: (gather_paged(cache_k, page_table, s_k, idx),
                                         gather_paged(cache_v, page_table, s_v, idx)), w_out1)
        hp = hp + yp
        hs = hs + ys
        hp = hp + sq_relu_mlp(rms_norm(hp, norm_mlp[layer]), w_up[layer], w_down[layer])
        hs = hs + sq_relu_mlp(rms_norm(hs, norm_mlp[layer]), w_up[layer], w_down[layer])
    y_prompt = rms_norm(hp, norm_final)
    y_sample = rms_norm(hs, norm_final)
    return (y_prompt, y_sample, p_s5_re, p_s5_im, p_c, p_n, p_m, p_k, p_v, p_kidx,
            s_s5_re, s_s5_im, s_c, s_n, s_m, s_k, s_v, s_kidx)


_drawn_inputs = setup_inputs


def setup_inputs(seed=0):
    import zlib

    import numpy as np

    out = dict(_drawn_inputs(seed))
    spreads = {}
    factors = {'norm_mlp': 17.418,
     'norm_final': 28.939,
     's5_lam_re': 15.596,
     's5_c_re': 3.028,
     's5_c_im': 2.942,
     'b_glu': 51.467,
     'cache_k': 8.0,
     'cache_v': 8.0,
     'cache_kidx': 8.0,
     'w_out1': 3.133}
    for name, (base, spread) in spreads.items():
        noise = np.random.default_rng([zlib.crc32(name.encode()), seed]).standard_normal(out[name].shape)
        drawn = base * np.exp(spread * noise) if base else spread * noise
        out[name] = __import__('jax').numpy.asarray(drawn.astype(out[name].dtype))
    for name, factor in factors.items():
        out[name] = (out[name] * factor).astype(out[name].dtype)
    return out
```

```python
import math

import concourse.bass as bass
import concourse.mybir as mybir

F32 = mybir.dt.float32
I32 = mybir.dt.int32
ALU = mybir.AluOpType
ACT = mybir.ActivationFunctionType
AX_X = mybir.AxisListType.X

P = 128
D = 1024
KT = D // P
T = 1024
B = 8
N = T + B
CHUNKS = 3
CH = N // CHUNKS
TB = T // P
FF_GROUPS = 4
EPS = 1e-6

S5_W = 512
G = 32
GC = 16
GS = 64
SC = 8
NC = T // SC
UW = NC + 2 * B
HW = NC + B

MH = 4
DH = 128
MC = 128
NMC = T // MC

AH = 8
KVH = 2
AG = AH // KVH
IH = 8
IDIM = 64
TOPK = 256
PAGE = 128
PAGES = 8
PAST = PAGE * PAGES
NEG = -1e30


class Signal:

    def __init__(self, ctx, nc, name):
        self.sem = ctx.enter_context(nc.semaphore(name))
        self.base = 0

    def at(self, n):
        return n + self.base

    def passed(self, n):
        self.base += n


class Tiles:
    pass


class Machine:

    def __init__(self, ctx, nc, ins, outs):
        self.nc, self.ctx = nc, ctx
        self.ins, self.outs = ins, outs

        def sb(name, shape, dt=F32):
            return ctx.enter_context(nc.sbuf_tensor(name, shape, dt))

        self.sb = sb
        self.resid = sb("resid", [P, KT, N])
        self.normed = sb("normed", [P, KT, N])
        self.hidden = sb("hidden", [P, KT, N])
        self.proj = sb("proj", [P, 20, N])
        self.wts = sb("wts", [P, 2, KT, P])
        self.inv_rms = sb("inv_rms", [P, N])
        self.mark = sb("mark", [P, 4])
        self.ident = sb("ident", [P, P])
        self.ones = sb("ones", [P, P])
        self.vec_rows = sb("vec_rows", [48, P])
        self.vecs = sb("vecs", [P, 48])
        self.g_mix = [self.vecs[:, 0:8], self.vecs[:, 8:16]]
        self.g_mlp = [self.vecs[:, 16:24], self.vecs[:, 24:32]]
        self.s5_d, self.b_glu, self.g_final = self.vecs[:, 32:36], self.vecs[:, 36:40], self.vecs[:, 40:48]
        self.eps = sb("eps", [P, 1])
        self.ps_pair = [ctx.enter_context(nc.psum_tensor(f"ps{b}", [P, 1024], F32)) for b in range(4)]
        self.ps = [self.ps_pair[b // 2][:, (b % 2) * 512:(b % 2) * 512 + 512] for b in range(8)]

        def signal(name):
            return Signal(ctx, nc, name)

        self.w_loaded0 = signal("w_loaded0")
        self.w_loaded1 = signal("w_loaded1")
        self.unit_done = signal("unit_done")
        self.set_free = signal("set_free")
        self.x_loaded = signal("x_loaded")
        self.consts_set = signal("consts_set")
        self.norm_g = signal("norm_g")
        self.sq_done = signal("sq_done")
        self.ssq_done = signal("ssq_done")
        self.mean_set = signal("mean_set")
        self.inv_done = signal("inv_done")
        self.tiles_ready = signal("tiles_ready")
        self.stored = signal("stored")
        self.x_stored = signal("x_stored")
        self.x_back = signal("x_back")
        self.evac_a = signal("evac_a")
        self.evac_b = signal("evac_b")
        self.pe_a = signal("pe_a")
        self.pe_b = signal("pe_b")
        self.pe_c = signal("pe_c")
        self.pe_d = signal("pe_d")
        self.act_a = signal("act_a")
        self.act_b = signal("act_b")
        self.act_c = signal("act_c")
        self.act_d = signal("act_d")
        self.dve_a = signal("dve_a")
        self.dve_b = signal("dve_b")
        self.dve_c = signal("dve_c")
        self.dve_d = signal("dve_d")
        self.dve_e = signal("dve_e")
        self.dve_f = signal("dve_f")
        self.pool_a = signal("pool_a")
        self.pool_b = signal("pool_b")
        self.pool_c = signal("pool_c")
        self.pool_d = signal("pool_d")
        self.dma_a = signal("dma_a")
        self.dma_b = signal("dma_b")
        self.dma_c = signal("dma_c")
        self.dma_d = signal("dma_d")
        self.dma_e = signal("dma_e")
        self.dma_f = signal("dma_f")
        self.dma_g = signal("dma_g")
        self.dma_h = signal("dma_h")



def token_cols(n):
    return slice(n * CH, (n + 1) * CH)


def phase_load_x(m):
    nc = m.nc
    x_tok = m.proj[:, 0:KT, 0:T].rearrange("p t f -> p t f")
    x_smp = m.proj[0:B, 8, 0:D]
    with nc.Block() as block:

        @block.sync
        def _(sp):
            src = m.ins["x_prompt"].rearrange("b (t p) f -> p (b t) f", p=P)
            sp.dma_start(x_tok[:, 0:4, :], src[:, 0:4, :]).then_inc(m.dma_a.sem, 16)
            sp.dma_start(x_tok[:, 4:8, :], src[:, 4:8, :]).then_inc(m.dma_b.sem, 16)
            sp.dma_start(x_smp, m.ins["x_sample"].rearrange("b o f -> (b o) f")).then_inc(m.dma_c.sem, 16)

        @block.gpsimd
        def _(pool):
            nc.gpsimd.memset(m.ident[:], 0.0)
            nc.gpsimd.memset(m.ones[:], 1.0)
            nc.gpsimd.memset(m.eps[:], EPS)
            pool.drain()
            nc.gpsimd.affine_select(out=m.ident[:], in_=m.ident[:], compare_op=ALU.not_equal, fill=1.0,
                                    base=0, pattern=[[-1, P]], channel_multiplier=1).then_inc(m.consts_set.sem, 1)

        @block.tensor
        def _(pe):
            pe.wait_ge(m.consts_set.sem, m.consts_set.at(1))
            pe.wait_ge(m.dma_a.sem, m.dma_a.at(16))
            pe.wait_ge(m.dma_b.sem, m.dma_b.at(16))
            pe.wait_ge(m.dma_c.sem, m.dma_c.at(16))
            for k in range(KT):
                if k >= 2:
                    pe.wait_ge(m.evac_a.sem, m.evac_a.at(k - 1))
                    pe.wait_ge(m.evac_b.sem, m.evac_b.at(k - 1))
                banks = m.ps[3 * (k % 2):3 * (k % 2) + 3]
                for t in range(TB):
                    nc.tensor.transpose(banks[t // 4][:, (t % 4) * P:(t % 4 + 1) * P],
                                        x_tok[:, t, k * P:(k + 1) * P], m.ident[:])
                nc.tensor.transpose(banks[2][:, 0:B], x_smp[:, k * P:(k + 1) * P],
                                    m.ident[0:B, 0:B]).then_inc(m.pe_a.sem, 1)
            pe.wait_ge(m.norm_g.sem, m.norm_g.at(80))
            nc.tensor.transpose(m.ps[6][:, 0:48], m.vec_rows[:], m.ident[0:48, 0:48]).then_inc(m.pe_b.sem, 1)

        @block.scalar
        def _(act):
            for name, r, n in (("norm_mix", 0, 16), ("norm_mlp", 16, 16), ("s5_d", 32, 4), ("b_glu", 36, 4),
                               ("norm_final", 40, 8)):
                src = m.ins[name]
                src = src.rearrange("l (k p) -> (l k) p", p=P) if len(src.shape) == 2 else src.rearrange("(k p) -> k p", p=P)
                act.dma_start(m.vec_rows[r:r + n, :], src).then_inc(m.norm_g.sem, 16)
            for k in range(KT):
                act.wait_ge(m.pe_a.sem, m.pe_a.at(k + 1))
                b = m.ps[3 * (k % 2):3 * (k % 2) + 3]
                nc.scalar.copy(m.resid[:, k, 512:T], b[1][:])
                nc.scalar.copy(m.resid[:, k, T:N], b[2][:, 0:B]).then_inc(m.evac_a.sem, 1)

        @block.vector
        def _(dve):
            nc.vector.memset(m.inv_rms[:, 0:1], 0.0).then_inc(m.set_free.sem, 2)
            nc.vector.memset(m.inv_rms[:, 1:2], 0.0).then_inc(m.unit_done.sem, 2)
            for k in range(KT):
                dve.wait_ge(m.pe_a.sem, m.pe_a.at(k + 1))
                nc.vector.tensor_copy(m.resid[:, k, 0:512], m.ps[3 * (k % 2)][:]).then_inc(m.evac_b.sem, 1)
            dve.wait_ge(m.pe_b.sem, m.pe_b.at(1))
            nc.vector.tensor_copy(m.vecs[:], m.ps[6][:, 0:48])

    m.consts_set.passed(1)
    m.unit_done.passed(2)
    for s in (m.dma_a, m.dma_b, m.dma_c):
        s.passed(16)
    m.norm_g.passed(80)
    m.pe_b.passed(1)
    m.pe_a.passed(KT)
    m.evac_a.passed(KT)
    m.evac_b.passed(KT)


def load_unit(sp, m, slot, j, src):
    w_loaded = m.w_loaded1 if slot else m.w_loaded0
    sp.wait_ge(m.unit_done.sem, m.unit_done.at(2 * j + slot - 1))
    sp.dma_start(m.wts[:, slot], src).then_inc(w_loaded.sem, 16)


def unit_matmuls(pe, m, slot, j, x, ready=None):
    nc = m.nc
    w_loaded = m.w_loaded1 if slot else m.w_loaded0
    pe.wait_ge(w_loaded.sem, w_loaded.at(16 * j + 16))
    pe.wait_ge(m.set_free.sem, m.set_free.at(2 * j + slot + 1))
    for k in range(KT):
        if ready:
            ready(k)
        for c in range(CHUNKS):
            last = nc.tensor.matmul(m.ps[3 * slot + c][:, 0:CH], m.wts[:, slot, k, :], x[:, k, token_cols(c)],
                                    start=(k == 0), stop=(k == KT - 1))
    last.then_inc(m.unit_done.sem, 1)


def units_passed(m, n):
    m.w_loaded0.passed(16 * (n // 2))
    m.w_loaded1.passed(16 * (n // 2))
    for s in (m.unit_done, m.set_free):
        s.passed(n)


def norm_act(act, m, gain):
    nc = m.nc
    for k in range(KT):
        nc.scalar.activation(m.hidden[:, k, :], m.resid[:, k, :], ACT.Square).then_inc(m.sq_done.sem, 1)
        nc.scalar.mul(m.normed[:, k, :], m.resid[:, k, :], gain[:, k:k + 1]).then_inc(m.tiles_ready.sem, 1)


def norm_pe(pe, m):
    nc = m.nc
    for k in range(KT):
        pe.wait_ge(m.sq_done.sem, m.sq_done.at(k + 1))
        for c in range(CHUNKS):
            last = nc.tensor.matmul(m.ps[3 + c][:, 0:CH], m.ones[:], m.hidden[:, k, token_cols(c)],
                                    start=(k == 0), stop=(k == KT - 1))
    last.then_inc(m.ssq_done.sem, 1)


def norm_dve(dve, m):
    nc = m.nc
    dve.wait_ge(m.ssq_done.sem, m.ssq_done.at(1))
    for c in range(CHUNKS):
        nc.vector.tensor_scalar(m.inv_rms[:, token_cols(c)], m.ps[3 + c][:, 0:CH], 1.0 / D, EPS, ALU.mult, ALU.add)
    dve.drain()
    nc.vector.reciprocal(m.inv_rms[:], m.inv_rms[:]).then_inc(m.mean_set.sem, 1)


def norm_root(act, m):
    nc = m.nc
    act.wait_ge(m.mean_set.sem, m.mean_set.at(1))
    nc.scalar.activation(m.inv_rms[:], m.inv_rms[:], ACT.Sqrt).then_inc(m.inv_done.sem, 1)


def norm_passed(m):
    m.sq_done.passed(KT)
    m.tiles_ready.passed(KT)
    for s in (m.ssq_done, m.mean_set, m.inv_done):
        s.passed(1)


def phase_in0(m):
    nc = m.nc
    w_in = m.ins["w_in0"].rearrange("(k p) n -> p k n", p=P)
    wg = m.sb("w_gates", [P, KT, 36])
    units = 20

    with nc.Block() as block:

        @block.gpsimd
        def _(pool):
            nc.gpsimd.memset(wg[:], 0.0).then_inc(m.pool_a.sem, 1)

        @block.sync
        def _(sp):
            sp.dma_start(m.spill, m.resid[:]).then_inc(m.x_stored.sem, 16)
            with sp.Fori(0, units // 2) as j:
                for slot in range(2):
                    load_unit(sp, m, slot, j, w_in[:, :, bass.ds((j * 2 + slot) * P, P)])
            sp.wait_ge(m.x_stored.sem, m.x_stored.at(16))

        @block.tensor
        def _(pe):
            norm_pe(pe, m)
            pe.wait_ge(m.mean_set.sem, m.mean_set.at(1))
            pe.wait_ge(m.tiles_ready.sem, m.tiles_ready.at(KT))
            with pe.Fori(0, units // 2) as j:
                for slot in range(2):
                    unit_matmuls(pe, m, slot, j, m.normed)
            pe.wait_ge(m.dma_a.sem, m.dma_a.at(32))
            pe.wait_ge(m.set_free.sem, m.set_free.at(units + 1))
            for k in range(KT):
                for c in range(CHUNKS):
                    last = nc.tensor.matmul(m.ps[c][0:36, 0:CH], wg[:, k, :], m.normed[:, k, token_cols(c)],
                                            start=(k == 0), stop=(k == KT - 1))
            last.then_inc(m.pe_a.sem, 1)

        @block.scalar
        def _(act):
            norm_act(act, m, m.g_mix[0])
            norm_root(act, m)
            act.wait_ge(m.pool_a.sem, m.pool_a.at(1))
            with nc.allow_non_contiguous_dma("16 bytes a row"):
                act.dma_start(wg[:, :, 0:4], w_in[:, :, 2560:2564]).then_inc(m.dma_a.sem, 16)
                act.dma_start(wg[:, :, 32:36], w_in[:, :, 2564:2568]).then_inc(m.dma_a.sem, 16)

        @block.vector
        def _(dve):
            norm_dve(dve, m)
            dve.wait_ge(m.inv_done.sem, m.inv_done.at(1))

            def scaled(u, slot, order):
                dve.wait_ge(m.unit_done.sem, m.unit_done.at(u + 1))
                for c in range(CHUNKS):
                    src = m.ps[3 * slot + c][:, 0:CH]
                    r = m.inv_rms[:, token_cols(c)]
                    dst = m.proj[:, bass.ds(u, 1), token_cols(c)].rearrange("p a n -> p (a n)")
                    if order == "chunked":
                        w = CH // SC if c < 2 else NC - 2 * (CH // SC)
                        c0 = c * (CH // SC)
                        tile = m.proj[:, bass.ds(u, 1), 0:T].rearrange("p a (s c) -> p (a c) s", s=SC)
                        if c == 2:
                            nc.vector.tensor_tensor(m.proj[:, bass.ds(u, 1), T:N].rearrange("p a n -> p (a n)"),
                                                    src[:, SC * w:CH], r[:, SC * w:CH], ALU.mult)
                        dst, src, r = (tile[:, c0:c0 + w, :], src[:, 0:SC * w].rearrange("p (c s) -> p c s", s=SC),
                                       r[:, 0:SC * w].rearrange("p (c s) -> p c s", s=SC))
                    last = nc.vector.tensor_tensor(dst, src, r, ALU.mult)
                last.then_inc(m.set_free.sem, 1)

            with dve.Fori(0, 2) as j:
                for slot in range(2):
                    scaled(j * 2 + slot, slot, "chunked")
            with dve.Fori(2, units // 2) as j:
                for slot in range(2):
                    scaled(j * 2 + slot, slot, "plain")
            dve.wait_ge(m.pe_a.sem, m.pe_a.at(1))
            for c in range(CHUNKS):
                nc.vector.tensor_tensor(m.gates[0:4, 0, token_cols(c)], m.ps[c][0:4, 0:CH],
                                        m.inv_rms[0:4, token_cols(c)], ALU.mult)
                nc.vector.tensor_tensor(m.gates[32:36, 0, token_cols(c)], m.ps[c][32:36, 0:CH],
                                        m.inv_rms[32:36, token_cols(c)], ALU.mult)

    m.pool_a.passed(1)
    m.pe_a.passed(1)
    m.dma_a.passed(32)
    m.x_stored.passed(16)
    norm_passed(m)
    units_passed(m, units)


class Carver:

    def __init__(self, tile):
        self.flat = tile.rearrange("p a n -> p (a n)")
        self.at = 0

    def take(self, *shape, parts=P):
        n = math.prod(shape)
        ap = self.flat[0:parts, self.at:self.at + n]
        self.at += n
        assert self.at <= self.flat.shape[1], self.at
        names = "abcd"[:len(shape)]
        spec = " ".join(names)
        return ap if len(shape) == 1 else ap.rearrange(f"p ({spec}) -> p {spec}", **dict(zip(names[1:], shape[1:])))


def s5_tiles(m):
    s = m.s5 = Tiles()
    a = Carver(m.resid[:])
    s.starts = a.take(G, HW)
    s.lam_rows = a.take(2, P, parts=G)
    s.dt = a.take(G)
    s.lam = a.take(2, G)
    s.tmp = a.take(6, G)
    s.tmp2 = a.take(6, G)
    s.bar = a.take(2, G)
    s.coef = a.take(2, G)
    s.pow_re = a.take(SC + 1, G)
    s.pow_im = a.take(SC + 1, G)
    s.b_in = a.take(2, G, GC)
    s.x1 = a.take(SC, G)
    s.x2 = a.take(SC, G)
    s.y2 = a.take(SC + 1, G)
    c = Carver(m.hidden[:])
    s.u = c.take(G, UW)
    s.e = [c.take(2 * SC * GC) for _ in range(2)]
    s.et = [c.take(P) for _ in range(2)]
    s.mt = [c.take(P) for _ in range(2)]
    s.ct = [c.take(SC + 1, GC) for _ in range(2)]
    s.t1 = c.take((SC + 1) * GC)
    s.t2 = c.take((SC + 1) * GC)
    s.t3 = c.take((SC + 1) * GC)
    s.t4 = c.take((SC + 1) * GC)
    b = Carver(m.normed[:])
    s.bt = Carver(m.normed[:]).take(4, G, GC)
    s.h = b.take(2, G, NC, parts=GS)
    x = Carver(m.s5_small[:])
    s.c_t = x.take(2, G, GC)
    s.y1 = x.take(SC + 1, G)
    s.s0 = x.take(2, B, G, parts=GS)
    s.sv = x.take(2, B, G, parts=GS)
    s.l8 = x.take(4, G, parts=GS)
    s.l1 = x.take(4, G, parts=GS)
    s.st = x.take(4, G, parts=GS)
    return s


def phase_s5_params(m):
    nc = m.nc
    s = s5_tiles(m)
    TWO_PI = 2 * math.pi
    C1 = 6.28125
    C2 = TWO_PI - C1
    rnd = 12582912.0
    s0_rows = [m.wts[:, 0, 0:2].rearrange("p a b -> p (a b)"), m.wts[:, 0, 2:4].rearrange("p a b -> p (a b)")]
    c_rows = m.wts[:, 1].rearrange("p (a t) b -> p a t b", a=2)
    with nc.Block() as block:

        @block.sync
        def _(sp):
            for half in range(2):
                h = slice(GS * half, GS * half + GS)
                sp.dma_start(s.lam_rows[:, 0, h], m.ins["s5_lam_re"]).then_inc(m.dma_a.sem, 16)
                sp.dma_start(s.lam_rows[:, 1, h], m.ins["s5_lam_im"]).then_inc(m.dma_a.sem, 16)
            sp.dma_start(s.dt, m.ins["s5_log_dt"].partition_broadcast(P)).then_inc(m.dma_a.sem, 16)
            sp.dma_start(m.s5_dram.rearrange("(k p) n -> p k n", p=P), m.proj[:, 0:4, :]).then_inc(m.dma_d.sem, 16)
            sp.wait_ge(m.dma_d.sem, m.dma_d.at(16))
            for step in range(SC):
                sp.dma_start(s.u[GC * step:GC * step + GC, :, 0:NC],
                             m.s5_dram.rearrange("(g c) n -> c g n", c=GC)[:, :, NC * step:NC * step + NC]
                             ).then_inc(m.dma_f.sem, 16)
            sp.wait_ge(m.pool_a.sem, m.pool_a.at(1))
            for rows, cols in ((slice(0, GC), slice(NC, NC + B)), (slice(P - GC, P), slice(NC + B, UW))):
                sp.dma_start(s.u[rows, :, cols], m.s5_dram.rearrange("(g c) n -> c g n", c=GC)[:, :, T:N]
                             ).then_inc(m.dma_f.sem, 16)
            sp.wait_ge(m.dma_f.sem, m.dma_f.at(10 * 16))

        @block.scalar
        def _(act):
            for part, name in enumerate(("re", "im")):
                for half in range(2):
                    act.dma_start(c_rows[:, part, :, GS * half:GS * half + GS],
                                  m.ins["s5_c_" + name].rearrange("(t g) c s -> (g c) t s", t=4)
                                  ).then_inc(m.dma_b.sem, 16)
            for part, name in enumerate(("re", "im")):
                act.dma_start(s0_rows[part][:, 0:2 * GS].rearrange("r (a s) -> r a s", a=2),
                              m.ins["state_s5_" + name].rearrange("(a b) g s -> (b g) a s", a=2)
                              ).then_inc(m.dma_c.sem, 16)
            act.wait_ge(m.dma_a.sem, m.dma_a.at(80))
            nc.scalar.activation(s.dt, s.dt, ACT.Exp).then_inc(m.act_a.sem, 1)
            act.wait_ge(m.dve_b.sem, m.dve_b.at(1))
            nc.scalar.activation(s.tmp[:, 0, :], s.tmp[:, 0, :], ACT.Exp).then_inc(m.act_b.sem, 1)
            act.wait_ge(m.dve_c.sem, m.dve_c.at(1))
            nc.scalar.activation(s.tmp[:, 2:4, :], s.tmp[:, 2:4, :], ACT.Sin).then_inc(m.act_c.sem, 1)

        @block.gpsimd
        def _(pool):
            nc.gpsimd.memset(s.u[:, :, NC:UW], 0.0).then_inc(m.pool_a.sem, 1)
            nc.gpsimd.memset(s.e[0][:, P:2 * P], 0.0)
            nc.gpsimd.memset(s.e[1][:, P:2 * P], 0.0)
            for half in range(2):
                h = slice(GS * half, GS * half + GS)
                for part, name in enumerate(("re", "im")):
                    pool.dma_start(s.b_in[h, part], m.ins["s5_b_" + name].rearrange("g s c -> s g c")
                                   ).then_inc(m.dma_e.sem, 16)
            pool.wait_ge(m.dma_e.sem, m.dma_e.at(64))

        @block.tensor
        def _(pe):
            pe.wait_ge(m.dma_a.sem, m.dma_a.at(80))
            for part in range(2):
                last = nc.tensor.transpose(m.ps[0][:, G * part:G * part + G], s.lam_rows[:, part, :],
                                           m.ident[0:G, 0:G])
            last.then_inc(m.pe_a.sem, 1)
            pe.wait_ge(m.dma_b.sem, m.dma_b.at(64))
            for part in range(2):
                for t in range(4):
                    last = nc.tensor.transpose(m.ps[1 + part][:, P * t:P * t + P], c_rows[:, part, t, :], m.ident[:])
            last.then_inc(m.pe_b.sem, 1)
            pe.wait_ge(m.dma_c.sem, m.dma_c.at(32))
            for part in range(2):
                for a in range(2):
                    last = nc.tensor.transpose(m.ps[3 + part][0:GS, P * a:P * a + P],
                                               s0_rows[part][:, GS * a:GS * a + GS], m.ident[:])
            last.then_inc(m.pe_c.sem, 1)

        @block.vector
        def _(dve):
            V = nc.vector
            dve.wait_ge(m.pe_a.sem, m.pe_a.at(1))
            V.tensor_copy(s.lam, m.ps[0][:, 0:2 * G].rearrange("p (a g) -> p a g", a=2))
            dve.drain()
            dve.wait_ge(m.act_a.sem, m.act_a.at(1))
            V.tensor_tensor(s.tmp[:, 0, :], s.lam[:, 0, :], s.dt, ALU.mult).then_inc(m.dve_b.sem, 1)
            V.tensor_tensor(s.tmp[:, 1, :], s.lam[:, 1, :], s.dt, ALU.mult)
            dve.drain()
            V.tensor_scalar(s.tmp[:, 4, :], s.tmp[:, 1, :], 1 / TWO_PI, rnd, ALU.mult, ALU.add)
            dve.drain()
            V.tensor_scalar(s.tmp[:, 4, :], s.tmp[:, 4, :], rnd, None, ALU.subtract)
            dve.drain()
            V.scalar_tensor_tensor(s.tmp[:, 1, :], s.tmp[:, 4, :], -C1, s.tmp[:, 1, :], ALU.mult, ALU.add)
            dve.drain()
            V.scalar_tensor_tensor(s.tmp[:, 2, :], s.tmp[:, 4, :], -C2, s.tmp[:, 1, :], ALU.mult, ALU.add)
            dve.drain()
            V.tensor_scalar(s.tmp[:, 5, :], s.tmp[:, 2, :], math.pi / 2, -TWO_PI, ALU.is_gt, ALU.mult)
            dve.drain()
            V.scalar_tensor_tensor(s.tmp[:, 3, :], s.tmp[:, 2, :], math.pi / 2, s.tmp[:, 5, :], ALU.add, ALU.add)
            dve.drain()
            V.tensor_scalar(s.tmp[:, 2:4, :], s.tmp[:, 2:4, :], 3.1415925, -3.1415925, ALU.min, ALU.max).then_inc(m.dve_c.sem, 1)
            dve.wait_ge(m.act_b.sem, m.act_b.at(1))
            dve.wait_ge(m.act_c.sem, m.act_c.at(1))
            V.tensor_tensor(s.bar[:, 0, :], s.tmp[:, 0, :], s.tmp[:, 3, :], ALU.mult)
            V.tensor_tensor(s.bar[:, 1, :], s.tmp[:, 0, :], s.tmp[:, 2, :], ALU.mult)
            dve.drain()
            lr, li, br, bi = s.lam[:, 0, :], s.lam[:, 1, :], s.bar[:, 0, :], s.bar[:, 1, :]
            t = s.tmp2
            V.tensor_scalar(t[:, 0, :], br, -1.0, None, ALU.add)
            V.tensor_tensor(t[:, 1, :], lr, lr, ALU.mult)
            V.tensor_tensor(t[:, 2, :], li, li, ALU.mult)
            dve.drain()
            V.tensor_tensor(t[:, 1, :], t[:, 1, :], t[:, 2, :], ALU.add)
            V.tensor_tensor(t[:, 3, :], t[:, 0, :], lr, ALU.mult)
            V.tensor_tensor(t[:, 4, :], bi, li, ALU.mult)
            dve.drain()
            V.reciprocal(t[:, 1, :], t[:, 1, :])
            V.tensor_tensor(t[:, 3, :], t[:, 3, :], t[:, 4, :], ALU.add)
            dve.drain()
            V.tensor_tensor(t[:, 4, :], bi, lr, ALU.mult)
            V.tensor_tensor(t[:, 5, :], t[:, 0, :], li, ALU.mult)
            dve.drain()
            V.tensor_tensor(t[:, 4, :], t[:, 4, :], t[:, 5, :], ALU.subtract)
            V.tensor_tensor(s.coef[:, 0, :], t[:, 3, :], t[:, 1, :], ALU.mult)
            dve.drain()
            V.tensor_tensor(s.coef[:, 1, :], t[:, 4, :], t[:, 1, :], ALU.mult)
            V.memset(s.pow_re[:, 0, :], 1.0)
            V.memset(s.pow_im[:, 0, :], 0.0)
            dve.drain()
            for j in range(SC):
                pr, pi = s.pow_re[:, j, :], s.pow_im[:, j, :]
                V.tensor_tensor(t[:, 0, :], pr, br, ALU.mult)
                V.tensor_tensor(t[:, 1, :], pi, bi, ALU.mult)
                V.tensor_tensor(t[:, 2, :], pr, bi, ALU.mult)
                V.tensor_tensor(t[:, 3, :], pi, br, ALU.mult)
                dve.drain()
                V.tensor_tensor(s.pow_re[:, j + 1, :], t[:, 0, :], t[:, 1, :], ALU.subtract)
                V.tensor_tensor(s.pow_im[:, j + 1, :], t[:, 2, :], t[:, 3, :], ALU.add)
                dve.drain()
            top, bot = slice(0, GS), slice(GS, P)
            for j in range(SC):
                V.tensor_copy(s.x1[top, j], s.pow_re[top, SC - 1 - j])
                V.tensor_copy(s.x1[bot, j], s.pow_im[bot, SC - 1 - j])
                V.tensor_scalar(s.x2[top, j], s.pow_im[top, SC - 1 - j], -1.0, None, ALU.mult)
                V.tensor_copy(s.x2[bot, j], s.pow_re[bot, SC - 1 - j])
            V.tensor_copy(s.y1[top], s.pow_re[top])
            V.tensor_scalar(s.y1[bot], s.pow_im[bot], -1.0, None, ALU.mult)
            V.tensor_scalar(s.y2[top], s.pow_im[top], -1.0, None, ALU.mult)
            V.tensor_scalar(s.y2[bot], s.pow_re[bot], -1.0, None, ALU.mult)
            for dst, j in ((s.l8, SC), (s.l1, 1)):
                V.tensor_copy(dst[:, 0, :], s.pow_re[top, j, :])
                V.tensor_copy(dst[:, 1, :], s.pow_re[top, j, :])
                V.tensor_copy(dst[:, 2, :], s.pow_im[top, j, :])
                V.tensor_scalar(dst[:, 3, :], s.pow_im[top, j, :], -1.0, None, ALU.mult)
            dve.wait_ge(m.dma_e.sem, m.dma_e.at(64))
            cr = s.coef[:, 0, :].unsqueeze(2).to_broadcast([P, G, GC])
            ci = s.coef[:, 1, :].unsqueeze(2).to_broadcast([P, G, GC])
            w = [s.bt[:, i] for i in range(4)]
            V.tensor_tensor(w[0], s.b_in[:, 0], cr, ALU.mult)
            V.tensor_tensor(w[1], s.b_in[:, 1], ci, ALU.mult)
            V.tensor_tensor(w[2], s.b_in[:, 0], ci, ALU.mult)
            V.tensor_tensor(w[3], s.b_in[:, 1], cr, ALU.mult)
            dve.drain()
            V.tensor_tensor(s.b_in[:, 0], w[0], w[1], ALU.subtract)
            V.tensor_tensor(s.b_in[:, 1], w[2], w[3], ALU.add)
            dve.wait_ge(m.pe_b.sem, m.pe_b.at(1))
            for part in range(2):
                V.tensor_copy(s.c_t[:, part], m.ps[1 + part][:].rearrange("p (g c) -> p g c", g=G))
            dve.wait_ge(m.pe_c.sem, m.pe_c.at(1))
            for part in range(2):
                V.tensor_copy(s.s0[:, part].rearrange("p b g -> p (b g)"), m.ps[3 + part][0:GS, 0:B * G])

    m.dma_a.passed(80)
    m.dma_b.passed(64)
    m.dma_c.passed(32)
    m.dma_d.passed(16)
    m.dma_e.passed(64)
    m.dma_f.passed(10 * 16)
    for x in (m.act_a, m.act_b, m.act_c, m.dve_b, m.dve_c, m.pool_a, m.pe_a, m.pe_b, m.pe_c):
        x.passed(1)


def s5_b_powers(pool, m, s, g, slot):
    x1 = s.x1[:, :, bass.ds(g, 1)].to_broadcast([P, SC, GC])
    x2 = s.x2[:, :, bass.ds(g, 1)].to_broadcast([P, SC, GC])
    view = lambda t: t[:, 0:P].rearrange("p (s c) -> p s c", s=SC)
    nc = m.nc
    nc.gpsimd.tensor_tensor(view(s.t1), x1, s.b_in[:, 0, bass.ds(g, 1), :].to_broadcast([P, SC, GC]), ALU.mult)
    nc.gpsimd.tensor_tensor(view(s.t2), x2, s.b_in[:, 1, bass.ds(g, 1), :].to_broadcast([P, SC, GC]), ALU.mult)
    pool.drain()
    return nc.gpsimd.tensor_tensor(s.e[slot][:, 0:P], s.t1[:, 0:P], s.t2[:, 0:P], ALU.add)


def phase_s5_states(m):
    nc = m.nc
    s = m.s5
    with nc.Block() as block:

        @block.gpsimd
        def _(pool):
            def step(g, slot, first):
                pool.drain()
                if not first:
                    pool.wait_ge(m.pe_a.sem, m.pe_a.at(g - 1))
                s5_b_powers(pool, m, s, g, slot).then_inc(m.pool_a.sem, 1)

            for g in range(2):
                step(g, g, True)
            with pool.Fori(1, G // 2) as i:
                for slot in range(2):
                    step(i * 2 + slot, slot, False)

        @block.tensor
        def _(pe):
            def turn(g, slot, first):
                pe.wait_ge(m.pool_a.sem, m.pool_a.at(g + 1))
                if not first:
                    pe.wait_ge(m.act_a.sem, m.act_a.at(g - 1))
                nc.tensor.transpose(m.ps[slot][:, 0:P], s.e[slot][:, 0:P], m.ident[:]).then_inc(m.pe_a.sem, 1)

            def add(g, slot, first):
                pe.wait_ge(m.act_a.sem, m.act_a.at(g + 1))
                if not first:
                    pe.wait_ge(m.act_b.sem, m.act_b.at(g - 1))
                    pe.wait_ge(m.dve_b.sem, m.dve_b.at(g - 1))
                nc.tensor.matmul(m.ps[2 + slot][:, 0:UW], s.et[slot], s.u[:, bass.ds(g, 1), :].rearrange("p a n -> p (a n)"),
                                 start=True, stop=True).then_inc(m.pe_b.sem, 1)

            def pair(g0, first):
                for slot in range(2):
                    turn(g0 + slot, slot, first)
                for slot in range(2):
                    add(g0 + slot, slot, first)

            pair(0, True)
            with pe.Fori(1, G // 2) as i:
                pair(i * 2, False)

        @block.scalar
        def _(act):
            def pair(g0, first):
                for slot in range(2):
                    g = g0 + slot
                    act.wait_ge(m.pe_a.sem, m.pe_a.at(g + 1))
                    if not first:
                        act.wait_ge(m.pe_b.sem, m.pe_b.at(g - 1))
                    nc.scalar.copy(s.et[slot], m.ps[slot][:, 0:P]).then_inc(m.act_a.sem, 1)
                for slot in range(2):
                    g = g0 + slot
                    act.wait_ge(m.pe_b.sem, m.pe_b.at(g + 1))
                    nc.scalar.copy(s.h[:, 0, bass.ds(g, 1), :].rearrange("p a n -> p (a n)"), m.ps[2 + slot][0:GS, 0:NC])
                    nc.scalar.copy(s.sv[:, 0, :, bass.ds(g, 1)].rearrange("p b a -> p (b a)"),
                                   m.ps[2 + slot][0:GS, NC + B:UW]).then_inc(m.act_b.sem, 1)

            pair(0, True)
            with act.Fori(1, G // 2) as i:
                pair(i * 2, False)

        @block.vector
        def _(dve):
            def move(g, slot):
                dve.wait_ge(m.pe_b.sem, m.pe_b.at(g + 1))
                if True:
                    dve.wait_ge(m.act_b.sem, m.act_b.at(g + 1))
                nc.vector.tensor_copy(s.h[:, 1, bass.ds(g, 1), :].rearrange("p a n -> p (a n)"), m.ps[2 + slot][GS:P, 0:NC])
                nc.vector.tensor_copy(s.sv[:, 1, :, bass.ds(g, 1)].rearrange("p b a -> p (b a)"),
                                      m.ps[2 + slot][GS:P, NC + B:UW]).then_inc(m.dve_b.sem, 1)

            with dve.Fori(0, G // 2) as i:
                for slot in range(2):
                    move(i * 2 + slot, slot)

            def advance(dst, h, mul, n=None):
                t1, t2 = n
                nc.vector.tensor_tensor(t1, mul[0], h, ALU.mult)
                nc.vector.tensor_tensor(t2, mul[1], h, ALU.mult)
                dve.drain()
                nc.vector.tensor_tensor(dst, dst, t1, ALU.add)
                dve.drain()
                nc.vector.tensor_tensor(dst[:, 0], dst[:, 0], t2[:, 1], ALU.add)
                nc.vector.tensor_tensor(dst[:, 1], dst[:, 1], t2[:, 0], ALU.add)
                dve.drain()

            dve.drain()
            t1, t2 = s.st[:, 0:2, :], s.st[:, 2:4, :]
            with dve.Fori(1, NC) as c:
                col = lambda k: s.h[:, :, :, bass.ds(k, 1)].rearrange("p r g a -> p r (g a)")
                advance(col(c), col(c - 1), (s.l8[:, 0:2, :], s.l8[:, 2:4, :]), (t1, t2))
            for b in range(B):
                dve.wait_ge(m.act_b.sem, m.act_b.at(G))
                advance(s.sv[:, :, b, :], s.s0[:, :, b, :], (s.l1[:, 0:2, :], s.l1[:, 2:4, :]), (t1, t2))

    m.pool_a.passed(G)
    m.pe_a.passed(G)
    m.pe_b.passed(G)
    m.act_a.passed(G)
    m.act_b.passed(G)
    m.dve_b.passed(G)


def phase_s5_outputs(m):
    nc = m.nc
    s = m.s5
    fin_sb = m.wts[:, 0].rearrange("p a b -> p (a b)")
    with nc.Block() as block:

        @block.gpsimd
        def _(pool):
            def step(g, slot, first):
                pool.drain()
                if not first:
                    pool.wait_ge(m.pe_a.sem, m.pe_a.at(g - 1))
                s5_b_powers(pool, m, s, g, slot).then_inc(m.pool_a.sem, 1)

            for g in range(2):
                step(g, g, True)
            with pool.Fori(1, G // 2) as i:
                for slot in range(2):
                    step(i * 2 + slot, slot, False)

        @block.vector
        def _(dve):
            nc.vector.memset(s.starts[:, :, 0:1], 0.0)
            nc.vector.tensor_copy(s.starts[GS:P, :, 1:NC], s.h[:, 1, :, 0:NC - 1])
            nc.vector.tensor_copy(s.starts[GS:P, :, NC:HW], s.s0[:, 1].rearrange("p b g -> p g b")).then_inc(m.dve_a.sem, 1)

            def c_powers(g, slot, first):
                dve.drain()
                if not first:
                    dve.wait_ge(m.pe_b.sem, m.pe_b.at(g - 1))
                y1 = s.y1[:, :, bass.ds(g, 1)].to_broadcast([P, SC + 1, GC])
                y2 = s.y2[:, :, bass.ds(g, 1)].to_broadcast([P, SC + 1, GC])
                view = lambda t: t.rearrange("p (s c) -> p s c", s=SC + 1)
                nc.vector.tensor_tensor(view(s.t3), y1, s.c_t[:, 0, bass.ds(g, 1), :].to_broadcast([P, SC + 1, GC]), ALU.mult)
                nc.vector.tensor_tensor(view(s.t4), y2, s.c_t[:, 1, bass.ds(g, 1), :].to_broadcast([P, SC + 1, GC]), ALU.mult)
                dve.drain()
                nc.vector.tensor_tensor(s.ct[slot], view(s.t3), view(s.t4), ALU.add).then_inc(m.dve_b.sem, 1)

            def out(g, slot):
                dve.wait_ge(m.pe_b.sem, m.pe_b.at(g + 1))
                nc.vector.tensor_copy(s.u[:, bass.ds(g, 1), 0:HW].rearrange("p a n -> p (a n)"),
                                      m.ps[2 + slot][:, 0:HW]).then_inc(m.dve_c.sem, 1)

            for g in range(2):
                c_powers(g, g, True)
            with dve.Fori(1, G // 2) as i:
                for slot in range(2):
                    c_powers(i * 2 + slot, slot, False)
                    out(i * 2 + slot - 2, slot)
            for slot in range(2):
                out(G - 2 + slot, slot)

        @block.scalar
        def _(act):
            nc.scalar.copy(s.starts[0:GS, :, 1:NC], s.h[:, 0, :, 0:NC - 1])
            nc.scalar.copy(s.starts[0:GS, :, NC:HW], s.s0[:, 0].rearrange("p b g -> p g b")).then_inc(m.act_a.sem, 1)

            def kernel_copy(g, slot, first):
                act.wait_ge(m.pe_a.sem, m.pe_a.at(g + 1))
                if not first:
                    act.wait_ge(m.pe_b.sem, m.pe_b.at(g - 1))
                nc.scalar.copy(s.mt[slot], m.ps[slot][:, 0:P]).then_inc(m.act_b.sem, 1)

            for g in range(2):
                kernel_copy(g, g, True)
            with act.Fori(1, G // 2) as i:
                for slot in range(2):
                    kernel_copy(i * 2 + slot, slot, False)
            act.wait_ge(m.pe_c.sem, m.pe_c.at(1))
            nc.scalar.copy(fin_sb[0:G, 0:P], m.ps[4][0:G, 0:P])
            nc.scalar.copy(fin_sb[:, P:P + 4 * GS], m.ps[5][:, 0:4 * GS]).then_inc(m.act_c.sem, 1)

        @block.tensor
        def _(pe):
            for part in range(2):
                nc.tensor.transpose(m.ps[4][0:G, GS * part:GS * part + GS], s.h[:, part, :, NC - 1], m.ident[0:GS, 0:GS])
                for a in range(2):
                    last = nc.tensor.transpose(m.ps[5][:, GS * (2 * part + a):GS * (2 * part + a) + GS],
                                               s.sv[:, part, 4 * a:4 * a + 4, :].rearrange("p b g -> p (b g)"),
                                               m.ident[0:GS, 0:GS])
            last.then_inc(m.pe_c.sem, 1)

            def kernel_of(g, slot, first):
                pe.wait_ge(m.pool_a.sem, m.pool_a.at(g + 1))
                pe.wait_ge(m.dve_b.sem, m.dve_b.at(g + 1))
                if not first:
                    pe.wait_ge(m.act_b.sem, m.act_b.at(g - 1))
                for t in range(SC):
                    last = nc.tensor.matmul(m.ps[slot][:, GC * t:GC * t + GC],
                                            s.e[slot][:, GC * (SC - 1 - t):GC * (SC - 1 - t) + P],
                                            s.ct[slot][:, 0, :], start=True, stop=True)
                last.then_inc(m.pe_a.sem, 1)

            def y_of(g, slot, first):
                pe.wait_ge(m.act_b.sem, m.act_b.at(g + 1))
                if not first:
                    pe.wait_ge(m.dve_c.sem, m.dve_c.at(g - 1))
                u = s.u[:, bass.ds(g, 1), 0:HW].rearrange("p a n -> p (a n)")
                h = s.starts[:, bass.ds(g, 1), :].rearrange("p a n -> p (a n)")
                nc.tensor.matmul(m.ps[2 + slot][:, 0:HW], s.mt[slot], u, start=True, stop=False)
                nc.tensor.matmul(m.ps[2 + slot][:, 0:HW], s.ct[slot][:, 1:, :].rearrange("p s c -> p (s c)"), h,
                                 start=False, stop=True).then_inc(m.pe_b.sem, 1)

            def pair(g0, first):
                for slot in range(2):
                    kernel_of(g0 + slot, slot, first)
                if first:
                    pe.wait_ge(m.dve_a.sem, m.dve_a.at(1))
                    pe.wait_ge(m.act_a.sem, m.act_a.at(1))
                for slot in range(2):
                    y_of(g0 + slot, slot, first)

            pair(0, True)
            with pe.Fori(1, G // 2) as i:
                pair(i * 2, False)

        @block.sync
        def _(sp):
            sp.wait_ge(m.act_c.sem, m.act_c.at(1))
            for part, name in enumerate(("re", "im")):
                sp.dma_start(m.outs["p_s5_" + name].rearrange("b g s -> (b g) s"),
                             fin_sb[0:G, GS * part:GS * part + GS]).then_inc(m.stored.sem, 16)
                sp.dma_start(m.outs["s_s5_" + name].rearrange("(a b) g s -> (b g) a s", a=2),
                             fin_sb[:, P + 2 * GS * part:P + 2 * GS * part + 2 * GS].rearrange("p (a s) -> p a s", a=2)
                             ).then_inc(m.stored.sem, 16)
            sp.wait_ge(m.stored.sem, m.stored.at(64))

    m.stored.passed(64)
    for x in (m.pool_a, m.pe_a, m.pe_b, m.act_b, m.dve_b, m.dve_c):
        x.passed(G)
    for x in (m.act_a, m.dve_a, m.pe_c, m.act_c):
        x.passed(1)


def phase_s5_glu(m):
    nc = m.nc
    s = m.s5
    w_glu = m.wts[:].rearrange("p a b c -> p (a b c)").rearrange("p (k n) -> p k n", k=4)
    y = m.normed[:, 4:8, :]
    x = Carver(m.resid[:])
    inner = x.take(4, N)
    gated = x.take(4, N)
    with nc.Block() as block:

        @block.sync
        def _(sp):
            sp.dma_start(w_glu, m.ins["w_glu"].rearrange("(k p) n -> p k n", p=P)).then_inc(m.dma_b.sem, 16)
            out = m.s5_dram.rearrange("(g c) n -> c g n", c=GC)
            for step in range(SC):
                sp.dma_start(out[:, :, NC * step:NC * step + NC], s.u[GC * step:GC * step + GC, :, 0:NC]
                             ).then_inc(m.dma_a.sem, 16)
            sp.dma_start(out[:, :, T:N], s.u[0:GC, :, NC:HW]).then_inc(m.dma_a.sem, 16)
            sp.wait_ge(m.dma_a.sem, m.dma_a.at(9 * 16))
            sp.dma_start(y, m.s5_dram.rearrange("(k p) n -> p k n", p=P)).then_inc(m.dma_c.sem, 16)

        @block.vector
        def _(dve):
            V = nc.vector
            dve.wait_ge(m.dma_c.sem, m.dma_c.at(16))
            for k in range(4):
                V.scalar_tensor_tensor(y[:, k], m.proj[:, k], m.s5_d[:, k:k + 1], y[:, k], ALU.mult, ALU.add)
                dve.drain()
                V.tensor_tensor(inner[:, k], y[:, k], y[:, k], ALU.mult)
                dve.drain()
                V.tensor_scalar(inner[:, k], inner[:, k], 0.044715, 1.0, ALU.mult, ALU.add)
                dve.drain()
                V.tensor_tensor(inner[:, k], inner[:, k], y[:, k], ALU.mult).then_inc(m.dve_a.sem, 1)
            for k in range(4):
                dve.wait_ge(m.act_a.sem, m.act_a.at(k + 1))
                V.tensor_scalar(inner[:, k], inner[:, k], 0.5, 0.5, ALU.mult, ALU.add)
                dve.drain()
                V.tensor_tensor(y[:, k], inner[:, k], y[:, k], ALU.mult).then_inc(m.dve_b.sem, 1)
            for k in range(4):
                dve.wait_ge(m.act_b.sem, m.act_b.at(k + 1))
                V.tensor_tensor(m.normed[:, k, 0:T].rearrange("p (c s) -> p s c", s=SC),
                                gated[:, k, 0:T].rearrange("p (s c) -> p s c", s=SC),
                                y[:, k, 0:T].rearrange("p (s c) -> p s c", s=SC), ALU.mult)
                V.tensor_tensor(m.normed[:, k, T:N], gated[:, k, T:N], y[:, k, T:N], ALU.mult)

        @block.scalar
        def _(act):
            for k in range(4):
                act.wait_ge(m.dve_a.sem, m.dve_a.at(k + 1))
                nc.scalar.activation(inner[:, k], inner[:, k], ACT.Tanh, scale=math.sqrt(2 / math.pi)).then_inc(m.act_a.sem, 1)
            for o in range(4):
                act.wait_ge(m.pe_a.sem, m.pe_a.at(o + 1))
                for c in range(CHUNKS):
                    last = nc.scalar.activation(gated[:, o, token_cols(c)], m.ps[3 * (o % 2) + c][:, 0:CH], ACT.Sigmoid,
                                                bias=m.b_glu[:, o:o + 1])
                last.then_inc(m.act_b.sem, 1)

        @block.tensor
        def _(pe):
            pe.wait_ge(m.dma_b.sem, m.dma_b.at(16))
            for o in range(4):
                if o >= 2:
                    pe.wait_ge(m.act_b.sem, m.act_b.at(o - 1))
                for k in range(4):
                    if o == 0:
                        pe.wait_ge(m.dve_b.sem, m.dve_b.at(k + 1))
                    for c in range(CHUNKS):
                        last = nc.tensor.matmul(m.ps[3 * (o % 2) + c][:, 0:CH], w_glu[:, k, o * P:(o + 1) * P],
                                                y[:, k, token_cols(c)], start=(k == 0), stop=(k == 3))
                last.then_inc(m.pe_a.sem, 1)

    m.dma_a.passed(9 * 16)
    m.dma_b.passed(16)
    m.dma_c.passed(16)
    for q in (m.dve_a, m.dve_b, m.act_a, m.act_b, m.pe_a):
        q.passed(4)


def ml_tiles(m):
    s = m.ml = Tiles()
    a = Carver(m.resid[:])
    s.ig, s.lf, s.b, s.mx, s.a, s.tmp, s.mask = (a.take(N, parts=MH) for _ in range(7))
    s.sel = a.take(MH, P, parts=MH)
    s.bias = a.take(2, parts=MH)
    s.m_prev = a.take(NMC, parts=MH)
    s.decay_row = a.take(NMC, parts=MH)
    s.gap = a.take(NMC, parts=MH)
    s.m0 = a.take(B, parts=MH)
    s.m_s = a.take(B, parts=MH)
    s.rows_s = a.take(3, B, parts=MH)
    c = Carver(m.hidden[:])
    s.stage = [c.take(12, MC) for _ in range(2)]
    s.c_state = c.take(MH, DH + 1)
    s.v_ext = c.take(MH, DH + 1)
    s.num = c.take(MH, DH + 1)
    s.inter = c.take(MH, DH + 1)
    s.k_tok = c.take(MH, DH)
    s.decays = c.take(MH, MC)
    s.probs = c.take(MH, MC)
    s.h_tok = c.take(MH, DH)
    s.pack = m.s5_small[:, 0, 0:T]
    x = Carver(m.s5_small[:])
    x.take(T)
    s.cols = x.take(NMC, 4, MH)
    s.decay = x.take(MH, NMC)
    s.bc_s = x.take(3, MH, B)
    s.den = x.take(2, MH)
    s.nt = x.take(B, MH)
    s.kw = x.take(MH, B)
    s.prod = x.take(MH, B)
    s.dn = x.take(3, MH, B)
    s.num_s = x.take(MH, B)
    s.n_rows = x.take(2, P)
    return s


def phase_ml_gates(m):
    nc = m.nc
    s = ml_tiles(m)
    with nc.Block() as block:

        @block.sync
        def _(sp):
            sp.dma_start(s.bias[:, 0:1], m.ins["b_igate"].rearrange("(h a) -> h a", a=1)).then_inc(m.dma_a.sem, 16)
            sp.dma_start(s.bias[:, 1:2], m.ins["b_fgate"].rearrange("(h a) -> h a", a=1)).then_inc(m.dma_a.sem, 16)
            with nc.allow_non_contiguous_dma("32 values"):
                sp.dma_start(s.m0, m.ins["state_mlstm_m"].rearrange("b h -> h b")).then_inc(m.dma_a.sem, 16)
            sp.wait_ge(m.dve_d.sem, m.dve_d.at(1))
            with nc.allow_non_contiguous_dma("36 values"):
                sp.dma_start(m.outs["p_m"].rearrange("b h -> h b"), s.mx[:, T - 1:T]).then_inc(m.stored.sem, 16)
                sp.dma_start(m.outs["s_m"].rearrange("b h -> h b"), s.m_s).then_inc(m.stored.sem, 16)
            sp.wait_ge(m.stored.sem, m.stored.at(32))

        @block.gpsimd
        def _(pool):
            nc.gpsimd.memset(s.sel, 0.0)
            nc.gpsimd.memset(s.pack, 0.0).then_inc(m.pool_b.sem, 1)
            nc.gpsimd.memset(s.mask[:, 0:T], 1.0)
            pool.drain()
            nc.gpsimd.memset(s.mask[:, 0:T:MC], 0.0)
            nc.gpsimd.affine_select(out=s.sel, in_=s.sel, compare_op=ALU.not_equal, fill=1.0, base=0,
                                    pattern=[[-1, MH], [0, P]], channel_multiplier=1).then_inc(m.pool_a.sem, 1)

        @block.scalar
        def _(act):
            act.wait_ge(m.dve_a.sem, m.dve_a.at(1))
            nc.scalar.activation(s.tmp, s.tmp, ACT.Exp, scale=-1.0).then_inc(m.act_a.sem, 1)
            act.wait_ge(m.dve_b.sem, m.dve_b.at(1))
            nc.scalar.activation(s.tmp, s.tmp, ACT.Ln).then_inc(m.act_b.sem, 1)
            act.wait_ge(m.dve_c.sem, m.dve_c.at(1))
            nc.scalar.copy(s.pack[0:4], s.ig[:, 0:T])
            nc.scalar.activation(s.pack[32:36], s.tmp[:, 0:T], ACT.Exp)
            nc.scalar.activation(s.pack[64:68], s.mask[:, 0:T], ACT.Exp)
            nc.scalar.activation(s.pack[96:100], s.mx[:, 0:T], ACT.Exp, scale=-1.0)
            nc.scalar.activation(s.decay_row, s.decay_row, ACT.Exp)
            nc.scalar.activation(s.rows_s, s.rows_s, ACT.Exp).then_inc(m.act_c.sem, 1)
            for h in range(MH):
                nc.scalar.activation(m.proj[:, 16 + h], m.proj[:, 16 + h], ACT.Sigmoid)

        @block.vector
        def _(dve):
            V = nc.vector
            dve.wait_ge(m.dma_a.sem, m.dma_a.at(48))
            V.tensor_scalar(s.ig, m.gates[0:4, 0], s.bias[:, 0:1], None, ALU.add)
            V.tensor_copy(s.b, m.gates[32:36, 0])
            dve.drain()
            V.tensor_scalar(s.lf, s.b, s.bias[:, 1:2], None, ALU.add)
            dve.drain()
            V.scalar_tensor_tensor(s.tmp, s.lf, -1.0, s.lf, ALU.mult, ALU.max).then_inc(m.dve_a.sem, 1)
            dve.wait_ge(m.act_a.sem, m.act_a.at(1))
            V.tensor_scalar(s.tmp, s.tmp, 1.0, None, ALU.add).then_inc(m.dve_b.sem, 1)
            dve.wait_ge(m.act_b.sem, m.act_b.at(1))
            V.scalar_tensor_tensor(s.lf, s.lf, 0.0, s.tmp, ALU.min, ALU.subtract)
            dve.drain()
            dve.wait_ge(m.pool_a.sem, m.pool_a.at(1))
            V.tensor_tensor_scan(s.b[:, 0:T], s.mask[:, 0:T], s.lf[:, 0:T], 0.0, ALU.mult, ALU.add)
            V.tensor_tensor_scan(s.mx[:, 0:T], s.lf[:, 0:T], s.ig[:, 0:T], 0.0, ALU.add, ALU.max)
            V.tensor_tensor(s.tmp[:, 0:B], s.lf[:, T:N], s.m0, ALU.add)
            dve.drain()
            V.tensor_tensor(s.m_s, s.tmp[:, 0:B], s.ig[:, T:N], ALU.max)
            V.memset(s.m_prev[:, 0:1], 0.0)
            V.tensor_copy(s.m_prev[:, 1:], s.mx[:, MC - 1:T - 1:MC])
            V.tensor_tensor(s.gap, s.b[:, MC - 1:T:MC], s.mx[:, MC - 1:T:MC], ALU.subtract)
            dve.drain()
            V.tensor_tensor(s.rows_s[:, 0], s.tmp[:, 0:B], s.m_s, ALU.subtract)
            V.tensor_tensor(s.rows_s[:, 1], s.ig[:, T:N], s.m_s, ALU.subtract)
            V.tensor_scalar(s.rows_s[:, 2], s.m_s, -1.0, None, ALU.mult)
            V.tensor_tensor(s.decay_row, s.gap, s.m_prev, ALU.add)
            V.tensor_tensor(s.a[:, 0:T], s.b[:, 0:T], s.mx[:, 0:T], ALU.subtract)
            V.tensor_tensor(s.ig[:, 0:T], s.ig[:, 0:T], s.b[:, 0:T], ALU.subtract)
            dve.drain()
            chunks = lambda x: x[:, 0:T].rearrange("p (c t) -> p c t", c=NMC)
            V.tensor_tensor(chunks(s.tmp), chunks(s.a), s.m_prev.unsqueeze(2).to_broadcast([MH, NMC, MC]), ALU.add)
            dve.wait_ge(m.pool_b.sem, m.pool_b.at(1))
            V.tensor_tensor(chunks(s.mask), chunks(s.ig), s.gap.unsqueeze(2).to_broadcast([MH, NMC, MC]),
                            ALU.add).then_inc(m.dve_c.sem, 1)
            dve.drain()
            V.memset(s.bias[:, 0:1], 0.0).then_inc(m.dve_d.sem, 1)
            dve.wait_ge(m.pe_a.sem, m.pe_a.at(1))
            for half in range(2):
                V.tensor_copy(s.cols[:, 4 * half:4 * half + 4].rearrange("p c q h -> p (c q) h"),
                              m.ps[half][:].rearrange("p (x w) -> p x w", w=32)[:, :, 0:MH])
            V.tensor_copy(s.decay, m.ps[2][:, 0:MH * NMC].rearrange("p (h c) -> p h c", h=MH))
            V.tensor_copy(s.bc_s.rearrange("p q h b -> p h q b"),
                          m.ps[3][:, 0:MH * 3 * B].rearrange("p (h q b) -> p h q b", h=MH, q=3))

        @block.tensor
        def _(pe):
            pe.wait_ge(m.act_c.sem, m.act_c.at(1))
            for c in range(NMC):
                nc.tensor.transpose(m.ps[c // 4][:, (c % 4) * P:(c % 4) * P + P], s.pack[:, c * MC:(c + 1) * MC], m.ident[:])
            for h in range(MH):
                nc.tensor.matmul(m.ps[2][:, NMC * h:NMC * h + NMC], s.sel[:, h], s.decay_row, start=True, stop=True)
                last = nc.tensor.matmul(m.ps[3][:, 3 * B * h:3 * B * h + 3 * B], s.sel[:, h],
                                        s.rows_s.rearrange("p q b -> p (q b)"), start=True, stop=True)
            last.then_inc(m.pe_a.sem, 1)

    m.dma_a.passed(48)
    m.stored.passed(32)
    for x in (m.pool_a, m.pool_b, m.act_a, m.act_b, m.act_c, m.dve_a, m.dve_b, m.dve_c, m.dve_d, m.pe_a):
        x.passed(1)


def phase_ml_chunks(m):
    nc = m.nc
    s = m.ml
    scale = DH ** -0.5
    ps_a, ps_s, ps_k, ps_v = m.ps[0], m.ps[1], m.ps[2], m.ps[3]
    W = DH + 1
    heads = lambda bank: bank[:].rearrange("p (h t) -> p h t", h=MH)
    with nc.Block() as block:

        @block.sync
        def _(sp):
            def stage(c, slot, first):
                if not first:
                    sp.wait_ge(m.pe_b.sem, m.pe_b.at(c - 1))
                load = m.dma_b if slot else m.dma_a
                sp.dma_start(s.stage[slot], m.proj[:, 4:16, bass.ds(c * MC, MC)]).then_inc(load.sem, 16)

            for c in range(2):
                stage(c, c, True)
            with sp.Fori(1, NMC // 2) as i:
                for slot in range(2):
                    stage(i * 2 + slot, slot, False)
            sp.wait_ge(m.dve_d.sem, m.dve_d.at(NMC))
            sp.dma_start(m.outs["p_c"].rearrange("b h k v -> k (b h) v"), s.c_state[:, :, 0:DH]).then_inc(m.stored.sem, 16)
            sp.wait_ge(m.act_d.sem, m.act_d.at(1))
            sp.dma_start(m.outs["p_n"].rearrange("b h k -> (b h) k"), s.n_rows[0:MH, 0]).then_inc(m.stored.sem, 16)
            sp.wait_ge(m.stored.sem, m.stored.at(32))

        @block.tensor
        def _(pe):
            def scores(c, slot, first):
                load = m.dma_b if slot else m.dma_a
                pe.wait_ge(load.sem, load.at((c - slot) * 8 + 16))
                if not first:
                    pe.wait_ge(m.act_a.sem, m.act_a.at(c))
                    pe.wait_ge(m.dve_e.sem, m.dve_e.at(c))
                    pe.wait_ge(m.dve_a.sem, m.dve_a.at(c))
                    pe.wait_ge(m.act_b.sem, m.act_b.at(c))
                x = s.stage[slot]
                for h in range(MH):
                    nc.tensor.matmul(heads(ps_a)[:, h], s.sel[:, h], s.a[:, bass.ds(c * MC, MC)], start=True, stop=True)
                for h in range(MH):
                    nc.tensor.matmul(heads(ps_s)[:, h], x[:, 4 + h], x[:, h], start=True, stop=True)
                for h in range(MH):
                    nc.tensor.transpose(heads(ps_k)[:, h], x[:, 4 + h], m.ident[:])
                    last = nc.tensor.transpose(heads(ps_v)[:, h], x[:, 8 + h], m.ident[:])
                last.then_inc(m.pe_a.sem, 1)

            def combine(c, slot, first):
                pe.wait_ge(m.dve_a.sem, m.dve_a.at(c + 1))
                pe.wait_ge(m.act_b.sem, m.act_b.at(c + 1))
                if not first:
                    pe.wait_ge(m.dve_d.sem, m.dve_d.at(c))
                x = s.stage[slot]
                for h in range(MH):
                    bank = m.ps[4 + h]
                    nc.tensor.matmul(bank[:, 0:W], s.probs[:, h], s.v_ext[:, h], start=True, stop=True)
                    nc.tensor.matmul(bank[:, W:2 * W], x[:, h], s.c_state[:, h], start=True, stop=True)
                    last = nc.tensor.matmul(bank[:, 2 * W:3 * W], s.k_tok[:, h], s.v_ext[:, h], start=True, stop=True)
                last.then_inc(m.pe_b.sem, 1)

            def turn(c):
                pe.wait_ge(m.dve_c.sem, m.dve_c.at(c + 1))
                for h in range(MH):
                    last = nc.tensor.transpose(heads(ps_a)[:, h], s.h_tok[:, h], m.ident[:])
                last.then_inc(m.pe_c.sem, 1)

            def chunk(c, slot, first):
                scores(c, slot, first)
                if first:
                    pe.wait_ge(m.pool_b.sem, m.pool_b.at(1))
                combine(c, slot, first)
                turn(c)

            chunk(0, 0, True)
            chunk(1, 1, False)
            with pe.Fori(1, NMC // 2) as i:
                for slot in range(2):
                    chunk(i * 2 + slot, slot, False)
            pe.wait_ge(m.dve_d.sem, m.dve_d.at(NMC))
            pe.wait_ge(m.dve_e.sem, m.dve_e.at(NMC))
            nc.tensor.transpose(ps_a[0:MH, 0:P], s.c_state[:, :, DH], m.ident[:]).then_inc(m.pe_d.sem, 1)

        @block.scalar
        def _(act):
            def chunk(c, first):
                cols = lambda q, h: s.cols[:, bass.ds(c, 1), q, h:h + 1].rearrange("p a b -> p (a b)")
                act.wait_ge(m.pe_a.sem, m.pe_a.at(c + 1))
                if not first:
                    act.wait_ge(m.dve_a.sem, m.dve_a.at(c))
                    act.wait_ge(m.pool_a.sem, m.pool_a.at(c))
                for h in range(MH):
                    last = nc.scalar.activation(s.decays[:, h], heads(ps_a)[:, h], ACT.Exp, bias=cols(0, h))
                last.then_inc(m.act_a.sem, 1)
                if not first:
                    act.wait_ge(m.pe_b.sem, m.pe_b.at(c))
                if first:
                    act.wait_ge(m.pool_b.sem, m.pool_b.at(1))
                nc.scalar.copy(s.v_ext[:, :, 0:DH], heads(ps_v))
                for h in range(MH):
                    last = nc.scalar.mul(s.k_tok[:, h], heads(ps_k)[:, h], cols(2, h))
                last.then_inc(m.act_b.sem, 1)
                act.wait_ge(m.pe_b.sem, m.pe_b.at(c + 1))
                if not first:
                    act.wait_ge(m.dve_b.sem, m.dve_b.at(c))
                for h in range(MH):
                    last = nc.scalar.mul(s.inter[:, h], m.ps[4 + h][:, W:2 * W], cols(1, h))
                last.then_inc(m.act_c.sem, 1)

            chunk(0, True)
            with act.Fori(1, NMC) as c:
                chunk(c, False)
            act.wait_ge(m.pe_d.sem, m.pe_d.at(1))
            nc.scalar.copy(s.n_rows[0:MH, 0], ps_a[0:MH, 0:P]).then_inc(m.act_d.sem, 1)

        @block.gpsimd
        def _(pool):
            nc.gpsimd.memset(s.c_state, 0.0)
            nc.gpsimd.memset(s.v_ext, 1.0).then_inc(m.pool_b.sem, 1)
            for c in range(NMC):
                pool.wait_ge(m.act_a.sem, m.act_a.at(c + 1))
                nc.gpsimd.affine_select(out=s.decays, in_=s.decays, compare_op=ALU.is_ge, fill=0.0, base=0,
                                        pattern=[[0, MH], [1, MC]], channel_multiplier=-1).then_inc(m.pool_a.sem, 1)

        @block.vector
        def _(dve):
            V = nc.vector

            def chunk(c, first):
                dve.wait_ge(m.pe_a.sem, m.pe_a.at(c + 1))
                dve.wait_ge(m.pool_a.sem, m.pool_a.at(c + 1))
                if not first:
                    dve.wait_ge(m.pe_b.sem, m.pe_b.at(c))
                V.scalar_tensor_tensor(s.probs, heads(ps_s), scale, s.decays, ALU.mult, ALU.mult).then_inc(m.dve_a.sem, 1)
                dve.wait_ge(m.act_c.sem, m.act_c.at(c + 1))
                for h in range(MH):
                    last = V.tensor_tensor(s.num[:, h], m.ps[4 + h][:, 0:W], s.inter[:, h], ALU.add)
                last.then_inc(m.dve_b.sem, 1)
                for h in range(MH):
                    decay = s.decay[:, h, bass.ds(c, 1)]
                    V.tensor_scalar(s.c_state[:, h], s.c_state[:, h], decay, None, ALU.mult)
                V.drain()
                for h in range(MH):
                    last = V.scalar_tensor_tensor(s.c_state[:, h], m.ps[4 + h][:, 2 * W:3 * W], scale,
                                                  s.c_state[:, h], ALU.mult, ALU.add)
                last.then_inc(m.dve_d.sem, 1)
                den = s.num[:, :, DH]
                V.scalar_tensor_tensor(s.den[:, 0], den, -1.0, den, ALU.mult, ALU.max)
                V.drain()
                V.tensor_tensor(s.den[:, 1], s.den[:, 0], s.cols[:, bass.ds(c, 1), 3, :].rearrange("p a h -> p (a h)"), ALU.max)
                V.drain()
                V.reciprocal(s.den[:, 0], s.den[:, 1])
                V.drain()
                if not first:
                    dve.wait_ge(m.pe_c.sem, m.pe_c.at(c))
                V.tensor_tensor(s.h_tok, s.num[:, :, 0:DH], s.den[:, 0].unsqueeze(2).to_broadcast([P, MH, DH]),
                                ALU.mult).then_inc(m.dve_c.sem, 1)
                dve.wait_ge(m.pe_c.sem, m.pe_c.at(c + 1))
                V.tensor_tensor(m.normed[:, 4:8, bass.ds(c * MC, MC)], heads(ps_a),
                                m.proj[:, 16:20, bass.ds(c * MC, MC)], ALU.mult).then_inc(m.dve_e.sem, 1)

            chunk(0, True)
            with dve.Fori(1, NMC) as c:
                chunk(c, False)

    m.dma_a.passed(16 * NMC // 2)
    m.dma_b.passed(16 * NMC // 2)
    m.stored.passed(32)
    for x in (m.pe_a, m.pe_b, m.pe_c, m.act_a, m.act_b, m.act_c, m.pool_a, m.dve_a, m.dve_b, m.dve_c, m.dve_d, m.dve_e):
        x.passed(NMC)
    for x in (m.pe_d, m.act_d, m.pool_b):
        x.passed(1)


def phase_ml_samples(m):
    nc = m.nc
    s = m.ml
    scale = DH ** -0.5
    c = Carver(m.hidden[:])
    c_old = [c.take(MH, DH) for _ in range(2)]
    c_new = [c.take(MH, DH) for _ in range(2)]
    v_tok = c.take(MH, DH, parts=B)
    v_one = [c.take(MH, DH, parts=B) for _ in range(2)]
    q, k, v, o = (m.proj[:, 4 * i:4 * i + 4, T:N] for i in range(1, 5))
    flat = lambda x: x.rearrange("p h v -> p (h v)")
    with nc.Block() as block:

        @block.sync
        def _(sp):
            sp.dma_start(s.n_rows[0:B * MH, 0], m.ins["state_mlstm_n"].rearrange("b h k -> (b h) k")).then_inc(m.dma_c.sem, 16)

            def load(b, slot, first):
                if not first:
                    sp.wait_ge(m.act_a.sem, m.act_a.at(b - 1))
                sem = m.dma_b if slot else m.dma_a
                sp.dma_start(c_old[slot], m.ins["state_mlstm_c"][bass.ds(b, 1)].rearrange("b h k v -> k (b h) v")
                             ).then_inc(sem.sem, 16)

            for b in range(2):
                load(b, b, True)
            with sp.Fori(1, B // 2) as i:
                for slot in range(2):
                    load(i * 2 + slot, slot, False)
            sp.wait_ge(m.act_b.sem, m.act_b.at(1))
            sp.dma_start(m.outs["s_n"].rearrange("b h k -> (b h) k"), s.n_rows[0:B * MH, 1]).then_inc(m.stored.sem, 16)
            sp.wait_ge(m.stored.sem, m.stored.at(16))

        @block.tensor
        def _(pe):
            for h in range(MH):
                last = nc.tensor.transpose(m.ps[0][0:B, h * DH:(h + 1) * DH], v[:, h], m.ident[:])
            last.then_inc(m.pe_a.sem, 1)
            pe.wait_ge(m.dma_c.sem, m.dma_c.at(16))
            nc.tensor.transpose(m.ps[1][:, 0:B * MH], s.n_rows[0:B * MH, 0], m.ident[0:B * MH, 0:B * MH]).then_inc(m.pe_a.sem, 1)
            pe.wait_ge(m.dve_b.sem, m.dve_b.at(1))
            nc.tensor.transpose(m.ps[2][0:B * MH, 0:P], s.nt.rearrange("p b h -> p (b h)"), m.ident[:])
            nc.tensor.matmul(m.ps[3][:, 0:MH * B], m.ones[:], s.prod.rearrange("p h b -> p (h b)"),
                             start=True, stop=True).then_inc(m.pe_b.sem, 1)

            def spread(b, slot, first):
                pe.wait_ge(m.dve_a.sem, m.dve_a.at(b + 1))
                if not first:
                    pe.wait_ge(m.dve_c.sem, m.dve_c.at(b - 1))
                nc.tensor.matmul(m.ps[4 + slot][:], m.ones[0:B, :], flat(v_one[slot]), start=True, stop=True
                                 ).then_inc(m.pe_c.sem, 1)

            def apply(b, slot):
                pe.wait_ge(m.dve_c.sem, m.dve_c.at(b + 1))
                for h in range(MH):
                    last = nc.tensor.matmul(m.ps[6][:, bass.ds(b + h * B, 1)], c_new[slot][:, h], q[:, h, bass.ds(b, 1)],
                                            start=True, stop=True)
                last.then_inc(m.pe_d.sem, 1)

            for b in range(2):
                spread(b, b, True)
            with pe.Fori(0, B // 2 - 1) as i:
                for slot in range(2):
                    apply(i * 2 + slot, slot)
                for slot in range(2):
                    spread(i * 2 + slot + 2, slot, False)
            for slot in range(2):
                apply(B - 2 + slot, slot)

        @block.scalar
        def _(act):
            def decayed(b, slot):
                sem = m.dma_b if slot else m.dma_a
                act.wait_ge(sem.sem, sem.at((b - slot) * 8 + 16))
                if slot >= 0:
                    act.wait_ge(m.dve_d.sem, m.dve_d.at(b + 1))
                for h in range(MH):
                    last = nc.scalar.mul(c_new[slot][:, h], c_old[slot][:, h], s.bc_s[:, 0, h, bass.ds(b, 1)])
                last.then_inc(m.act_a.sem, 1)
                act.wait_ge(m.dve_c.sem, m.dve_c.at(b + 1))
                out = m.dma_h if slot else m.dma_g
                act.dma_start(m.outs["s_c"][bass.ds(b, 1)].rearrange("b h k v -> k (b h) v"), c_new[slot]).then_inc(out.sem, 16)

            with act.Fori(0, B // 2) as i:
                for slot in range(2):
                    decayed(i * 2 + slot, slot)
            act.wait_ge(m.dma_g.sem, m.dma_g.at(16 * B // 2))
            act.wait_ge(m.dma_h.sem, m.dma_h.at(16 * B // 2))
            act.wait_ge(m.pe_b.sem, m.pe_b.at(1))
            nc.scalar.copy(s.n_rows[0:B * MH, 1], m.ps[2][0:B * MH, 0:P]).then_inc(m.act_b.sem, 1)

        @block.vector
        def _(dve):
            V = nc.vector
            by_head = lambda x: x.rearrange("p b h -> p h b")
            dve.wait_ge(m.pe_a.sem, m.pe_a.at(2))
            V.tensor_copy(flat(v_tok), m.ps[0][0:B, :])
            V.scalar_tensor_tensor(s.kw, k, scale, s.bc_s[:, 1], ALU.mult, ALU.mult)
            V.tensor_tensor(s.dn[:, 0], by_head(m.ps[1][:, 0:B * MH].rearrange("p (b h) -> p b h", h=MH)),
                            s.bc_s[:, 0], ALU.mult)
            V.drain()
            V.tensor_tensor(by_head(s.nt), s.dn[:, 0], s.kw, ALU.add)
            V.drain()
            V.tensor_tensor(s.prod, by_head(s.nt), q, ALU.mult).then_inc(m.dve_b.sem, 1)
            dve.wait_ge(m.pe_b.sem, m.pe_b.at(1))
            V.tensor_copy(s.dn[:, 0], m.ps[3][:, 0:MH * B].rearrange("p (h b) -> p h b", h=MH))
            V.drain()
            V.scalar_tensor_tensor(s.dn[:, 1], s.dn[:, 0], -1.0, s.dn[:, 0], ALU.mult, ALU.max)
            V.drain()
            V.tensor_tensor(s.dn[:, 1], s.dn[:, 1], s.bc_s[:, 2], ALU.max)
            V.drain()
            V.reciprocal(s.dn[:, 2], s.dn[:, 1])
            V.memset(s.dn[:, 0], 0.0).then_inc(m.dve_d.sem, 2)

            def alone(b, slot):
                V.tensor_scalar(v_one[slot], v_tok, m.ident[0:B, bass.ds(b, 1)], None, ALU.mult).then_inc(m.dve_a.sem, 1)

            def update(b, slot, last_pair):
                dve.wait_ge(m.pe_c.sem, m.pe_c.at(b + 1))
                dve.wait_ge(m.act_a.sem, m.act_a.at(b + 1))
                for h in range(MH):
                    last = V.scalar_tensor_tensor(c_new[slot][:, h], m.ps[4 + slot][:, h * DH:(h + 1) * DH],
                                                  s.kw[:, h, bass.ds(b, 1)], c_new[slot][:, h], ALU.mult, ALU.add)
                last.then_inc(m.dve_c.sem, 1)
                if not last_pair:
                    alone(b + 2, slot)
                    out = m.dma_h if slot else m.dma_g
                    dve.wait_ge(m.pe_d.sem, m.pe_d.at(b + 1))
                    dve.wait_ge(out.sem, out.at((b - slot) * 8 + 16))
                    V.memset(s.dn[:, 0, 0, 0:1], 0.0).then_inc(m.dve_d.sem, 1)

            for b in range(2):
                alone(b, b)
            with dve.Fori(0, B // 2 - 1) as i:
                for slot in range(2):
                    update(i * 2 + slot, slot, False)
            for slot in range(2):
                update(B - 2 + slot, slot, True)
            dve.wait_ge(m.pe_d.sem, m.pe_d.at(B))
            V.tensor_tensor(s.num_s, m.ps[6][:, 0:MH * B].rearrange("p (h b) -> p h b", h=MH), s.dn[:, 2], ALU.mult)
            V.drain()
            V.tensor_tensor(m.normed[:, 4:8, T:N], s.num_s, o, ALU.mult)

    m.dma_c.passed(16)
    m.stored.passed(16)
    for x in (m.dma_a, m.dma_b, m.dma_g, m.dma_h):
        x.passed(16 * B // 2)
    for x in (m.pe_c, m.pe_d, m.act_a, m.dve_a, m.dve_c, m.dve_d):
        x.passed(B)
    m.pe_a.passed(2)
    for x in (m.pe_b, m.act_b, m.dve_b):
        x.passed(1)


def phase_out(m, w_name):
    nc = m.nc
    w = m.ins[w_name].rearrange("(k p) n -> p k n", p=P)
    with nc.Block() as block:

        @block.scalar
        def _(act):
            act.dma_start(m.resid[:], m.spill).then_inc(m.x_back.sem, 16)

        @block.sync
        def _(sp):
            with sp.Fori(0, KT // 2) as j:
                for slot in range(2):
                    load_unit(sp, m, slot, j, w[:, :, bass.ds((j * 2 + slot) * P, P)])

        @block.tensor
        def _(pe):
            with pe.Fori(0, KT // 2) as j:
                for slot in range(2):
                    unit_matmuls(pe, m, slot, j, m.normed)

        @block.vector
        def _(dve):
            dve.wait_ge(m.x_back.sem, m.x_back.at(16))
            with dve.Fori(0, KT // 2) as j:
                for slot in range(2):
                    add_unit(dve, m, slot, j * 2 + slot, j * 2 + slot)

    m.x_back.passed(16)
    units_passed(m, KT)


def add_unit(dve, m, slot, u, tile):
    nc = m.nc
    dve.wait_ge(m.unit_done.sem, m.unit_done.at(u + 1))
    for c in range(CHUNKS):
        x = m.resid[:, bass.ds(tile, 1), token_cols(c)].rearrange("p a n -> p (a n)")
        last = nc.vector.tensor_tensor(x, m.ps[3 * slot + c][:, 0:CH], x, ALU.add)
    last.then_inc(m.set_free.sem, 1)


def phase_mlp(m, layer):
    nc = m.nc
    w_up = m.ins["w_up"][layer].rearrange("(k p) n -> p k n", p=P)
    w_down = m.ins["w_down"][layer].rearrange("(q k p) n -> p q k n", p=P, k=KT)
    per_group = 2 * KT
    with nc.Block() as block:

        @block.sync
        def _(sp):
            with sp.Fori(0, FF_GROUPS) as g:
                with sp.Fori(0, KT // 2) as j:
                    for slot in range(2):
                        load_unit(sp, m, slot, g * KT + j, w_up[:, :, bass.ds(g * D + (j * 2 + slot) * P, P)])
                with sp.Fori(0, KT // 2) as j:
                    for slot in range(2):
                        load_unit(sp, m, slot, g * KT + KT // 2 + j,
                                  w_down[:, bass.ds(g, 1), :, bass.ds((j * 2 + slot) * P, P)].rearrange("p a k n -> p (a k) n"))

        @block.tensor
        def _(pe):
            norm_pe(pe, m)
            pe.wait_ge(m.mean_set.sem, m.mean_set.at(1))
            pe.wait_ge(m.tiles_ready.sem, m.tiles_ready.at(KT))
            with pe.Fori(0, FF_GROUPS) as g:
                with pe.Fori(0, KT // 2) as j:
                    for slot in range(2):
                        unit_matmuls(pe, m, slot, g * KT + j, m.normed)

                def down(j, slot, first):
                    hidden_tile = lambda k: pe.wait_ge(m.act_a.sem, m.act_a.at(g * KT + k + 1))
                    unit_matmuls(pe, m, slot, g * KT + KT // 2 + j, m.hidden, ready=hidden_tile if first else None)

                down(0, 0, True)
                down(0, 1, False)
                with pe.Fori(1, KT // 2) as j:
                    for slot in range(2):
                        down(j, slot, False)

        @block.scalar
        def _(act):
            norm_act(act, m, m.g_mlp[layer])
            norm_root(act, m)
            with act.Fori(0, FF_GROUPS * KT // 2) as i:
                for slot in range(2):
                    u = i * 2 + slot
                    act.wait_ge(m.dve_a.sem, m.dve_a.at(u + 1))
                    x = m.hidden[:, bass.ds((i % (KT // 2)) * 2 + slot, 1), :].rearrange("p a n -> p (a n)")
                    nc.scalar.activation(x, m.relu[slot][:], ACT.Square).then_inc(m.act_a.sem, 1)

        @block.vector
        def _(dve):
            norm_dve(dve, m)
            dve.wait_ge(m.inv_done.sem, m.inv_done.at(1))

            def rectify(g, j, slot, first=False):
                u = j * 2 + slot
                dve.wait_ge(m.unit_done.sem, m.unit_done.at(g * per_group + u + 1))
                if not first:
                    dve.wait_ge(m.act_a.sem, m.act_a.at(g * KT + u - 1))
                for c in range(CHUNKS):
                    last = nc.vector.scalar_tensor_tensor(m.relu[slot][:, token_cols(c)], m.ps[3 * slot + c][:, 0:CH], 0.0,
                                                          m.inv_rms[:, token_cols(c)], ALU.max, ALU.mult)
                last.then_inc(m.dve_a.sem, 1)
                dve.wait_ge(m.dve_a.sem, m.dve_a.at(g * KT + u + 1))
                nc.vector.memset(m.mark[:], 0.0).then_inc(m.set_free.sem, 1)

            def group(g, first):
                for slot in range(2):
                    rectify(g, 0, slot, first)
                with dve.Fori(1, KT // 2) as j:
                    for slot in range(2):
                        rectify(g, j, slot)
                with dve.Fori(0, KT // 2) as j:
                    for slot in range(2):
                        add_unit(dve, m, slot, g * per_group + KT + j * 2 + slot, j * 2 + slot)

            group(0, True)
            with dve.Fori(1, FF_GROUPS) as g:
                group(g, False)

    norm_passed(m)
    units_passed(m, FF_GROUPS * per_group)
    m.act_a.passed(FF_GROUPS * KT)
    m.dve_a.passed(FF_GROUPS * KT)


def phase_final(m):
    nc = m.nc
    g_row = m.proj[:, 0, 0:D]
    y = [m.proj[:, 2 + i, 0:D] for i in range(2)]
    sq = m.proj[:, 4, 0:D]
    st = m.proj[:, 5, 0:4]
    n_out = TB + 1
    with nc.Block() as block:

        @block.sync
        def _(sp):
            sp.dma_start(g_row, m.ins["norm_final"].partition_broadcast(P)).then_inc(m.dma_a.sem, 16)
            for t in range(n_out):
                sp.wait_ge(m.dve_b.sem, m.dve_b.at(t + 1))
                out = m.dma_c if t % 2 else m.dma_b
                if t < TB:
                    sp.dma_start(m.outs["y_prompt"][0, t * P:(t + 1) * P, :], y[t % 2]).then_inc(out.sem, 16)
                else:
                    sp.dma_start(m.outs["y_sample"].rearrange("b o f -> (b o) f"), y[t % 2][0:B]).then_inc(out.sem, 16)
            sp.wait_ge(m.dma_b.sem, m.dma_b.at(16 * 5))
            sp.wait_ge(m.dma_c.sem, m.dma_c.at(16 * 4))

        @block.tensor
        def _(pe):
            for t in range(n_out):
                n = P if t < TB else B
                if t >= 2:
                    pe.wait_ge(m.dve_b.sem, m.dve_b.at(t - 1))
                for k in range(KT):
                    last = nc.tensor.transpose(m.ps[2 * (t % 2) + k // 4][0:n, (k % 4) * P:(k % 4 + 1) * P],
                                               m.resid[:, k, t * P:t * P + n], m.ident[:])
                last.then_inc(m.pe_a.sem, 1)

        @block.scalar
        def _(act):
            for t in range(n_out):
                n = P if t < TB else B
                act.wait_ge(m.pe_a.sem, m.pe_a.at(t + 1))
                if t >= 1:
                    act.wait_ge(m.dve_a.sem, m.dve_a.at(t))
                act.drain()
                for half in range(2):
                    last = nc.scalar.activation(sq[0:n, 512 * half:512 * half + 512], m.ps[2 * (t % 2) + half][0:n, :],
                                                ACT.Square, accum_out=st[0:n, half:half + 1])
                last.then_inc(m.act_a.sem, 1)
                act.wait_ge(m.dve_a.sem, m.dve_a.at(t + 1))
                nc.scalar.activation(st[0:n, 3:4], st[0:n, 2:3], ACT.Sqrt).then_inc(m.act_b.sem, 1)

        @block.vector
        def _(dve):
            V = nc.vector
            for t in range(n_out):
                n = P if t < TB else B
                dve.wait_ge(m.act_a.sem, m.act_a.at(t + 1))
                V.tensor_tensor(st[0:n, 2:3], st[0:n, 0:1], st[0:n, 1:2], ALU.add)
                V.drain()
                V.tensor_scalar(st[0:n, 2:3], st[0:n, 2:3], 1.0 / D, EPS, ALU.mult, ALU.add)
                V.drain()
                V.reciprocal(st[0:n, 2:3], st[0:n, 2:3]).then_inc(m.dve_a.sem, 1)
                if t == 0:
                    dve.wait_ge(m.dma_a.sem, m.dma_a.at(16))
                if t >= 2:
                    out = m.dma_c if t % 2 else m.dma_b
                    dve.wait_ge(out.sem, out.at(16 * (t // 2)))
                dve.wait_ge(m.act_b.sem, m.act_b.at(t + 1))
                for half in range(2):
                    h = slice(512 * half, 512 * half + 512)
                    last = V.scalar_tensor_tensor(y[t % 2][0:n, h], m.ps[2 * (t % 2) + half][0:n, :], st[0:n, 3:4],
                                                  g_row[0:n, h], ALU.mult, ALU.mult)
                last.then_inc(m.dve_b.sem, 1)

    m.dma_a.passed(16)
    m.dma_b.passed(16 * 5)
    m.dma_c.passed(16 * 4)
    for x in (m.pe_a, m.act_a, m.act_b, m.dve_a, m.dve_b):
        x.passed(n_out)


QT, KT1, VT1, QIT, KI, KI2 = 0, 8, 10, 12, 16, 17


def score_width(i):
    return P * (i + 1)


def l1_tiles(m):
    s = m.l1 = Tiles()
    c = Carver(m.hidden[:])
    s.v_tok = c.take(TB, KVH * DH)
    s.score = [c.take(score_width(i)) for i in range(TB)]
    s.samples = m.proj[0:B, 18, :]
    s.new = m.proj[0:B, 19, 0:1]
    x = Carver(m.s5_small[:])
    s.w_last = x.take(KT, IDIM + IH)
    s.w_tok = x.take(TB, IH)
    s.qi_s = x.take(B, IH, parts=IDIM)
    s.w_s = x.take(B, parts=IH)
    s.table = x.take(B * PAGES, parts=1).bitcast(I32)
    s.q_s = x.take(B, AH)
    s.cand = x.take(TB)
    s.cnt = x.take(TB)
    s.prefix = x.take(TB).bitcast(I32)
    s.key = x.take(TB).bitcast(I32)
    s.flip = x.take(TB).bitcast(I32)
    s.bit = x.take(TB).bitcast(I32)
    s.tau = x.take(TB)
    s.need = x.take(TB)
    s.sel = x.take(B, 36, parts=B)
    s.stat = x.take(16)
    return s


def phase_in1(m):
    nc = m.nc
    s = l1_tiles(m)
    w_in = m.ins["w_in1"].rearrange("(k p) n -> p k n", p=P)
    units = 16
    M = IDIM + IH
    with nc.Block() as block:

        @block.sync
        def _(sp):
            sp.dma_start(m.spill, m.resid[:]).then_inc(m.x_stored.sem, 16)
            sp.dma_start(s.w_last, w_in[:, :, units * P:units * P + M]).then_inc(m.dma_a.sem, 16)
            with sp.Fori(0, units // 2) as j:
                for slot in range(2):
                    load_unit(sp, m, slot, j, w_in[:, :, bass.ds((j * 2 + slot) * P, P)])
            sp.wait_ge(m.x_stored.sem, m.x_stored.at(16))

        @block.tensor
        def _(pe):
            norm_pe(pe, m)
            pe.wait_ge(m.mean_set.sem, m.mean_set.at(1))
            pe.wait_ge(m.tiles_ready.sem, m.tiles_ready.at(KT))
            with pe.Fori(0, units // 2) as j:
                for slot in range(2):
                    unit_matmuls(pe, m, slot, j, m.normed)
            pe.wait_ge(m.dma_a.sem, m.dma_a.at(16))
            pe.wait_ge(m.set_free.sem, m.set_free.at(units + 1))
            for k in range(KT):
                for c in range(CHUNKS):
                    last = nc.tensor.matmul(m.ps[c][0:M, 0:CH], s.w_last[:, k, :], m.normed[:, k, token_cols(c)],
                                            start=(k == 0), stop=(k == KT - 1))
            last.then_inc(m.pe_a.sem, 1)

        @block.scalar
        def _(act):
            norm_act(act, m, m.g_mix[1])
            norm_root(act, m)

        @block.vector
        def _(dve):
            norm_dve(dve, m)
            dve.wait_ge(m.inv_done.sem, m.inv_done.at(1))
            with dve.Fori(0, units // 2) as j:
                for slot in range(2):
                    u = j * 2 + slot
                    dve.wait_ge(m.unit_done.sem, m.unit_done.at(u + 1))
                    for c in range(CHUNKS):
                        last = nc.vector.tensor_tensor(
                            m.proj[:, bass.ds(u, 1), token_cols(c)].rearrange("p a n -> p (a n)"),
                            m.ps[3 * slot + c][:, 0:CH], m.inv_rms[:, token_cols(c)], ALU.mult)
                    last.then_inc(m.set_free.sem, 1)
            dve.wait_ge(m.pe_a.sem, m.pe_a.at(1))
            for c in range(CHUNKS):
                nc.vector.tensor_tensor(m.proj[0:M, KI, token_cols(c)], m.ps[c][0:M, 0:CH],
                                        m.inv_rms[0:M, token_cols(c)], ALU.mult)

    m.pe_a.passed(1)
    m.dma_a.passed(16)
    m.x_stored.passed(16)
    norm_passed(m)
    units_passed(m, units)


def phase_rows(m):
    nc = m.nc
    s = m.l1
    r = Carver(m.resid[:])
    k_rows = r.take(TB, KVH * DH)
    ki_rows = r.take(TB, IDIM)
    smp = r.take(2 * KVH * DH + IDIM, parts=B)
    x = m.proj
    n_blocks = TB + 1
    with nc.Block() as block:

        @block.tensor
        def _(pe):
            for t in range(n_blocks):
                n = P if t < TB else B
                cols = slice(t * P, t * P + n)
                if t >= 2:
                    pe.wait_ge(m.dve_a.sem, m.dve_a.at(t - 1))
                    pe.wait_ge(m.act_a.sem, m.act_a.at(t - 1))
                for i, tile in enumerate((KT1, KT1 + 1, VT1, VT1 + 1)):
                    nc.tensor.transpose(m.ps[2 * (t % 2) + i // 2][0:n, (i % 2) * P:(i % 2 + 1) * P], x[:, tile, cols], m.ident[:])
                nc.tensor.transpose(m.ps[4 + t % 2][0:n, 0:IDIM + IH], x[0:IDIM + IH, KI, cols],
                                    m.ident[0:IDIM + IH, 0:IDIM + IH]).then_inc(m.pe_a.sem, 1)

        @block.vector
        def _(dve):
            V = nc.vector
            for t in range(TB):
                dve.wait_ge(m.pe_a.sem, m.pe_a.at(t + 1))
                V.tensor_copy(k_rows[:, t], m.ps[2 * (t % 2)][:, 0:KVH * DH])
                V.tensor_copy(ki_rows[:, t], m.ps[4 + t % 2][:, 0:IDIM])
                V.tensor_scalar(s.w_tok[:, t], m.ps[4 + t % 2][:, IDIM:IDIM + IH], (IDIM * IH) ** -0.5, None,
                                ALU.mult).then_inc(m.dve_a.sem, 1)
            dve.wait_ge(m.pe_a.sem, m.pe_a.at(n_blocks))
            V.tensor_copy(smp[:, 0:KVH * DH], m.ps[0][0:B, 0:KVH * DH])
            V.tensor_copy(smp[:, 2 * KVH * DH:], m.ps[4][0:B, 0:IDIM]).then_inc(m.dve_b.sem, 1)
            V.tensor_copy(x[IDIM:P, KI2, 0:T], x[0:IDIM, KI, 0:T])
            V.tensor_scalar(s.w_s, x[IDIM:IDIM + IH, KI, T:N], (IDIM * IH) ** -0.5, None, ALU.mult)
            for half in range(2):
                V.tensor_copy(s.qi_s[:, :, half::2].rearrange("p b t -> p t b"),
                              x[IDIM * half:IDIM * half + IDIM, QIT:QIT + 4, T:N])
            V.tensor_copy(s.q_s.rearrange("p b h -> p h b"), x[:, QT:QT + AH, T:N])

        @block.scalar
        def _(act):
            for t in range(TB):
                act.wait_ge(m.pe_a.sem, m.pe_a.at(t + 1))
                nc.scalar.copy(s.v_tok[:, t], m.ps[2 * (t % 2) + 1][:, 0:KVH * DH]).then_inc(m.act_a.sem, 1)
            act.wait_ge(m.pe_a.sem, m.pe_a.at(n_blocks))
            nc.scalar.copy(smp[:, KVH * DH:2 * KVH * DH], m.ps[1][0:B, 0:KVH * DH]).then_inc(m.act_b.sem, 1)

        @block.gpsimd
        def _(pool):
            for i in range(2):
                nc.gpsimd.memset(s.score[i], 0.0)
            nc.gpsimd.memset(s.sel, 1.0)
            pool.drain()
            for i in range(2):
                nc.gpsimd.affine_select(out=s.score[i], in_=s.score[i], compare_op=ALU.is_ge, fill=NEG, base=P * i,
                                        pattern=[[-1, score_width(i)]], channel_multiplier=1)
            nc.gpsimd.affine_select(out=s.sel, in_=s.sel, compare_op=ALU.is_equal, fill=0.0, base=0,
                                    pattern=[[-1, B], [0, 36]], channel_multiplier=1)

        @block.sync
        def _(sp):
            sp.dma_start(s.table, m.ins["page_table"].rearrange("(a b) j -> a (b j)", a=1)).then_inc(m.dma_a.sem, 16)
            sp.wait_ge(m.dve_a.sem, m.dve_a.at(TB))
            sp.dma_start(m.outs["p_k"].rearrange("b (t p) h d -> p (b t) (h d)", p=P), k_rows).then_inc(m.stored.sem, 16)
            sp.dma_start(m.outs["p_kidx"].rearrange("b (t p) d -> p (b t) d", p=P), ki_rows).then_inc(m.stored.sem, 16)
            sp.wait_ge(m.act_a.sem, m.act_a.at(TB))
            sp.dma_start(m.outs["p_v"].rearrange("b (t p) h d -> p (b t) (h d)", p=P), s.v_tok).then_inc(m.stored.sem, 16)
            sp.wait_ge(m.dve_b.sem, m.dve_b.at(1))
            sp.wait_ge(m.act_b.sem, m.act_b.at(1))
            for i, name in enumerate(("s_k", "s_v")):
                sp.dma_start(m.outs[name].rearrange("b a h d -> (b a) (h d)"), smp[:, KVH * DH * i:KVH * DH * (i + 1)]
                             ).then_inc(m.stored.sem, 16)
            sp.dma_start(m.outs["s_kidx"].rearrange("b a d -> (b a) d"), smp[:, 2 * KVH * DH:]).then_inc(m.stored.sem, 16)
            sp.wait_ge(m.stored.sem, m.stored.at(6 * 16))
            sp.wait_ge(m.dma_a.sem, m.dma_a.at(16))

    m.pe_a.passed(n_blocks)
    m.dve_a.passed(TB)
    m.act_a.passed(TB)
    m.dve_b.passed(1)
    m.act_b.passed(1)
    m.dma_a.passed(16)
    m.stored.passed(6 * 16)


def phase_index(m):
    nc = m.nc
    s = m.l1
    x = m.proj
    r = Carver(m.resid[:])
    rect = [r.take(1024) for _ in range(2)]
    steps = [(i, h) for i in range(2, TB) for h in range(IH)]
    with nc.Block() as block:

        @block.tensor
        def _(pe):
            for n, (i, h) in enumerate(steps):
                if n >= 4:
                    pe.wait_ge(m.act_a.sem, m.act_a.at(n - 3))
                half, w = h % 2, score_width(i)
                rows = slice(IDIM * half, IDIM * half + IDIM)
                for c in range(0, w, 512):
                    e = min(w, c + 512)
                    last = nc.tensor.matmul(m.ps[2 * (n % 4) + c // 512][:, 0:e - c], x[rows, QIT + h // 2, i * P:(i + 1) * P],
                                            x[rows, KI2 if half else KI, c:e], start=True, stop=True)
                last.then_inc(m.pe_a.sem, 1)

        @block.scalar
        def _(act):
            for n, (i, h) in enumerate(steps):
                act.wait_ge(m.pe_a.sem, m.pe_a.at(n + 1))
                if n >= 2:
                    act.wait_ge(m.dve_a.sem, m.dve_a.at(n - 1))
                w = score_width(i)
                for c in range(0, w, 512):
                    e = min(w, c + 512)
                    last = nc.scalar.activation(rect[n % 2][:, c:e], m.ps[2 * (n % 4) + c // 512][:, 0:e - c], ACT.Relu)
                last.then_inc(m.act_a.sem, 1)

        @block.vector
        def _(dve):
            V = nc.vector
            for n, (i, h) in enumerate(steps):
                dve.wait_ge(m.act_a.sem, m.act_a.at(n + 1))
                V.drain()
                w = score_width(i)
                if h == 0:
                    ins = V.tensor_scalar(s.score[i], rect[n % 2][:, 0:w], s.w_tok[:, i, h:h + 1], None, ALU.mult)
                else:
                    ins = V.scalar_tensor_tensor(s.score[i], rect[n % 2][:, 0:w], s.w_tok[:, i, h:h + 1], s.score[i],
                                                 ALU.mult, ALU.add)
                ins.then_inc(m.dve_a.sem, 1)

        @block.gpsimd
        def _(pool):
            for i in range(2, TB):
                pool.wait_ge(m.dve_a.sem, m.dve_a.at(IH * (i - 1)))
                diag = s.score[i][:, i * P:(i + 1) * P]
                nc.gpsimd.affine_select(out=diag, in_=diag, compare_op=ALU.is_ge, fill=NEG, base=0,
                                        pattern=[[-1, P]], channel_multiplier=1)

    m.pe_a.passed(len(steps))
    m.act_a.passed(len(steps))
    m.dve_a.passed(len(steps))


def phase_index_samples(m):
    nc = m.nc
    s = m.l1
    r = Carver(m.resid[:])
    pages = [r.take(PAGES, IDIM) for _ in range(2)]
    keys = r.take(PAST + 1, parts=IDIM)
    rect = r.take(PAST + 1, parts=IH)
    row = r.take(PAST + 1, parts=1)
    qi = r.take(IH, parts=IDIM)
    pieces = ((0, 512), (512, 1024), (1024, 1025))
    last_page = m.ins["cache_kidx"].shape[0] - 1
    with nc.Block() as block:

        @block.sync
        def _(sp):
            def load(b, slot, first):
                sem = m.dma_b if slot else m.dma_a
                if not first:
                    sp.wait_ge(m.pe_a.sem, m.pe_a.at(b - 1))
                for j in range(PAGES):
                    page = sp.value_load(s.table[0:1, b * PAGES + j:b * PAGES + j + 1], min_val=0, max_val=last_page)
                    sp.dma_start(pages[slot][:, j], m.ins["cache_kidx"][bass.ds(page, 1)].rearrange("a p d -> p (a d)")
                                 ).then_inc(sem.sem, 16)

            for b in range(B):
                load(b, b % 2, b < 2)
            sp.wait_ge(m.dma_c.sem, m.dma_c.at(16 * B))
            sp.dma_start(s.samples[:, 0:PAST + 1], m.score_dram).then_inc(m.dma_d.sem, 16)
            sp.wait_ge(m.dma_d.sem, m.dma_d.at(16))

        @block.tensor
        def _(pe):
            def sample(b, slot, first):
                sem = m.dma_b if slot else m.dma_a
                pe.wait_ge(sem.sem, sem.at((b - slot) * (8 * PAGES) + 16 * PAGES))
                if not first:
                    pe.wait_ge(m.act_a.sem, m.act_a.at(b))
                for j in range(PAGES):
                    last = nc.tensor.transpose(m.ps[j // 4][0:IDIM, (j % 4) * PAGE:(j % 4 + 1) * PAGE], pages[slot][:, j], m.ident[:])
                last.then_inc(m.pe_a.sem, 1)
                pe.wait_ge(m.act_a.sem, m.act_a.at(b + 1))
                pe.wait_ge(m.dve_a.sem, m.dve_a.at(b + 1))
                for n, (c, e) in enumerate(pieces):
                    last = nc.tensor.matmul(m.ps[2 + n][0:IH, 0:e - c], qi, keys[:, c:e], start=True, stop=True)
                last.then_inc(m.pe_b.sem, 1)
                pe.wait_ge(m.dve_b.sem, m.dve_b.at(b + 1))
                if not first:
                    pe.wait_ge(m.act_b.sem, m.act_b.at(b))
                for n, (c, e) in enumerate(pieces):
                    last = nc.tensor.matmul(m.ps[5 + n][0:1, 0:e - c], m.ones[0:IH, 0:1], rect[:, c:e], start=True, stop=True)
                last.then_inc(m.pe_c.sem, 1)

            for b in range(B):
                sample(b, b % 2, b == 0)

        @block.scalar
        def _(act):
            def sample(b, first):
                act.wait_ge(m.pe_a.sem, m.pe_a.at(b + 1))
                if not first:
                    act.wait_ge(m.pe_b.sem, m.pe_b.at(b))
                for half in range(2):
                    last = nc.scalar.copy(keys[:, 512 * half:512 * half + 512], m.ps[half][0:IDIM, :])
                last.then_inc(m.act_a.sem, 1)
                act.wait_ge(m.pe_c.sem, m.pe_c.at(b + 1))
                if not first:
                    act.wait_ge(m.dma_c.sem, m.dma_c.at(b * 16))
                for n, (c, e) in enumerate(pieces):
                    last = nc.scalar.copy(row[:, c:e], m.ps[5 + n][0:1, 0:e - c])
                last.then_inc(m.act_b.sem, 1)
                act.wait_ge(m.act_b.sem, m.act_b.at(b + 1))
                act.dma_start(m.score_dram[bass.ds(b, 1)], row).then_inc(m.dma_c.sem, 16)

            sample(0, True)
            with act.Fori(1, B) as b:
                sample(b, False)

        @block.vector
        def _(dve):
            V = nc.vector

            def sample(b, first):
                if not first:
                    dve.wait_ge(m.pe_b.sem, m.pe_b.at(b))
                V.tensor_copy(keys[:, PAST:PAST + 1], m.proj[0:IDIM, KI, bass.ds(b + T, 1)])
                V.tensor_copy(qi, s.qi_s[:, bass.ds(b, 1), :].rearrange("p a h -> p (a h)")).then_inc(m.dve_a.sem, 1)
                dve.wait_ge(m.pe_b.sem, m.pe_b.at(b + 1))
                if not first:
                    dve.wait_ge(m.pe_c.sem, m.pe_c.at(b))
                for n, (c, e) in enumerate(pieces):
                    last = V.tensor_scalar(rect[:, c:e], m.ps[2 + n][0:IH, 0:e - c], 0.0, s.w_s[:, bass.ds(b, 1)],
                                           ALU.max, ALU.mult)
                last.then_inc(m.dve_b.sem, 1)

            sample(0, True)
            with dve.Fori(1, B) as b:
                sample(b, False)

    m.dma_a.passed(16 * PAGES * B // 2)
    m.dma_b.passed(16 * PAGES * B // 2)
    m.dma_c.passed(16 * B)
    m.dma_d.passed(16)
    for q in (m.pe_a, m.pe_b, m.pe_c, m.act_a, m.act_b, m.dve_a, m.dve_b):
        q.passed(B)


def phase_topk(m):
    nc = m.nc
    s = m.l1
    r = Carver(m.resid[:])
    junk = r.take(1032)
    equal = r.take(1032)
    rank = r.take(1032)
    sets = [(0, s.samples[:, 0:PAST + 1], B)] + [(i, s.score[i], P) for i in range(2, TB)]
    SIGN = -2 ** 31
    with nc.Block() as block:

        @block.vector
        def _(dve):
            V = nc.vector
            V.memset(s.prefix, 0)
            V.memset(s.bit, SIGN)
            V.memset(s.cnt, 0.0)
            V.drain()
            with dve.Fori(0, 32):
                V.tensor_tensor(s.key, s.prefix, s.bit, ALU.bitwise_or)
                V.drain()
                V.tensor_scalar(s.flip, s.key, 31, -1, ALU.arith_shift_right, ALU.bitwise_xor)
                V.drain()
                V.tensor_scalar(s.flip, s.flip, SIGN, None, ALU.bitwise_or)
                V.drain()
                V.tensor_tensor(s.cand.bitcast(I32), s.key, s.flip, ALU.bitwise_xor)
                V.drain()
                for i, x, n in sets:
                    V.tensor_scalar(junk[0:n, 0:x.shape[1]], x, s.cand[0:n, i:i + 1], 0.0, ALU.is_ge, ALU.add,
                                    accum_out=s.cnt[0:n, i:i + 1])
                    V.drain()
                V.tensor_scalar(s.flip, s.cnt, TOPK - 0.5, -1.0, ALU.is_ge, ALU.mult)
                V.drain()
                V.tensor_tensor(s.key, s.flip, s.bit, ALU.bitwise_and)
                V.drain()
                V.tensor_tensor(s.prefix, s.prefix, s.key, ALU.bitwise_or)
                V.tensor_scalar(s.flip, s.bit, 1, None, ALU.logical_shift_right)
                V.drain()
                V.tensor_copy(s.bit, s.flip)
                V.drain()
            V.tensor_scalar(s.flip, s.prefix, 31, -1, ALU.arith_shift_right, ALU.bitwise_xor)
            V.drain()
            V.tensor_scalar(s.flip, s.flip, SIGN, None, ALU.bitwise_or)
            V.drain()
            V.tensor_tensor(s.tau.bitcast(I32), s.prefix, s.flip, ALU.bitwise_xor)
            V.drain()
            for i, x, n in sets:
                w = x.shape[1]
                tau, cnt, need = s.tau[0:n, i:i + 1], s.cnt[0:n, i:i + 1], s.need[0:n, i:i + 1]
                V.tensor_scalar(junk[0:n, 0:w], x, tau, 0.0, ALU.is_gt, ALU.add, accum_out=cnt)
                V.tensor_scalar(equal[0:n, 0:w], x, tau, None, ALU.is_equal)
                V.drain()
                V.tensor_scalar(need, cnt, -1.0, float(TOPK), ALU.mult, ALU.add)
                V.tensor_tensor_scan(rank[0:n, 0:w], equal[0:n, 0:w], equal[0:n, 0:w], 0.0, ALU.add, ALU.max)
                V.drain()
                V.scalar_tensor_tensor(rank[0:n, 0:w], rank[0:n, 0:w], need, equal[0:n, 0:w], ALU.is_le, ALU.mult)
                V.drain()
                V.tensor_tensor(rank[0:n, 0:w], rank[0:n, 0:w], junk[0:n, 0:w], ALU.add)
                V.drain()
                V.tensor_scalar(x, rank[0:n, 0:w], -NEG, NEG, ALU.mult, ALU.add)
                V.drain()


def phase_attend(m):
    nc = m.nc
    s = m.l1
    scale = DH ** -0.5
    r = Carver(m.resid[:])
    q = [r.take(P) for _ in range(2)]
    masked = [r.take(T) for _ in range(2)]
    probs_t = r.take(TB, P)
    o_tok = [r.take(DH) for _ in range(2)]
    ps_s = [m.ps_pair[0], m.ps_pair[1]]
    ps_t = m.ps_pair[2]
    ps_o, ps_ot = m.ps[6], m.ps[7]
    st = s.stat
    k_t = m.proj
    flat = lambda ap: ap.rearrange("p a n -> p (a n)")
    with nc.Block() as block:
        n_units = TB * AH

        @block.sync
        def _(sp):
            def load(n, h, slot, i, first):
                if not first:
                    sp.wait_ge(m.pe_a.sem, m.pe_a.at(n - 1))
                sem = m.dma_b if slot else m.dma_a
                sp.dma_start(q[slot], flat(m.proj[:, bass.ds(h, 1), i * P:(i + 1) * P])).then_inc(sem.sem, 16)

            for i in range(TB):
                if i == 0:
                    load(0, 0, 0, 0, True)
                    load(1, 1, 1, 0, True)
                with sp.Fori(1 if i == 0 else 0, AH // 2) as j:
                    for slot in range(2):
                        load(i * AH + j * 2 + slot, j * 2 + slot, slot, i, False)

        @block.tensor
        def _(pe):
            def scores(n, g, slot, i, first):
                sem = m.dma_b if slot else m.dma_a
                pe.wait_ge(sem.sem, sem.at((n - slot) * 8 + 16))
                if not first:
                    pe.wait_ge(m.dve_a.sem, m.dve_a.at(n - 1))
                w = score_width(i)
                for c in range(0, w, 512):
                    e = min(w, c + 512)
                    last = nc.tensor.matmul(ps_s[slot][:, c:e], q[slot], flat(k_t[:, bass.ds(g + KT1, 1), c:e]),
                                            start=True, stop=True)
                last.then_inc(m.pe_a.sem, 1)

            def values(n, g, slot, i, first):
                pe.wait_ge(m.act_a.sem, m.act_a.at(n + 1))
                if not first:
                    pe.wait_ge(m.act_b.sem, m.act_b.at(n))
                    pe.wait_ge(m.dve_b.sem, m.dve_b.at(n))
                for b in range(i + 1):
                    last = nc.tensor.transpose(ps_t[:, b * P:(b + 1) * P], masked[slot][:, b * P:(b + 1) * P], m.ident[:])
                last.then_inc(m.pe_b.sem, 1)
                pe.wait_ge(m.act_b.sem, m.act_b.at(n + 1))
                pe.wait_ge(m.dve_b.sem, m.dve_b.at(n + 1))
                if not first:
                    pe.wait_ge(m.dve_c.sem, m.dve_c.at(n))
                for b in range(i + 1):
                    last = nc.tensor.matmul(ps_o[:, 0:DH], probs_t[:, b], s.v_tok[:, b, bass.ds(g * DH, DH)],
                                            start=(b == 0), stop=(b == i))
                last.then_inc(m.pe_c.sem, 1)

            def turn(n, slot, first):
                pe.wait_ge(m.dve_c.sem, m.dve_c.at(n + 1))
                if not first:
                    pe.wait_ge(m.act_c.sem, m.act_c.at(n))
                nc.tensor.transpose(ps_ot[:, 0:P], o_tok[slot], m.ident[:]).then_inc(m.pe_d.sem, 1)

            for i in range(TB):
                n0 = i * AH
                scores(n0, 0, 0, i, i == 0)
                scores(n0 + 1, 0, 1, i, i == 0)
                values(n0, 0, 0, i, i == 0)
                scores(n0 + 2, 0, 0, i, False)
                turn(n0, 0, i == 0)
                values(n0 + 1, 0, 1, i, False)
                scores(n0 + 3, 0, 1, i, False)
                turn(n0 + 1, 1, False)
                with pe.Fori(1, AH // 2 - 1) as j:
                    for slot in range(2):
                        n = n0 + j * 2 + slot
                        values(n, j // 2, slot, i, False)
                        scores(n + 2, (j + 1) // 2, slot, i, False)
                        turn(n, slot, False)
                for slot in range(2):
                    n = n0 + AH - 2 + slot
                    values(n, KVH - 1, slot, i, False)
                    turn(n, slot, False)

        @block.vector
        def _(dve):
            V = nc.vector

            def mask(n, slot, i, first):
                w = score_width(i)
                a = 4 * slot
                dve.wait_ge(m.pe_a.sem, m.pe_a.at(n + 1))
                V.memset(m.mark[:, 0:1], 0.0)
                if not first:
                    dve.wait_ge(m.pe_b.sem, m.pe_b.at(n - 1))
                V.memset(m.mark[:, 1:2], 0.0)
                V.tensor_tensor_reduce(masked[slot][:, 0:w], ps_s[slot][:, 0:w], s.score[i], 1.0, -3e38, ALU.add, ALU.max,
                                       st[:, a:a + 1])
                V.drain()
                V.tensor_scalar(st[:, a + 1:a + 2], st[:, a:a + 1], -scale, None, ALU.mult).then_inc(m.dve_a.sem, 1)

            def copy_t(n, slot, i):
                half = (i + 1) // 2
                dve.wait_ge(m.pe_b.sem, m.pe_b.at(n + 1))
                V.memset(m.mark[:, 2:3], 0.0)
                ins = V.tensor_copy(probs_t[:, 0:half].rearrange("p a n -> p (a n)"), ps_t[:, 0:half * P]) if half else \
                    V.memset(m.mark[:, 3:4], 0.0)
                ins.then_inc(m.dve_b.sem, 1)

            def norm(n, slot):
                a = 4 * slot
                V.reciprocal(st[:, a + 3:a + 4], st[:, a + 2:a + 3])
                V.drain()
                dve.wait_ge(m.pe_c.sem, m.pe_c.at(n + 1))
                V.tensor_scalar(o_tok[slot], ps_o[:, 0:DH], st[:, a + 3:a + 4], None, ALU.mult).then_inc(m.dve_c.sem, 1)

            for i in range(TB):
                n0 = i * AH
                mask(n0, 0, i, i == 0)
                mask(n0 + 1, 1, i, i == 0)
                with dve.Fori(0, AH // 2 - 1) as j:
                    for slot in range(2):
                        n = n0 + j * 2 + slot
                        copy_t(n, slot, i)
                        norm(n, slot)
                        mask(n + 2, slot, i, False)
                for slot in range(2):
                    n = n0 + AH - 2 + slot
                    copy_t(n, slot, i)
                    norm(n, slot)

        @block.scalar
        def _(act):
            def exps(n, slot, i):
                a = 4 * slot
                w = score_width(i)
                act.wait_ge(m.dve_a.sem, m.dve_a.at(n + 1))
                nc.scalar.activation(masked[slot][:, 0:w], masked[slot][:, 0:w], ACT.Exp, bias=st[:, a + 1:a + 2],
                                     scale=scale, accum_out=st[:, a + 2:a + 3]).then_inc(m.act_a.sem, 1)

            def rest(n, h, slot, i):
                half = (i + 1) // 2
                act.wait_ge(m.pe_b.sem, m.pe_b.at(n + 1))
                act.wait_ge(m.dve_b.sem, m.dve_b.at(n + 1))
                nc.scalar.copy(probs_t[:, half:i + 1].rearrange("p a n -> p (a n)"), ps_t[:, half * P:(i + 1) * P]
                               ).then_inc(m.act_b.sem, 1)
                act.wait_ge(m.pe_d.sem, m.pe_d.at(n + 1))
                nc.scalar.copy(flat(m.normed[:, bass.ds(h, 1), i * P:(i + 1) * P]), ps_ot[:, 0:P]).then_inc(m.act_c.sem, 1)

            for i in range(TB):
                n0 = i * AH
                exps(n0, 0, i)
                exps(n0 + 1, 1, i)
                with act.Fori(0, AH // 2 - 1) as j:
                    for slot in range(2):
                        h = j * 2 + slot
                        rest(n0 + h, h, slot, i)
                        exps(n0 + h + 2, slot, i)
                for slot in range(2):
                    rest(n0 + AH - 2 + slot, AH - 2 + slot, slot, i)

    m.dma_a.passed(16 * n_units // 2)
    m.dma_b.passed(16 * n_units // 2)
    for x in (m.pe_a, m.pe_b, m.pe_c, m.pe_d, m.act_a, m.act_b, m.act_c, m.dve_a, m.dve_b, m.dve_c):
        x.passed(n_units)


def phase_attend_samples(m):
    nc = m.nc
    s = m.l1
    scale = DH ** -0.5
    R = 36
    r = Carver(m.resid[:])
    k_page = r.take(PAGES, KVH * DH)
    v_page = r.take(PAGES, KVH * DH)
    c = Carver(m.hidden[:])
    keys = c.take(KVH, PAST + 1)
    masked = c.take(PAST + 1, parts=R)
    probs_t = c.take(PAGES, R)
    new_t = c.take(R, parts=1)
    v_new = c.take(KVH * DH, parts=1)
    q = c.take(AH)
    sel = c.take(R, parts=B)
    pieces = ((0, 512), (512, 1024), (1024, 1025))
    n_pages = m.ins["cache_k"].shape[0]
    st = s.stat
    with nc.Block() as block:

        @block.sync
        def _(sp):
            def load(b, first):
                for j in range(PAGES):
                    page = sp.value_load(s.table[0:1, b * PAGES + j:b * PAGES + j + 1], min_val=0, max_val=n_pages - 1)
                    if j == 0 and not first:
                        sp.wait_ge(m.pe_a.sem, m.pe_a.at(b))
                        sp.wait_ge(m.pe_d.sem, m.pe_d.at(b))
                    sp.dma_start(k_page[:, j], m.ins["cache_k"][bass.ds(page, 1)].rearrange("a p h d -> p (a h d)")
                                 ).then_inc(m.dma_a.sem, 16)
                    sp.dma_start(v_page[:, j], m.ins["cache_v"][bass.ds(page, 1)].rearrange("a p h d -> p (a h d)")
                                 ).then_inc(m.dma_b.sem, 16)
                sp.dma_start(v_new, m.outs["s_v"][bass.ds(b, 1)].rearrange("b a h d -> (b a) (h d)")).then_inc(m.dma_b.sem, 16)

            for b in range(B):
                load(b, b == 0)

        @block.tensor
        def _(pe):
            def sample(b, first):
                pe.wait_ge(m.dma_a.sem, m.dma_a.at(b * (16 * PAGES) + 16 * PAGES))
                if not first:
                    pe.wait_ge(m.act_a.sem, m.act_a.at(b))
                    pe.wait_ge(m.dve_a.sem, m.dve_a.at(b))
                    pe.wait_ge(m.act_c.sem, m.act_c.at(b))
                for g in range(KVH):
                    for j in range(PAGES):
                        last = nc.tensor.transpose(m.ps_pair[g][:, j * PAGE:(j + 1) * PAGE],
                                                   k_page[:, j, g * DH:(g + 1) * DH], m.ident[:])
                last.then_inc(m.pe_a.sem, 1)
                pe.wait_ge(m.act_a.sem, m.act_a.at(b + 1))
                pe.wait_ge(m.dve_a.sem, m.dve_a.at(b + 1))
                if not first:
                    pe.wait_ge(m.dve_c.sem, m.dve_c.at(b))
                for n, (c0, e) in enumerate(pieces):
                    ps = m.ps[4 + n][:, 0:e - c0]
                    nc.tensor.matmul(ps[0:R], sel, s.samples[:, c0:e], start=True, stop=False, skip_group_check=True)
                    for g in range(KVH):
                        last = nc.tensor.matmul(ps[32 * g:32 * g + AG], q[:, g * AG:(g + 1) * AG], keys[:, g, c0:e],
                                                start=False, stop=True, skip_group_check=True)
                last.then_inc(m.pe_b.sem, 1)
                pe.wait_ge(m.dve_b.sem, m.dve_b.at(b + 1))
                for j in range(PAGES):
                    nc.tensor.transpose(m.ps[7][:, j * R:(j + 1) * R], masked[:, j * PAGE:(j + 1) * PAGE], m.ident[0:R, 0:R])
                nc.tensor.transpose(m.ps[7][0:1, PAGES * R:(PAGES + 1) * R], masked[:, PAST:PAST + 1],
                                    m.ident[0:R, 0:R]).then_inc(m.pe_c.sem, 1)
                pe.wait_ge(m.dve_d.sem, m.dve_d.at(b + 1))
                pe.wait_ge(m.dma_b.sem, m.dma_b.at(b * (16 * (PAGES + 1)) + 16 * (PAGES + 1)))
                for g in range(KVH):
                    rows = slice(32 * g, 32 * g + AG)
                    out = m.ps[7][:, 384 + AG * g:384 + AG * (g + 1)]
                    for j in range(PAGES):
                        nc.tensor.matmul(out, v_page[:, j, g * DH:(g + 1) * DH], probs_t[:, j, rows], start=(j == 0), stop=False)
                    last = nc.tensor.matmul(out, v_new[:, g * DH:(g + 1) * DH], new_t[:, rows], start=False, stop=True)
                last.then_inc(m.pe_d.sem, 1)

            for b in range(B):
                sample(b, b == 0)

        @block.scalar
        def _(act):
            def sample(b, first):
                act.wait_ge(m.pe_a.sem, m.pe_a.at(b + 1))
                if not first:
                    act.wait_ge(m.pe_b.sem, m.pe_b.at(b))
                for g in range(KVH):
                    last = nc.scalar.copy(keys[:, g, 0:PAST], m.ps_pair[g][:])
                last.then_inc(m.act_a.sem, 1)
                act.wait_ge(m.dve_c.sem, m.dve_c.at(b + 1))
                nc.scalar.activation(masked, masked, ACT.Exp, bias=st[0:R, 1:2], scale=scale,
                                     accum_out=st[0:R, 2:3]).then_inc(m.act_b.sem, 1)
                act.wait_ge(m.pe_d.sem, m.pe_d.at(b + 1))
                nc.scalar.copy(m.normed[:, :, bass.ds(b + T, 1)].rearrange("p h a -> p (h a)"), m.ps[7][:, 384:384 + AH]
                               ).then_inc(m.act_c.sem, 1)

            sample(0, True)
            with act.Fori(1, B) as b:
                sample(b, False)

        @block.vector
        def _(dve):
            V = nc.vector

            def sample(b, first):
                if not first:
                    dve.wait_ge(m.pe_b.sem, m.pe_b.at(b))
                V.tensor_copy(keys[:, :, PAST:PAST + 1], m.proj[:, KT1:KT1 + KVH, bass.ds(b + T, 1)])
                V.tensor_copy(q, s.q_s[:, bass.ds(b, 1), :].rearrange("p a h -> p (a h)"))
                V.tensor_copy(sel, s.sel[:, bass.ds(b, 1), :].rearrange("p a h -> p (a h)")).then_inc(m.dve_a.sem, 1)
                dve.wait_ge(m.pe_b.sem, m.pe_b.at(b + 1))
                if not first:
                    dve.wait_ge(m.pe_c.sem, m.pe_c.at(b))
                for n, (c0, e) in enumerate(pieces):
                    V.tensor_copy(masked[:, c0:e], m.ps[4 + n][0:R, 0:e - c0])
                V.drain()
                V.reduce_max(st[0:R, 0:1], masked, AX_X)
                V.drain()
                V.tensor_scalar(st[0:R, 1:2], st[0:R, 0:1], -scale, None, ALU.mult).then_inc(m.dve_c.sem, 1)
                dve.wait_ge(m.act_b.sem, m.act_b.at(b + 1))
                V.reciprocal(st[0:R, 3:4], st[0:R, 2:3])
                V.drain()
                V.tensor_scalar(masked, masked, st[0:R, 3:4], None, ALU.mult).then_inc(m.dve_b.sem, 1)
                dve.wait_ge(m.pe_c.sem, m.pe_c.at(b + 1))
                if not first:
                    dve.wait_ge(m.pe_d.sem, m.pe_d.at(b))
                V.tensor_copy(new_t, m.ps[7][0:1, PAGES * R:(PAGES + 1) * R])
                V.tensor_copy(probs_t.rearrange("p j r -> p (j r)"), m.ps[7][:, 0:PAGES * R]).then_inc(m.dve_d.sem, 1)

            sample(0, True)
            with dve.Fori(1, B) as b:
                sample(b, False)

    m.dma_a.passed(16 * PAGES * B)
    m.dma_b.passed(16 * (PAGES + 1) * B)
    for x in (m.pe_a, m.pe_b, m.pe_c, m.pe_d, m.act_a, m.act_b, m.act_c, m.dve_a, m.dve_b, m.dve_c, m.dve_d):
        x.passed(B)


PHASES = [phase_load_x, phase_in0, phase_s5_params, phase_s5_states, phase_s5_outputs, phase_s5_glu,
          phase_ml_gates, phase_ml_chunks, phase_ml_samples,
          lambda m: phase_out(m, "w_out0"), lambda m: phase_mlp(m, 0),
          phase_in1, phase_rows, phase_index, phase_index_samples, phase_topk, phase_attend, phase_attend_samples,
          lambda m: phase_out(m, "w_out1"), lambda m: phase_mlp(m, 1), phase_final]


def program(nc, ins, outs):
    from contextlib import ExitStack
    with ExitStack() as ctx:
        m = Machine(ctx, nc, ins, outs)
        m.spill = nc.dram_tensor("resid_spill", [P, KT, N], F32).ap()
        m.s5_dram = nc.dram_tensor("s5_by_channel", [S5_W, N], F32).ap()
        m.gates = m.sb("gates", [36, 1, N])
        m.s5_small = m.sb("s5_small", [P, 1, 2720])
        m.score_dram = nc.dram_tensor("sample_scores", [B, PAST + 1], F32).ap()
        m.relu = [m.proj[:, 18 + i] for i in range(2)]
        for phase in PHASES:
            phase(m)


_INS = ["x_prompt", "x_sample", "state_s5_re", "state_s5_im", "state_mlstm_c", "state_mlstm_n", "state_mlstm_m",
        "cache_k", "cache_v", "cache_kidx", "page_table", "norm_mix", "norm_mlp", "norm_final", "w_in0",
        "s5_lam_re", "s5_lam_im", "s5_log_dt", "s5_b_re", "s5_b_im", "s5_c_re", "s5_c_im", "s5_d", "w_glu",
        "b_glu", "b_igate", "b_fgate", "w_out0", "w_in1", "w_out1", "w_up", "w_down"]
_OUTS = [("y_prompt", (1, 1024, 1024)), ("y_sample", (8, 1, 1024)),
         ("p_s5_re", (1, 32, 64)), ("p_s5_im", (1, 32, 64)), ("p_c", (1, 4, 128, 128)), ("p_n", (1, 4, 128)),
         ("p_m", (1, 4)), ("p_k", (1, 1024, 2, 128)), ("p_v", (1, 1024, 2, 128)), ("p_kidx", (1, 1024, 64)),
         ("s_s5_re", (8, 32, 64)), ("s_s5_im", (8, 32, 64)), ("s_c", (8, 4, 128, 128)), ("s_n", (8, 4, 128)),
         ("s_m", (8, 4)), ("s_k", (8, 1, 2, 128)), ("s_v", (8, 1, 2, 128)), ("s_kidx", (8, 1, 64))]


def kernel(**inputs):
    import numpy as _np
    import concourse.bacc as _bacc
    from concourse import mybir as _mybir
    from concourse.bass_utils import run_bass_kernel_spmd as _run

    nc = _bacc.Bacc("TRN2", target_bir_lowering=False, num_devices=1)
    arrays, ins, outs = {}, {}, {}
    for name in _INS:
        a = _np.ascontiguousarray(inputs[name])
        arrays[f"in_{name}"] = a
        ins[name] = nc.dram_tensor(f"in_{name}", a.shape, _mybir.dt.from_np(a.dtype), kind="ExternalInput").ap()
    for name, shape in _OUTS:
        outs[name] = nc.dram_tensor(f"out_{name}", shape, _mybir.dt.float32, kind="ExternalOutput").ap()
    program(nc, ins, outs)
    r = _run(nc, [arrays], core_ids=[0])
    return tuple(r.results[0][f"out_{name}"] for name, _ in _OUTS)
```

```python
import math
from contextlib import ExitStack

import concourse.bass as bass
import concourse.mybir as mybir

F32 = mybir.dt.float32
F32R = mybir.dt.float32r
I32 = mybir.dt.int32
ALU = mybir.AluOpType
ACT = mybir.ActivationFunctionType
AX_X = mybir.AxisListType.X

P = 128
D = 1024
KT = D // P
T = 1024
B = 8
N = T + B
CHUNKS = 3
CH = N // CHUNKS
TB = T // P
FF_GROUPS = 4
EPS = 1e-6

S5_W = 512
G = 32
GC = 16
GS = 64
SC = 8
NC = T // SC
RUN = 8
UW = NC + 2 * B
HW = NC + B

MH = 4
DH = 128
MC = 128
NMC = T // MC

AH = 8
KVH = 2
AG = AH // KVH
IH = 8
IDIM = 64
TOPK = 256
PAGE = 128
PAGES = 8
PAST = PAGE * PAGES
NEG = -1e30


class Signal:

    def __init__(self, ctx, nc, name):
        self.sem = ctx.enter_context(nc.semaphore(name))
        self.base = 0

    def at(self, n):
        return n + self.base

    def passed(self, n):
        self.base += n


class Tiles:
    pass


class Machine:

    def __init__(self, ctx, nc, ins, outs):
        self.nc, self.ctx = nc, ctx
        self.ins, self.outs = ins, outs

        def sb(name, shape, dt=F32):
            return ctx.enter_context(nc.sbuf_tensor(name, shape, dt))

        self.left, self.mixed, self.right = ExitStack(), ExitStack(), ExitStack()
        self.layer = 0
        self.resid = sb("resid", [P, KT, N])
        self.inv_rms = sb("inv_rms", [P, N])
        self.mark = sb("mark", [P, 4])
        self.ident = sb("ident", [P, P])
        self.ones = sb("ones", [P, P])
        self.vec_rows = sb("vec_rows", [48, P])
        self.vecs = sb("vecs", [P, 48])
        self.g_mix = [self.vecs[:, 0:8], self.vecs[:, 8:16]]
        self.g_mlp = [self.vecs[:, 16:24], self.vecs[:, 24:32]]
        self.s5_d, self.b_glu, self.g_final = self.vecs[:, 32:36], self.vecs[:, 36:40], self.vecs[:, 40:48]
        self.eps = sb("eps", [P, 1])
        self.ps_pair = [ctx.enter_context(nc.psum_tensor(f"ps{b}", [P, 1024], F32)) for b in range(4)]
        self.ps = [self.ps_pair[b // 2][:, (b % 2) * 512:(b % 2) * 512 + 512] for b in range(8)]

        def signal(name):
            return Signal(ctx, nc, name)

        self.w_loaded0 = signal("w_loaded0")
        self.w_loaded1 = signal("w_loaded1")
        self.unit_done = signal("unit_done")
        self.set_free = signal("set_free")
        self.consts_set = signal("consts_set")
        self.norm_g = signal("norm_g")
        self.w_split = signal("w_split")
        self.lo_ready = signal("lo_ready")
        self.sq_used = signal("sq_used")
        self.mean_part = signal("mean_part")
        self.sq_done = signal("sq_done")
        self.ssq_done = signal("ssq_done")
        self.mean_set = signal("mean_set")
        self.inv_done = signal("inv_done")
        self.tiles_ready = signal("tiles_ready")
        self.stored = signal("stored")
        self.x_stored = signal("x_stored")
        self.x_back = signal("x_back")
        self.evac_a = signal("evac_a")
        self.evac_b = signal("evac_b")
        self.pe_a = signal("pe_a")
        self.pe_b = signal("pe_b")
        self.pe_c = signal("pe_c")
        self.pe_d = signal("pe_d")
        self.act_a = signal("act_a")
        self.act_b = signal("act_b")
        self.act_c = signal("act_c")
        self.act_d = signal("act_d")
        self.dve_a = signal("dve_a")
        self.dve_b = signal("dve_b")
        self.dve_c = signal("dve_c")
        self.dve_d = signal("dve_d")
        self.dve_e = signal("dve_e")
        self.pool_a = signal("pool_a")
        self.pool_b = signal("pool_b")
        self.dma_a = signal("dma_a")
        self.dma_b = signal("dma_b")
        self.dma_c = signal("dma_c")
        self.dma_d = signal("dma_d")
        self.dma_e = signal("dma_e")
        self.dma_f = signal("dma_f")
        self.dma_g = signal("dma_g")
        self.dma_h = signal("dma_h")

    def tile(self, stack, name, shape, side="left"):
        return stack.enter_context(self.nc.sbuf_tensor(f"{name}{self.layer}", shape, F32, side=side))


def place_wide(m, name="proj"):
    m.proj = m.tile(m.right, name, [P, 20, N], side="right")


def place_in(m, layer):
    m.left.close()
    m.right.close()
    m.layer = layer
    place_wide(m)
    if layer == 0:
        m.gates = m.tile(m.right, "gates", [36, 1, N], side="right")
    m.x_hi = m.tile(m.left, "in_x_hi", [P, KT, N])
    m.x_lo = m.tile(m.left, "in_x_lo", [P, KT, N])
    m.w_hi = m.tile(m.left, "in_w_hi", [P, 2, KT, P])
    m.w_lo = m.tile(m.left, "in_w_lo", [P, 2, KT, P])
    row = lambda t, n: t[:, 0:n].rearrange("p (k n) -> p k n", k=KT)
    m.raw_first = [row(m.proj[:, 17], D), row(m.proj[:, 19], D)]
    m.raw = [row(m.resid[:, slot], D) for slot in range(2)]
    m.last_width = 36 if layer == 0 else IDIM + IH
    m.last_raw = row(m.proj[:, 18], KT * m.last_width)
    m.last_hi = m.tile(m.left, "in_last_hi", [P, KT, m.last_width])
    m.last_lo = m.tile(m.left, "in_last_lo", [P, KT, m.last_width])
    m.sq = [m.proj[:, 8 + i] for i in range(2)]


def place_mixer(m):
    m.left.close()
    m.normed = m.tile(m.mixed, "normed", [P, KT, N])
    m.hidden = m.tile(m.left, "hidden", [P, KT, N])
    m.wts = m.tile(m.left, "wts", [P, 2, KT, P])
    m.s5_small = m.tile(m.left, "s5_small", [P, 1, 2720])


def place_out(m):
    m.left.close()
    m.right.close()
    m.x_hi = m.tile(m.left, "out_x_hi", [P, KT, N])
    m.x_lo = m.tile(m.left, "out_x_lo", [P, KT, N])
    m.w_hi = m.tile(m.left, "out_w_hi", [P, 2, KT, P])
    m.w_lo = m.tile(m.left, "out_w_lo", [P, 2, KT, P])
    wts = m.tile(m.left, "out_wts", [P, 2, KT, P])
    m.raw = m.raw_first = [wts[:, slot] for slot in range(2)]


def place_mlp(m):
    m.left.close()
    m.mixed.close()
    m.x_hi = m.tile(m.left, "mlp_x_hi", [P, KT, N])
    m.x_lo = m.tile(m.left, "mlp_x_lo", [P, KT, N])
    m.h_hi = m.tile(m.left, "mlp_h_hi", [P, KT, N])
    m.h_lo = m.tile(m.left, "mlp_h_lo", [P, KT, N])
    m.w_hi = m.tile(m.left, "mlp_w_hi", [P, 2, KT, P])
    m.w_lo = m.tile(m.left, "mlp_w_lo", [P, 2, KT, P])
    wts = m.tile(m.left, "mlp_wts", [P, 2, KT, P])
    m.raw = m.raw_first = [wts[:, slot] for slot in range(2)]
    m.relu = m.sq = [m.tile(m.left, f"relu_{slot}_", [P, N])[:] for slot in range(2)]


def token_cols(n):
    return slice(n * CH, (n + 1) * CH)


def phase_load_x(m):
    nc = m.nc
    place_wide(m, "x_rows")
    x_tok = m.proj[:, 0:KT, 0:T]
    x_smp = m.proj[0:B, 8, 0:D]
    with nc.Block() as block:

        @block.sync
        def _(sp):
            src = m.ins["x_prompt"].rearrange("b (t p) f -> p (b t) f", p=P)
            sp.dma_start(x_tok[:, 0:4, :], src[:, 0:4, :]).then_inc(m.dma_a.sem, 16)
            sp.dma_start(x_tok[:, 4:8, :], src[:, 4:8, :]).then_inc(m.dma_b.sem, 16)
            sp.dma_start(x_smp, m.ins["x_sample"].rearrange("b o f -> (b o) f")).then_inc(m.dma_c.sem, 16)

        @block.gpsimd
        def _(pool):
            nc.gpsimd.memset(m.ident[:], 0.0)
            nc.gpsimd.memset(m.ones[:], 1.0)
            nc.gpsimd.memset(m.eps[:], EPS)
            pool.drain()
            nc.gpsimd.affine_select(out=m.ident[:], in_=m.ident[:], compare_op=ALU.not_equal, fill=1.0,
                                    base=0, pattern=[[-1, P]], channel_multiplier=1).then_inc(m.consts_set.sem, 1)

        @block.tensor
        def _(pe):
            pe.wait_ge(m.consts_set.sem, m.consts_set.at(1))
            pe.wait_ge(m.dma_a.sem, m.dma_a.at(16))
            pe.wait_ge(m.dma_b.sem, m.dma_b.at(16))
            pe.wait_ge(m.dma_c.sem, m.dma_c.at(16))
            for k in range(KT):
                if k >= 2:
                    pe.wait_ge(m.evac_a.sem, m.evac_a.at(k - 1))
                    pe.wait_ge(m.evac_b.sem, m.evac_b.at(k - 1))
                banks = m.ps[3 * (k % 2):3 * (k % 2) + 3]
                for t in range(TB):
                    nc.tensor.transpose(banks[t // 4][:, (t % 4) * P:(t % 4 + 1) * P],
                                        x_tok[:, t, k * P:(k + 1) * P], m.ident[:])
                nc.tensor.transpose(banks[2][:, 0:B], x_smp[:, k * P:(k + 1) * P],
                                    m.ident[0:B, 0:B]).then_inc(m.pe_a.sem, 1)
            pe.wait_ge(m.norm_g.sem, m.norm_g.at(80))
            nc.tensor.transpose(m.ps[6][:, 0:48], m.vec_rows[:], m.ident[0:48, 0:48]).then_inc(m.pe_b.sem, 1)

        @block.scalar
        def _(act):
            for name, r, n in (("norm_mix", 0, 16), ("norm_mlp", 16, 16), ("s5_d", 32, 4), ("b_glu", 36, 4),
                               ("norm_final", 40, 8)):
                src = m.ins[name]
                src = src.rearrange("l (k p) -> (l k) p", p=P) if len(src.shape) == 2 else src.rearrange("(k p) -> k p", p=P)
                act.dma_start(m.vec_rows[r:r + n, :], src).then_inc(m.norm_g.sem, 16)
            for k in range(KT):
                act.wait_ge(m.pe_a.sem, m.pe_a.at(k + 1))
                b = m.ps[3 * (k % 2):3 * (k % 2) + 3]
                nc.scalar.copy(m.resid[:, k, 512:T], b[1][:])
                nc.scalar.copy(m.resid[:, k, T:N], b[2][:, 0:B]).then_inc(m.evac_a.sem, 1)

        @block.vector
        def _(dve):
            nc.vector.memset(m.inv_rms[:, 0:1], 0.0).then_inc(m.set_free.sem, 2)
            nc.vector.memset(m.inv_rms[:, 1:2], 0.0).then_inc(m.unit_done.sem, 2)
            nc.vector.memset(m.inv_rms[:, 2:3], 0.0).then_inc(m.w_split.sem, 2)
            for k in range(KT):
                dve.wait_ge(m.pe_a.sem, m.pe_a.at(k + 1))
                nc.vector.tensor_copy(m.resid[:, k, 0:512], m.ps[3 * (k % 2)][:]).then_inc(m.evac_b.sem, 1)
            dve.wait_ge(m.pe_b.sem, m.pe_b.at(1))
            nc.vector.tensor_copy(m.vecs[:], m.ps[6][:, 0:48])

    m.consts_set.passed(1)
    m.unit_done.passed(2)
    m.w_split.passed(2)
    for s in (m.dma_a, m.dma_b, m.dma_c):
        s.passed(16)
    m.norm_g.passed(80)
    m.pe_b.passed(1)
    m.pe_a.passed(KT)
    m.evac_a.passed(KT)
    m.evac_b.passed(KT)


def load_unit(sp, m, slot, j, src, raw=None):
    w_loaded = m.w_loaded1 if slot else m.w_loaded0
    sp.wait_ge(m.w_split.sem, m.w_split.at(2 * j + slot - 1))
    sp.dma_start((raw or m.raw)[slot], src).then_inc(w_loaded.sem, 16)


def flat(ap):
    return ap.rearrange("p a n -> p (a n)")


def parts(ap):
    return ap.bitcast(F32R)


def split_unit(pool, m, slot, j, raw=None):
    w_loaded = m.w_loaded1 if slot else m.w_loaded0
    pool.wait_ge(w_loaded.sem, w_loaded.at(16 * j + 16))
    pool.wait_ge(m.unit_done.sem, m.unit_done.at(2 * j + slot - 1))
    split(pool, m, (raw or m.raw)[slot], m.w_hi[:, slot], m.w_lo[:, slot]).then_inc(m.w_split.sem, 1)


def split(pool, m, x, hi, lo):
    one = m.ones[:, 0:x.shape[2]].unsqueeze(1).to_broadcast(list(x.shape))
    m.nc.gpsimd.tensor_tensor(parts(hi), x, one, ALU.mult)
    pool.drain()
    return m.nc.gpsimd.tensor_tensor(parts(lo), x, hi, ALU.subtract)


def product_parts(nc, out, w_hi, w_lo, x_hi, x_lo, first, last):
    for n, (w, x) in enumerate(((w_hi, x_hi), (w_hi, x_lo), (w_lo, x_hi))):
        for c in range(CHUNKS):
            ins = nc.tensor.matmul(out[c], parts(w), parts(x[:, token_cols(c)]), start=first and n == 0,
                                   stop=last and n == 2)
    return ins


def unit_matmuls(pe, m, slot, j, x_hi, x_lo, ready=None):
    banks = [m.ps[3 * slot + c][:, 0:CH] for c in range(CHUNKS)]
    pe.wait_ge(m.w_split.sem, m.w_split.at(2 * j + slot + 1))
    pe.wait_ge(m.set_free.sem, m.set_free.at(2 * j + slot + 1))
    for k in range(KT):
        if ready:
            ready(k)
        last = product_parts(m.nc, banks, m.w_hi[:, slot, k, :], m.w_lo[:, slot, k, :], x_hi[:, k], x_lo[:, k],
                             k == 0, k == KT - 1)
    last.then_inc(m.unit_done.sem, 1)


def units_passed(m, n):
    m.w_loaded0.passed(16 * (n // 2))
    m.w_loaded1.passed(16 * (n // 2))
    for s in (m.unit_done, m.set_free, m.w_split):
        s.passed(n)


def norm_act(act, m, gain):
    nc = m.nc
    for k in range(KT):
        nc.scalar.mul(parts(m.x_hi[:, k, :]), m.resid[:, k, :], gain[:, k:k + 1]).then_inc(m.tiles_ready.sem, 1)
    for k in range(KT):
        if k >= 3:
            act.wait_ge(m.sq_used.sem, m.sq_used.at(k - 2))
        nc.scalar.activation(m.sq[k % 2] if k else m.inv_rms[:], m.resid[:, k, :], ACT.Square).then_inc(m.sq_done.sem, 1)


def norm_dve(dve, m, gain):
    nc = m.nc
    for k in range(KT):
        dve.wait_ge(m.tiles_ready.sem, m.tiles_ready.at(k + 1))
        nc.vector.scalar_tensor_tensor(parts(m.x_lo[:, k, :]), m.resid[:, k, :], gain[:, k:k + 1], m.x_hi[:, k, :],
                                       ALU.mult, ALU.subtract).then_inc(m.lo_ready.sem, 1)
    for k in range(1, KT):
        dve.drain()
        dve.wait_ge(m.sq_done.sem, m.sq_done.at(k + 1))
        nc.vector.tensor_tensor(m.inv_rms[:], m.inv_rms[:], m.sq[k % 2], ALU.add).then_inc(m.sq_used.sem, 1)
    for c in range(CHUNKS):
        dve.wait_ge(m.ssq_done.sem, m.ssq_done.at(c + 1))
        ins = nc.vector.tensor_scalar(m.inv_rms[:, token_cols(c)], m.ps[6 + c % 2][:, 0:CH], 1.0 / D, EPS, ALU.mult, ALU.add)
        if c == 0:
            ins.then_inc(m.mean_part.sem, 1)
    dve.drain()
    nc.vector.reciprocal(m.inv_rms[:], m.inv_rms[:]).then_inc(m.mean_set.sem, 1)


def norm_ready(pe, m):
    def ready(k):
        pe.wait_ge(m.tiles_ready.sem, m.tiles_ready.at(k + 1))
        pe.wait_ge(m.lo_ready.sem, m.lo_ready.at(k + 1))
    return ready


def norm_first_units(pe, m):
    nc = m.nc
    unit_matmuls(pe, m, 0, 0, m.x_hi, m.x_lo, ready=norm_ready(pe, m))
    unit_matmuls(pe, m, 1, 0, m.x_hi, m.x_lo)
    pe.wait_ge(m.sq_used.sem, m.sq_used.at(KT - 1))
    for c in range(CHUNKS):
        if c == 2:
            pe.wait_ge(m.mean_part.sem, m.mean_part.at(1))
        nc.tensor.matmul(m.ps[6 + c % 2][:, 0:CH], m.ones[:], m.inv_rms[:, token_cols(c)], start=True, stop=True
                         ).then_inc(m.ssq_done.sem, 1)


def norm_root(act, m):
    nc = m.nc
    act.wait_ge(m.mean_set.sem, m.mean_set.at(1))
    nc.scalar.activation(m.inv_rms[:], m.inv_rms[:], ACT.Sqrt).then_inc(m.inv_done.sem, 1)


def norm_passed(m):
    for s in (m.sq_done, m.tiles_ready, m.lo_ready):
        s.passed(KT)
    m.ssq_done.passed(CHUNKS)
    m.sq_used.passed(KT - 1)
    for s in (m.mean_part, m.mean_set, m.inv_done):
        s.passed(1)


def phase_in0(m):
    nc = m.nc
    w_in = m.ins["w_in0"].rearrange("(k p) n -> p k n", p=P)
    place_in(m, 0)
    wg = m.last_raw
    units = 20

    with nc.Block() as block:

        @block.gpsimd
        def _(pool):
            nc.gpsimd.memset(wg, 0.0).then_inc(m.pool_a.sem, 1)
            for slot in range(2):
                split_unit(pool, m, slot, 0, m.raw_first)
            pool.wait_ge(m.dma_a.sem, m.dma_a.at(32))
            split(pool, m, wg, m.last_hi[:], m.last_lo[:]).then_inc(m.pool_a.sem, 1)
            with pool.Fori(1, units // 2) as j:
                for slot in range(2):
                    split_unit(pool, m, slot, j)

        @block.sync
        def _(sp):
            for slot in range(2):
                load_unit(sp, m, slot, 0, w_in[:, :, slot * P:slot * P + P], m.raw_first)
            sp.wait_ge(m.w_loaded0.sem, m.w_loaded0.at(16))
            sp.dma_start(m.spill, m.resid[:]).then_inc(m.x_stored.sem, 16)
            sp.wait_ge(m.x_stored.sem, m.x_stored.at(16))
            sp.wait_ge(m.sq_done.sem, m.sq_done.at(KT))
            sp.wait_ge(m.lo_ready.sem, m.lo_ready.at(KT))
            with sp.Fori(1, units // 2) as j:
                for slot in range(2):
                    load_unit(sp, m, slot, j, w_in[:, :, bass.ds((j * 2 + slot) * P, P)])
            sp.wait_ge(m.x_stored.sem, m.x_stored.at(16))

        @block.tensor
        def _(pe):
            norm_first_units(pe, m)
            with pe.Fori(1, units // 2) as j:
                for slot in range(2):
                    unit_matmuls(pe, m, slot, j, m.x_hi, m.x_lo)
            pe.wait_ge(m.pool_a.sem, m.pool_a.at(2))
            pe.wait_ge(m.set_free.sem, m.set_free.at(units + 1))
            for k in range(KT):
                last = product_parts(nc, [m.ps[c][0:36, 0:CH] for c in range(CHUNKS)], m.last_hi[:, k], m.last_lo[:, k],
                                     m.x_hi[:, k], m.x_lo[:, k], k == 0, k == KT - 1)
            last.then_inc(m.pe_a.sem, 1)

        @block.scalar
        def _(act):
            norm_act(act, m, m.g_mix[0])
            act.wait_ge(m.pool_a.sem, m.pool_a.at(1))
            with nc.allow_non_contiguous_dma("16 bytes a row"):
                act.dma_start(wg[:, :, 0:4], w_in[:, :, 2560:2564]).then_inc(m.dma_a.sem, 16)
                act.dma_start(wg[:, :, 32:36], w_in[:, :, 2564:2568]).then_inc(m.dma_a.sem, 16)
            norm_root(act, m)

        @block.vector
        def _(dve):
            norm_dve(dve, m, m.g_mix[0])
            dve.wait_ge(m.inv_done.sem, m.inv_done.at(1))

            def scaled(u, slot, order):
                dve.wait_ge(m.unit_done.sem, m.unit_done.at(u + 1))
                for c in range(CHUNKS):
                    src = m.ps[3 * slot + c][:, 0:CH]
                    r = m.inv_rms[:, token_cols(c)]
                    dst = m.proj[:, bass.ds(u, 1), token_cols(c)].rearrange("p a n -> p (a n)")
                    if order == "chunked":
                        w = CH // SC if c < 2 else NC - 2 * (CH // SC)
                        c0 = c * (CH // SC)
                        tile = m.proj[:, bass.ds(u, 1), 0:T].rearrange("p a (s c) -> p (a c) s", s=SC)
                        if c == 2:
                            nc.vector.tensor_tensor(m.proj[:, bass.ds(u, 1), T:N].rearrange("p a n -> p (a n)"),
                                                    src[:, SC * w:CH], r[:, SC * w:CH], ALU.mult)
                        dst, src, r = (tile[:, c0:c0 + w, :], src[:, 0:SC * w].rearrange("p (c s) -> p c s", s=SC),
                                       r[:, 0:SC * w].rearrange("p (c s) -> p c s", s=SC))
                    last = nc.vector.tensor_tensor(dst, src, r, ALU.mult)
                last.then_inc(m.set_free.sem, 1)

            with dve.Fori(0, 2) as j:
                for slot in range(2):
                    scaled(j * 2 + slot, slot, "chunked")
            with dve.Fori(2, units // 2) as j:
                for slot in range(2):
                    scaled(j * 2 + slot, slot, "plain")
            dve.wait_ge(m.pe_a.sem, m.pe_a.at(1))
            for c in range(CHUNKS):
                nc.vector.tensor_tensor(m.gates[0:4, 0, token_cols(c)], m.ps[c][0:4, 0:CH],
                                        m.inv_rms[0:4, token_cols(c)], ALU.mult)
                nc.vector.tensor_tensor(m.gates[32:36, 0, token_cols(c)], m.ps[c][32:36, 0:CH],
                                        m.inv_rms[32:36, token_cols(c)], ALU.mult)

    m.pool_a.passed(2)
    m.pe_a.passed(1)
    m.dma_a.passed(32)
    m.x_stored.passed(16)
    norm_passed(m)
    units_passed(m, units)


class Carver:

    def __init__(self, tile):
        self.flat = tile.rearrange("p a n -> p (a n)")
        self.at = 0

    def take(self, *shape, parts=P):
        n = math.prod(shape)
        ap = self.flat[0:parts, self.at:self.at + n]
        self.at += n
        assert self.at <= self.flat.shape[1], self.at
        names = "abcd"[:len(shape)]
        spec = " ".join(names)
        return ap if len(shape) == 1 else ap.rearrange(f"p ({spec}) -> p {spec}", **dict(zip(names[1:], shape[1:])))


def s5_tiles(m):
    s = m.s5 = Tiles()
    a = Carver(m.resid[:])
    s.starts = a.take(G, HW)
    s.lam_rows = a.take(2, P, parts=G)
    s.dt = a.take(G)
    s.lam = a.take(2, G)
    s.tmp = a.take(6, G)
    s.tmp2 = a.take(6, G)
    s.bar = a.take(2, G)
    s.coef = a.take(2, G)
    s.pow_re = a.take(SC + 1, G)
    s.pow_im = a.take(SC + 1, G)
    s.b_in = a.take(2, G, GC)
    s.x1 = a.take(SC, G)
    s.x2 = a.take(SC, G)
    s.y2 = a.take(SC + 1, G)
    c = Carver(m.hidden[:])
    s.u = c.take(G, UW)
    s.e = [c.take(2 * SC * GC) for _ in range(2)]
    s.et = [c.take(P) for _ in range(2)]
    s.mt = [c.take(P) for _ in range(2)]
    s.ct = [c.take(SC + 1, GC) for _ in range(2)]
    s.t1 = c.take((SC + 1) * GC)
    s.t2 = c.take((SC + 1) * GC)
    s.t3 = c.take((SC + 1) * GC)
    s.t4 = c.take((SC + 1) * GC)
    s.powers = c.take(RUN, 4, G, parts=GS)
    more = Carver(m.wts[:, 1])
    s.e += [more.take(2 * SC * GC) for _ in range(2)]
    s.ct += [more.take(SC + 1, GC) for _ in range(2)]
    b = Carver(m.normed[:])
    s.bt = Carver(m.normed[:]).take(4, G, GC)
    s.h = b.take(2, G, NC, parts=GS)
    x = Carver(m.s5_small[:])
    s.c_t = x.take(2, G, GC)
    s.y1 = x.take(SC + 1, G)
    s.s0 = x.take(2, B, G, parts=GS)
    s.sv = x.take(2, B, G, parts=GS)
    s.l1 = x.take(4, G, parts=GS)
    s.st = x.take(4, G, parts=GS)
    return s


def phase_s5_params(m):
    nc = m.nc
    place_mixer(m)
    s = s5_tiles(m)
    TWO_PI = 2 * math.pi
    C1 = 6.28125
    C2 = TWO_PI - C1
    rnd = 12582912.0
    s0_rows = [m.wts[:, 0, 0:2].rearrange("p a b -> p (a b)"), m.wts[:, 0, 2:4].rearrange("p a b -> p (a b)")]
    c_rows = m.wts[:, 1].rearrange("p (a t) b -> p a t b", a=2)
    with nc.Block() as block:

        @block.sync
        def _(sp):
            for half in range(2):
                h = slice(GS * half, GS * half + GS)
                sp.dma_start(s.lam_rows[:, 0, h], m.ins["s5_lam_re"]).then_inc(m.dma_a.sem, 16)
                sp.dma_start(s.lam_rows[:, 1, h], m.ins["s5_lam_im"]).then_inc(m.dma_a.sem, 16)
            sp.dma_start(s.dt, m.ins["s5_log_dt"].partition_broadcast(P)).then_inc(m.dma_a.sem, 16)
            sp.dma_start(m.s5_dram.rearrange("(k p) n -> p k n", p=P), m.proj[:, 0:4, :]).then_inc(m.dma_d.sem, 16)
            sp.wait_ge(m.dma_d.sem, m.dma_d.at(16))
            for step in range(SC):
                sp.dma_start(s.u[GC * step:GC * step + GC, :, 0:NC],
                             m.s5_dram.rearrange("(g c) n -> c g n", c=GC)[:, :, NC * step:NC * step + NC]
                             ).then_inc(m.dma_f.sem, 16)
            sp.wait_ge(m.pool_a.sem, m.pool_a.at(1))
            for rows, cols in ((slice(0, GC), slice(NC, NC + B)), (slice(P - GC, P), slice(NC + B, UW))):
                sp.dma_start(s.u[rows, :, cols], m.s5_dram.rearrange("(g c) n -> c g n", c=GC)[:, :, T:N]
                             ).then_inc(m.dma_f.sem, 16)
            sp.wait_ge(m.dma_f.sem, m.dma_f.at(10 * 16))

        @block.scalar
        def _(act):
            for part, name in enumerate(("re", "im")):
                for half in range(2):
                    act.dma_start(c_rows[:, part, :, GS * half:GS * half + GS],
                                  m.ins["s5_c_" + name].rearrange("(t g) c s -> (g c) t s", t=4)
                                  ).then_inc(m.dma_b.sem, 16)
            for part, name in enumerate(("re", "im")):
                act.dma_start(s0_rows[part][:, 0:2 * GS].rearrange("r (a s) -> r a s", a=2),
                              m.ins["state_s5_" + name].rearrange("(a b) g s -> (b g) a s", a=2)
                              ).then_inc(m.dma_c.sem, 16)
            act.wait_ge(m.dma_a.sem, m.dma_a.at(80))
            nc.scalar.activation(s.dt, s.dt, ACT.Exp).then_inc(m.act_a.sem, 1)
            act.wait_ge(m.dve_b.sem, m.dve_b.at(1))
            nc.scalar.activation(s.tmp[:, 0, :], s.tmp[:, 0, :], ACT.Exp).then_inc(m.act_b.sem, 1)
            act.wait_ge(m.dve_c.sem, m.dve_c.at(1))
            nc.scalar.activation(s.tmp[:, 2:4, :], s.tmp[:, 2:4, :], ACT.Sin).then_inc(m.act_c.sem, 1)

        @block.gpsimd
        def _(pool):
            nc.gpsimd.memset(s.u[:, :, NC:UW], 0.0).then_inc(m.pool_a.sem, 1)
            nc.gpsimd.memset(s.e[0][:, P:2 * P], 0.0)
            nc.gpsimd.memset(s.e[1][:, P:2 * P], 0.0)
            for half in range(2):
                h = slice(GS * half, GS * half + GS)
                for part, name in enumerate(("re", "im")):
                    pool.dma_start(s.b_in[h, part], m.ins["s5_b_" + name].rearrange("g s c -> s g c")
                                   ).then_inc(m.dma_e.sem, 16)
            pool.wait_ge(m.dma_e.sem, m.dma_e.at(64))

        @block.tensor
        def _(pe):
            pe.wait_ge(m.dma_a.sem, m.dma_a.at(80))
            for part in range(2):
                last = nc.tensor.transpose(m.ps[0][:, G * part:G * part + G], s.lam_rows[:, part, :],
                                           m.ident[0:G, 0:G])
            last.then_inc(m.pe_a.sem, 1)
            pe.wait_ge(m.dma_b.sem, m.dma_b.at(64))
            for part in range(2):
                for t in range(4):
                    last = nc.tensor.transpose(m.ps[1 + part][:, P * t:P * t + P], c_rows[:, part, t, :], m.ident[:])
            last.then_inc(m.pe_b.sem, 1)
            pe.wait_ge(m.dma_c.sem, m.dma_c.at(32))
            for part in range(2):
                for a in range(2):
                    last = nc.tensor.transpose(m.ps[3 + part][0:GS, P * a:P * a + P],
                                               s0_rows[part][:, GS * a:GS * a + GS], m.ident[:])
            last.then_inc(m.pe_c.sem, 1)

        @block.vector
        def _(dve):
            V = nc.vector
            dve.wait_ge(m.pe_a.sem, m.pe_a.at(1))
            V.tensor_copy(s.lam, m.ps[0][:, 0:2 * G].rearrange("p (a g) -> p a g", a=2))
            dve.drain()
            dve.wait_ge(m.act_a.sem, m.act_a.at(1))
            V.tensor_tensor(s.tmp[:, 0, :], s.lam[:, 0, :], s.dt, ALU.mult).then_inc(m.dve_b.sem, 1)
            V.tensor_tensor(s.tmp[:, 1, :], s.lam[:, 1, :], s.dt, ALU.mult)
            dve.drain()
            V.tensor_scalar(s.tmp[:, 4, :], s.tmp[:, 1, :], 1 / TWO_PI, rnd, ALU.mult, ALU.add)
            dve.drain()
            V.tensor_scalar(s.tmp[:, 4, :], s.tmp[:, 4, :], rnd, None, ALU.subtract)
            dve.drain()
            V.scalar_tensor_tensor(s.tmp[:, 1, :], s.tmp[:, 4, :], -C1, s.tmp[:, 1, :], ALU.mult, ALU.add)
            dve.drain()
            V.scalar_tensor_tensor(s.tmp[:, 2, :], s.tmp[:, 4, :], -C2, s.tmp[:, 1, :], ALU.mult, ALU.add)
            dve.drain()
            V.tensor_scalar(s.tmp[:, 5, :], s.tmp[:, 2, :], math.pi / 2, -TWO_PI, ALU.is_gt, ALU.mult)
            dve.drain()
            V.scalar_tensor_tensor(s.tmp[:, 3, :], s.tmp[:, 2, :], math.pi / 2, s.tmp[:, 5, :], ALU.add, ALU.add)
            dve.drain()
            V.tensor_scalar(s.tmp[:, 2:4, :], s.tmp[:, 2:4, :], 3.1415925, -3.1415925, ALU.min, ALU.max).then_inc(m.dve_c.sem, 1)
            dve.wait_ge(m.act_b.sem, m.act_b.at(1))
            dve.wait_ge(m.act_c.sem, m.act_c.at(1))
            V.tensor_tensor(s.bar[:, 0, :], s.tmp[:, 0, :], s.tmp[:, 3, :], ALU.mult)
            V.tensor_tensor(s.bar[:, 1, :], s.tmp[:, 0, :], s.tmp[:, 2, :], ALU.mult)
            dve.drain()
            lr, li, br, bi = s.lam[:, 0, :], s.lam[:, 1, :], s.bar[:, 0, :], s.bar[:, 1, :]
            t = s.tmp2
            V.tensor_scalar(t[:, 0, :], br, -1.0, None, ALU.add)
            V.tensor_tensor(t[:, 1, :], lr, lr, ALU.mult)
            V.tensor_tensor(t[:, 2, :], li, li, ALU.mult)
            dve.drain()
            V.tensor_tensor(t[:, 1, :], t[:, 1, :], t[:, 2, :], ALU.add)
            V.tensor_tensor(t[:, 3, :], t[:, 0, :], lr, ALU.mult)
            V.tensor_tensor(t[:, 4, :], bi, li, ALU.mult)
            dve.drain()
            V.reciprocal(t[:, 1, :], t[:, 1, :])
            V.tensor_tensor(t[:, 3, :], t[:, 3, :], t[:, 4, :], ALU.add)
            dve.drain()
            V.tensor_tensor(t[:, 4, :], bi, lr, ALU.mult)
            V.tensor_tensor(t[:, 5, :], t[:, 0, :], li, ALU.mult)
            dve.drain()
            V.tensor_tensor(t[:, 4, :], t[:, 4, :], t[:, 5, :], ALU.subtract)
            V.tensor_tensor(s.coef[:, 0, :], t[:, 3, :], t[:, 1, :], ALU.mult)
            dve.drain()
            V.tensor_tensor(s.coef[:, 1, :], t[:, 4, :], t[:, 1, :], ALU.mult)
            V.memset(s.pow_re[:, 0, :], 1.0)
            V.memset(s.pow_im[:, 0, :], 0.0)
            dve.drain()
            for j in range(SC):
                pr, pi = s.pow_re[:, j, :], s.pow_im[:, j, :]
                V.tensor_tensor(t[:, 0, :], pr, br, ALU.mult)
                V.tensor_tensor(t[:, 1, :], pi, bi, ALU.mult)
                V.tensor_tensor(t[:, 2, :], pr, bi, ALU.mult)
                V.tensor_tensor(t[:, 3, :], pi, br, ALU.mult)
                dve.drain()
                V.tensor_tensor(s.pow_re[:, j + 1, :], t[:, 0, :], t[:, 1, :], ALU.subtract)
                V.tensor_tensor(s.pow_im[:, j + 1, :], t[:, 2, :], t[:, 3, :], ALU.add)
                dve.drain()
            top, bot = slice(0, GS), slice(GS, P)
            for j in range(SC):
                V.tensor_copy(s.x1[top, j], s.pow_re[top, SC - 1 - j])
                V.tensor_copy(s.x1[bot, j], s.pow_im[bot, SC - 1 - j])
                V.tensor_scalar(s.x2[top, j], s.pow_im[top, SC - 1 - j], -1.0, None, ALU.mult)
                V.tensor_copy(s.x2[bot, j], s.pow_re[bot, SC - 1 - j])
            V.tensor_copy(s.y1[top], s.pow_re[top])
            V.tensor_scalar(s.y1[bot], s.pow_im[bot], -1.0, None, ALU.mult)
            V.tensor_scalar(s.y2[top], s.pow_im[top], -1.0, None, ALU.mult)
            V.tensor_scalar(s.y2[bot], s.pow_re[bot], -1.0, None, ALU.mult)
            for dst, j in ((s.powers[:, 0], SC), (s.l1, 1)):
                V.tensor_copy(dst[:, 0, :], s.pow_re[top, j, :])
                V.tensor_copy(dst[:, 1, :], s.pow_re[top, j, :])
                V.tensor_copy(dst[:, 2, :], s.pow_im[top, j, :])
                V.tensor_scalar(dst[:, 3, :], s.pow_im[top, j, :], -1.0, None, ALU.mult)
            dve.wait_ge(m.dma_e.sem, m.dma_e.at(64))
            cr = s.coef[:, 0, :].unsqueeze(2).to_broadcast([P, G, GC])
            ci = s.coef[:, 1, :].unsqueeze(2).to_broadcast([P, G, GC])
            w = [s.bt[:, i] for i in range(4)]
            V.tensor_tensor(w[0], s.b_in[:, 0], cr, ALU.mult)
            V.tensor_tensor(w[1], s.b_in[:, 1], ci, ALU.mult)
            V.tensor_tensor(w[2], s.b_in[:, 0], ci, ALU.mult)
            V.tensor_tensor(w[3], s.b_in[:, 1], cr, ALU.mult)
            dve.drain()
            V.tensor_tensor(s.b_in[:, 0], w[0], w[1], ALU.subtract)
            V.tensor_tensor(s.b_in[:, 1], w[2], w[3], ALU.add)
            dve.wait_ge(m.pe_b.sem, m.pe_b.at(1))
            for part in range(2):
                V.tensor_copy(s.c_t[:, part], m.ps[1 + part][:].rearrange("p (g c) -> p g c", g=G))
            dve.wait_ge(m.pe_c.sem, m.pe_c.at(1))
            for part in range(2):
                V.tensor_copy(s.s0[:, part].rearrange("p b g -> p (b g)"), m.ps[3 + part][0:GS, 0:B * G])

    m.dma_a.passed(80)
    m.dma_b.passed(64)
    m.dma_c.passed(32)
    m.dma_d.passed(16)
    m.dma_e.passed(64)
    m.dma_f.passed(10 * 16)
    for x in (m.act_a, m.act_b, m.act_c, m.dve_b, m.dve_c, m.pool_a, m.pe_a, m.pe_b, m.pe_c):
        x.passed(1)


def s5_b_powers(pool, m, s, g, slot):
    x1 = s.x1[:, :, bass.ds(g, 1)].to_broadcast([P, SC, GC])
    x2 = s.x2[:, :, bass.ds(g, 1)].to_broadcast([P, SC, GC])
    view = lambda t: t[:, 0:P].rearrange("p (s c) -> p s c", s=SC)
    nc = m.nc
    nc.gpsimd.tensor_tensor(view(s.t1), x1, s.b_in[:, 0, bass.ds(g, 1), :].to_broadcast([P, SC, GC]), ALU.mult)
    nc.gpsimd.tensor_tensor(view(s.t2), x2, s.b_in[:, 1, bass.ds(g, 1), :].to_broadcast([P, SC, GC]), ALU.mult)
    pool.drain()
    return nc.gpsimd.tensor_tensor(s.e[slot][:, 0:P], s.t1[:, 0:P], s.t2[:, 0:P], ALU.add)


def phase_s5_states(m):
    nc = m.nc
    s = m.s5
    with nc.Block() as block:

        @block.gpsimd
        def _(pool):
            def step(g, slot, first):
                pool.drain()
                if not first:
                    pool.wait_ge(m.pe_a.sem, m.pe_a.at(g - 1))
                s5_b_powers(pool, m, s, g, slot).then_inc(m.pool_a.sem, 1)

            for g in range(2):
                step(g, g, True)
            with pool.Fori(1, G // 2) as i:
                for slot in range(2):
                    step(i * 2 + slot, slot, False)

        @block.tensor
        def _(pe):
            def turn(g, slot, first):
                pe.wait_ge(m.pool_a.sem, m.pool_a.at(g + 1))
                if not first:
                    pe.wait_ge(m.act_a.sem, m.act_a.at(g - 1))
                nc.tensor.transpose(m.ps[slot][:, 0:P], s.e[slot][:, 0:P], m.ident[:]).then_inc(m.pe_a.sem, 1)

            def add(g, slot, first):
                pe.wait_ge(m.act_a.sem, m.act_a.at(g + 1))
                if not first:
                    pe.wait_ge(m.act_b.sem, m.act_b.at(g - 1))
                    pe.wait_ge(m.dve_b.sem, m.dve_b.at(g - 1))
                nc.tensor.matmul(m.ps[2 + slot][:, 0:UW], s.et[slot], s.u[:, bass.ds(g, 1), :].rearrange("p a n -> p (a n)"),
                                 start=True, stop=True).then_inc(m.pe_b.sem, 1)

            def pair(g0, first):
                for slot in range(2):
                    turn(g0 + slot, slot, first)
                for slot in range(2):
                    add(g0 + slot, slot, first)

            pair(0, True)
            with pe.Fori(1, G // 2) as i:
                pair(i * 2, False)

        @block.scalar
        def _(act):
            def pair(g0, first):
                for slot in range(2):
                    g = g0 + slot
                    act.wait_ge(m.pe_a.sem, m.pe_a.at(g + 1))
                    if not first:
                        act.wait_ge(m.pe_b.sem, m.pe_b.at(g - 1))
                    nc.scalar.copy(s.et[slot], m.ps[slot][:, 0:P]).then_inc(m.act_a.sem, 1)
                for slot in range(2):
                    g = g0 + slot
                    act.wait_ge(m.pe_b.sem, m.pe_b.at(g + 1))
                    nc.scalar.copy(s.h[:, 0, bass.ds(g, 1), :].rearrange("p a n -> p (a n)"), m.ps[2 + slot][0:GS, 0:NC])
                    nc.scalar.copy(s.sv[:, 0, :, bass.ds(g, 1)].rearrange("p b a -> p (b a)"),
                                   m.ps[2 + slot][0:GS, NC + B:UW]).then_inc(m.act_b.sem, 1)

            pair(0, True)
            with act.Fori(1, G // 2) as i:
                pair(i * 2, False)

        @block.vector
        def _(dve):
            def move(g, slot):
                dve.wait_ge(m.pe_b.sem, m.pe_b.at(g + 1))
                dve.wait_ge(m.act_b.sem, m.act_b.at(g + 1))
                nc.vector.tensor_copy(s.h[:, 1, bass.ds(g, 1), :].rearrange("p a n -> p (a n)"), m.ps[2 + slot][GS:P, 0:NC])
                nc.vector.tensor_copy(s.sv[:, 1, :, bass.ds(g, 1)].rearrange("p b a -> p (b a)"),
                                      m.ps[2 + slot][GS:P, NC + B:UW]).then_inc(m.dve_b.sem, 1)

            with dve.Fori(0, G // 2) as i:
                for slot in range(2):
                    move(i * 2 + slot, slot)

            def advance(dst, h, mul, t1, t2):
                nc.vector.tensor_tensor(t1, mul[0], h, ALU.mult)
                nc.vector.tensor_tensor(t2, mul[1], h, ALU.mult)
                dve.drain()
                nc.vector.tensor_tensor(dst, dst, t1, ALU.add)
                dve.drain()
                nc.vector.tensor_tensor(dst[:, 0], dst[:, 0], t2[:, 1], ALU.add)
                nc.vector.tensor_tensor(dst[:, 1], dst[:, 1], t2[:, 0], ALU.add)
                dve.drain()

            def power(j):
                row = s.powers[:, bass.ds(j, 1)]
                return row[:, :, 0:2, :].rearrange("p a r g -> p (a r) g"), row[:, :, 2:4, :].rearrange("p a r g -> p (a r) g")

            def wide(mul, n):
                return [x.unsqueeze(3).to_broadcast([GS, 2, G, n]) for x in mul]

            l8 = (s.powers[:, 0, 0:2, :], s.powers[:, 0, 2:4, :])
            t1, t2 = s.st[:, 0:2, :], s.st[:, 2:4, :]
            for j in range(1, RUN):
                was, now = s.powers[:, j - 1], s.powers[:, j]
                nc.vector.tensor_tensor(t1, was[:, 2:4, :], l8[1], ALU.mult)
                nc.vector.tensor_tensor(t2, was[:, 2:4, :], l8[0], ALU.mult)
                nc.vector.tensor_tensor(now[:, 0:2, :], was[:, 0:2, :], l8[0], ALU.mult)
                nc.vector.tensor_tensor(now[:, 2:4, :], was[:, 0:2, :], l8[1], ALU.mult)
                dve.drain()
                nc.vector.tensor_tensor(now[:, 0:2, :], now[:, 0:2, :], t1, ALU.subtract)
                nc.vector.tensor_tensor(now[:, 2:4, :], now[:, 2:4, :], t2, ALU.add)
                dve.drain()
            runs = s.h.rearrange("p r g (b j) -> p r g b j", j=RUN)
            n_runs = NC // RUN

            def chunk(j, b0, b1):
                return runs[:, :, :, b0:b1, bass.ds(j, 1)].rearrange("p r g b a -> p r g (b a)")

            scratch = m.wts[0:GS].rearrange("p a b c -> p (a b c)")
            size = 2 * G * n_runs
            w1, w2 = (scratch[:, size * i:size * i + size].rearrange("p (r g b) -> p r g b", r=2, g=G) for i in range(2))
            with dve.Fori(1, RUN) as j:
                advance(chunk(j, 0, n_runs), chunk(j - 1, 0, n_runs), wide(l8, n_runs), w1, w2)
            end = lambda b: runs[:, :, :, bass.ds(b, 1), RUN - 1].rearrange("p r g a -> p r (g a)")
            with dve.Fori(1, n_runs) as b:
                advance(end(b), end(b - 1), power(RUN - 1), t1, t2)
            with dve.Fori(0, RUN - 1) as j:
                advance(chunk(j, 1, n_runs), runs[:, :, :, 0:n_runs - 1, RUN - 1], wide(power(j), n_runs - 1),
                        w1[:, :, :, 0:n_runs - 1], w2[:, :, :, 0:n_runs - 1])
            for b in range(B):
                dve.wait_ge(m.act_b.sem, m.act_b.at(G))
                advance(s.sv[:, :, b, :], s.s0[:, :, b, :], (s.l1[:, 0:2, :], s.l1[:, 2:4, :]), t1, t2)

    m.pool_a.passed(G)
    m.pe_a.passed(G)
    m.pe_b.passed(G)
    m.act_a.passed(G)
    m.act_b.passed(G)
    m.dve_b.passed(G)


def phase_s5_outputs(m):
    nc = m.nc
    s = m.s5
    fin_sb = m.wts[:, 0].rearrange("p a b -> p (a b)")
    with nc.Block() as block:

        @block.gpsimd
        def _(pool):
            def step(g, slot, first):
                pool.drain()
                if not first:
                    pool.wait_ge(m.pe_a.sem, m.pe_a.at(g - 3))
                s5_b_powers(pool, m, s, g, slot).then_inc(m.pool_a.sem, 1)

            for slot in range(2, 4):
                nc.gpsimd.memset(s.e[slot][:, P:2 * P], 0.0)
            for g in range(4):
                step(g, g, True)
            with pool.Fori(1, G // 4) as i:
                for slot in range(4):
                    step(i * 4 + slot, slot, False)

        @block.vector
        def _(dve):
            nc.vector.memset(s.starts[:, :, 0:1], 0.0)
            nc.vector.tensor_copy(s.starts[GS:P, :, 1:NC], s.h[:, 1, :, 0:NC - 1])
            nc.vector.tensor_copy(s.starts[GS:P, :, NC:HW], s.s0[:, 1].rearrange("p b g -> p g b")).then_inc(m.dve_a.sem, 1)

            def c_powers(g, slot, first):
                dve.drain()
                if not first:
                    dve.wait_ge(m.pe_b.sem, m.pe_b.at(g - 3))
                y1 = s.y1[:, :, bass.ds(g, 1)].to_broadcast([P, SC + 1, GC])
                y2 = s.y2[:, :, bass.ds(g, 1)].to_broadcast([P, SC + 1, GC])
                view = lambda t: t.rearrange("p (s c) -> p s c", s=SC + 1)
                nc.vector.tensor_tensor(view(s.t3), y1, s.c_t[:, 0, bass.ds(g, 1), :].to_broadcast([P, SC + 1, GC]), ALU.mult)
                nc.vector.tensor_tensor(view(s.t4), y2, s.c_t[:, 1, bass.ds(g, 1), :].to_broadcast([P, SC + 1, GC]), ALU.mult)
                dve.drain()
                nc.vector.tensor_tensor(s.ct[slot], view(s.t3), view(s.t4), ALU.add).then_inc(m.dve_b.sem, 1)

            def out(g, slot):
                dve.wait_ge(m.pe_b.sem, m.pe_b.at(g + 1))
                nc.vector.tensor_copy(s.u[:, bass.ds(g, 1), 0:HW].rearrange("p a n -> p (a n)"),
                                      m.ps[2 + slot][:, 0:HW]).then_inc(m.dve_c.sem, 1)

            for g in range(4):
                c_powers(g, g, True)
            out(0, 0)
            with dve.Fori(1, G // 4) as i:
                for slot in range(4):
                    c_powers(i * 4 + slot, slot, False)
                    out(i * 4 + slot - 3, (slot + 1) % 2)
            for g in range(G - 3, G):
                out(g, g % 2)

        @block.scalar
        def _(act):
            nc.scalar.copy(s.starts[0:GS, :, 1:NC], s.h[:, 0, :, 0:NC - 1])
            nc.scalar.copy(s.starts[0:GS, :, NC:HW], s.s0[:, 0].rearrange("p b g -> p g b")).then_inc(m.act_a.sem, 1)

            def kernel_copy(g, slot, first):
                act.wait_ge(m.pe_a.sem, m.pe_a.at(g + 1))
                if not first:
                    act.wait_ge(m.pe_b.sem, m.pe_b.at(g - 1))
                nc.scalar.copy(s.mt[slot], m.ps[slot][:, 0:P]).then_inc(m.act_b.sem, 1)

            for g in range(2):
                kernel_copy(g, g, True)
            with act.Fori(1, G // 2) as i:
                for slot in range(2):
                    kernel_copy(i * 2 + slot, slot, False)
            act.wait_ge(m.pe_c.sem, m.pe_c.at(1))
            nc.scalar.copy(fin_sb[0:G, 0:P], m.ps[4][0:G, 0:P])
            nc.scalar.copy(fin_sb[:, P:P + 4 * GS], m.ps[5][:, 0:4 * GS]).then_inc(m.act_c.sem, 1)

        @block.tensor
        def _(pe):
            for part in range(2):
                nc.tensor.transpose(m.ps[4][0:G, GS * part:GS * part + GS], s.h[:, part, :, NC - 1], m.ident[0:GS, 0:GS])
                for a in range(2):
                    last = nc.tensor.transpose(m.ps[5][:, GS * (2 * part + a):GS * (2 * part + a) + GS],
                                               s.sv[:, part, 4 * a:4 * a + 4, :].rearrange("p b g -> p (b g)"),
                                               m.ident[0:GS, 0:GS])
            last.then_inc(m.pe_c.sem, 1)

            def kernel_of(g, slot, four, first):
                pe.wait_ge(m.pool_a.sem, m.pool_a.at(g + 1))
                pe.wait_ge(m.dve_b.sem, m.dve_b.at(g + 1))
                if not first:
                    pe.wait_ge(m.act_b.sem, m.act_b.at(g - 1))
                for t in range(SC):
                    last = nc.tensor.matmul(m.ps[slot][:, GC * t:GC * t + GC],
                                            s.e[four][:, GC * (SC - 1 - t):GC * (SC - 1 - t) + P],
                                            s.ct[four][:, 0, :], start=True, stop=True)
                last.then_inc(m.pe_a.sem, 1)

            def y_of(g, slot, four, first):
                pe.wait_ge(m.act_b.sem, m.act_b.at(g + 1))
                if not first:
                    pe.wait_ge(m.dve_c.sem, m.dve_c.at(g - 1))
                u = s.u[:, bass.ds(g, 1), 0:HW].rearrange("p a n -> p (a n)")
                h = s.starts[:, bass.ds(g, 1), :].rearrange("p a n -> p (a n)")
                nc.tensor.matmul(m.ps[2 + slot][:, 0:HW], s.mt[slot], u, start=True, stop=False)
                nc.tensor.matmul(m.ps[2 + slot][:, 0:HW], s.ct[four][:, 1:, :].rearrange("p s c -> p (s c)"), h,
                                 start=False, stop=True).then_inc(m.pe_b.sem, 1)

            def pair(g0, four, first):
                for slot in range(2):
                    kernel_of(g0 + slot, slot, four + slot, first)
                if first:
                    pe.wait_ge(m.dve_a.sem, m.dve_a.at(1))
                    pe.wait_ge(m.act_a.sem, m.act_a.at(1))
                for slot in range(2):
                    y_of(g0 + slot, slot, four + slot, first)

            pair(0, 0, True)
            pair(2, 2, False)
            with pe.Fori(1, G // 4) as i:
                pair(i * 4, 0, False)
                pair(i * 4 + 2, 2, False)

        @block.sync
        def _(sp):
            sp.wait_ge(m.act_c.sem, m.act_c.at(1))
            for part, name in enumerate(("re", "im")):
                sp.dma_start(m.outs["p_s5_" + name].rearrange("b g s -> (b g) s"),
                             fin_sb[0:G, GS * part:GS * part + GS]).then_inc(m.stored.sem, 16)
                sp.dma_start(m.outs["s_s5_" + name].rearrange("(a b) g s -> (b g) a s", a=2),
                             fin_sb[:, P + 2 * GS * part:P + 2 * GS * part + 2 * GS].rearrange("p (a s) -> p a s", a=2)
                             ).then_inc(m.stored.sem, 16)
            sp.wait_ge(m.stored.sem, m.stored.at(64))

    m.stored.passed(64)
    for x in (m.pool_a, m.pe_a, m.pe_b, m.act_b, m.dve_b, m.dve_c):
        x.passed(G)
    for x in (m.act_a, m.dve_a, m.pe_c, m.act_c):
        x.passed(1)


def phase_s5_glu(m):
    nc = m.nc
    s = m.s5
    w_glu = m.wts[:].rearrange("p a b c -> p (a b c)").rearrange("p (k n) -> p k n", k=4)
    y = m.normed[:, 4:8, :]
    x = Carver(m.resid[:])
    inner = x.take(4, N)
    gated = x.take(4, N)
    with nc.Block() as block:

        @block.sync
        def _(sp):
            sp.dma_start(w_glu, m.ins["w_glu"].rearrange("(k p) n -> p k n", p=P)).then_inc(m.dma_b.sem, 16)
            out = m.s5_dram.rearrange("(g c) n -> c g n", c=GC)
            for step in range(SC):
                sp.dma_start(out[:, :, NC * step:NC * step + NC], s.u[GC * step:GC * step + GC, :, 0:NC]
                             ).then_inc(m.dma_a.sem, 16)
            sp.dma_start(out[:, :, T:N], s.u[0:GC, :, NC:HW]).then_inc(m.dma_a.sem, 16)
            sp.wait_ge(m.dma_a.sem, m.dma_a.at(9 * 16))
            sp.dma_start(y, m.s5_dram.rearrange("(k p) n -> p k n", p=P)).then_inc(m.dma_c.sem, 16)

        @block.vector
        def _(dve):
            V = nc.vector
            dve.wait_ge(m.dma_c.sem, m.dma_c.at(16))
            for k in range(4):
                V.scalar_tensor_tensor(y[:, k], m.proj[:, k], m.s5_d[:, k:k + 1], y[:, k], ALU.mult, ALU.add)
                dve.drain()
                V.tensor_tensor(inner[:, k], y[:, k], y[:, k], ALU.mult)
                dve.drain()
                V.tensor_scalar(inner[:, k], inner[:, k], 0.044715, 1.0, ALU.mult, ALU.add)
                dve.drain()
                V.tensor_tensor(inner[:, k], inner[:, k], y[:, k], ALU.mult).then_inc(m.dve_a.sem, 1)
            for k in range(4):
                dve.wait_ge(m.act_a.sem, m.act_a.at(k + 1))
                V.tensor_scalar(inner[:, k], inner[:, k], 0.5, 0.5, ALU.mult, ALU.add)
                dve.drain()
                V.tensor_tensor(y[:, k], inner[:, k], y[:, k], ALU.mult).then_inc(m.dve_b.sem, 1)
            for k in range(4):
                dve.wait_ge(m.act_b.sem, m.act_b.at(k + 1))
                V.tensor_tensor(m.normed[:, k, 0:T].rearrange("p (c s) -> p s c", s=SC),
                                gated[:, k, 0:T].rearrange("p (s c) -> p s c", s=SC),
                                y[:, k, 0:T].rearrange("p (s c) -> p s c", s=SC), ALU.mult)
                V.tensor_tensor(m.normed[:, k, T:N], gated[:, k, T:N], y[:, k, T:N], ALU.mult)

        @block.scalar
        def _(act):
            for k in range(4):
                act.wait_ge(m.dve_a.sem, m.dve_a.at(k + 1))
                nc.scalar.activation(inner[:, k], inner[:, k], ACT.Tanh, scale=math.sqrt(2 / math.pi)).then_inc(m.act_a.sem, 1)
            for o in range(4):
                act.wait_ge(m.pe_a.sem, m.pe_a.at(o + 1))
                for c in range(CHUNKS):
                    last = nc.scalar.activation(gated[:, o, token_cols(c)], m.ps[3 * (o % 2) + c][:, 0:CH], ACT.Sigmoid,
                                                bias=m.b_glu[:, o:o + 1])
                last.then_inc(m.act_b.sem, 1)

        @block.tensor
        def _(pe):
            pe.wait_ge(m.dma_b.sem, m.dma_b.at(16))
            for o in range(4):
                if o >= 2:
                    pe.wait_ge(m.act_b.sem, m.act_b.at(o - 1))
                for k in range(4):
                    if o == 0:
                        pe.wait_ge(m.dve_b.sem, m.dve_b.at(k + 1))
                    for c in range(CHUNKS):
                        last = nc.tensor.matmul(m.ps[3 * (o % 2) + c][:, 0:CH], w_glu[:, k, o * P:(o + 1) * P],
                                                y[:, k, token_cols(c)], start=(k == 0), stop=(k == 3))
                last.then_inc(m.pe_a.sem, 1)

    m.dma_a.passed(9 * 16)
    m.dma_b.passed(16)
    m.dma_c.passed(16)
    for q in (m.dve_a, m.dve_b, m.act_a, m.act_b, m.pe_a):
        q.passed(4)


def ml_tiles(m):
    s = m.ml = Tiles()
    a = Carver(m.resid[:])
    s.ig, s.lf, s.b, s.mx, s.a, s.tmp, s.mask = (a.take(N, parts=MH) for _ in range(7))
    s.sel = a.take(MH, P, parts=MH)
    s.bias = a.take(2, parts=MH)
    s.m_prev = a.take(NMC, parts=MH)
    s.decay_row = a.take(NMC, parts=MH)
    s.gap = a.take(NMC, parts=MH)
    s.m0 = a.take(B, parts=MH)
    s.m_s = a.take(B, parts=MH)
    s.rows_s = a.take(3, B, parts=MH)
    c = Carver(m.hidden[:])
    s.stage = [c.take(12, MC) for _ in range(2)]
    s.c_state = c.take(MH, DH + 1)
    s.v_ext = c.take(MH, DH + 1)
    s.num = c.take(MH, DH + 1)
    s.inter = c.take(MH, DH + 1)
    s.k_tok = c.take(MH, DH)
    s.decays = c.take(MH, MC)
    s.probs = c.take(MH, MC)
    s.h_tok = c.take(MH, DH)
    s.pack = m.s5_small[:, 0, 0:T]
    x = Carver(m.s5_small[:])
    x.take(T)
    s.cols = x.take(NMC, 4, MH)
    s.decay = x.take(MH, NMC)
    s.bc_s = x.take(3, MH, B)
    s.den = x.take(2, MH)
    s.nt = x.take(B, MH)
    s.kw = x.take(MH, B)
    s.prod = x.take(MH, B)
    s.dn = x.take(3, MH, B)
    s.num_s = x.take(MH, B)
    s.n_rows = x.take(2, P)
    return s


def phase_ml_gates(m):
    nc = m.nc
    s = ml_tiles(m)
    with nc.Block() as block:

        @block.sync
        def _(sp):
            sp.dma_start(s.bias[:, 0:1], m.ins["b_igate"].rearrange("(h a) -> h a", a=1)).then_inc(m.dma_a.sem, 16)
            sp.dma_start(s.bias[:, 1:2], m.ins["b_fgate"].rearrange("(h a) -> h a", a=1)).then_inc(m.dma_a.sem, 16)
            with nc.allow_non_contiguous_dma("32 values"):
                sp.dma_start(s.m0, m.ins["state_mlstm_m"].rearrange("b h -> h b")).then_inc(m.dma_a.sem, 16)
            sp.wait_ge(m.dve_d.sem, m.dve_d.at(1))
            with nc.allow_non_contiguous_dma("36 values"):
                sp.dma_start(m.outs["p_m"].rearrange("b h -> h b"), s.mx[:, T - 1:T]).then_inc(m.stored.sem, 16)
                sp.dma_start(m.outs["s_m"].rearrange("b h -> h b"), s.m_s).then_inc(m.stored.sem, 16)
            sp.wait_ge(m.stored.sem, m.stored.at(32))

        @block.gpsimd
        def _(pool):
            nc.gpsimd.memset(s.sel, 0.0)
            nc.gpsimd.memset(s.pack, 0.0).then_inc(m.pool_b.sem, 1)
            nc.gpsimd.memset(s.mask[:, 0:T], 1.0)
            pool.drain()
            nc.gpsimd.memset(s.mask[:, 0:T:MC], 0.0)
            nc.gpsimd.affine_select(out=s.sel, in_=s.sel, compare_op=ALU.not_equal, fill=1.0, base=0,
                                    pattern=[[-1, MH], [0, P]], channel_multiplier=1).then_inc(m.pool_a.sem, 1)

        @block.scalar
        def _(act):
            act.wait_ge(m.dve_a.sem, m.dve_a.at(1))
            nc.scalar.activation(s.tmp, s.tmp, ACT.Exp, scale=-1.0).then_inc(m.act_a.sem, 1)
            act.wait_ge(m.dve_b.sem, m.dve_b.at(1))
            nc.scalar.activation(s.tmp, s.tmp, ACT.Ln).then_inc(m.act_b.sem, 1)
            act.wait_ge(m.dve_c.sem, m.dve_c.at(1))
            nc.scalar.copy(s.pack[0:4], s.ig[:, 0:T])
            nc.scalar.activation(s.pack[32:36], s.tmp[:, 0:T], ACT.Exp)
            nc.scalar.activation(s.pack[64:68], s.mask[:, 0:T], ACT.Exp)
            nc.scalar.activation(s.pack[96:100], s.mx[:, 0:T], ACT.Exp, scale=-1.0)
            nc.scalar.activation(s.decay_row, s.decay_row, ACT.Exp)
            nc.scalar.activation(s.rows_s, s.rows_s, ACT.Exp).then_inc(m.act_c.sem, 1)
            for h in range(MH):
                nc.scalar.activation(m.proj[:, 16 + h], m.proj[:, 16 + h], ACT.Sigmoid)

        @block.vector
        def _(dve):
            V = nc.vector
            dve.wait_ge(m.dma_a.sem, m.dma_a.at(48))
            V.tensor_scalar(s.ig, m.gates[0:4, 0], s.bias[:, 0:1], None, ALU.add)
            V.tensor_copy(s.b, m.gates[32:36, 0])
            dve.drain()
            V.tensor_scalar(s.lf, s.b, s.bias[:, 1:2], None, ALU.add)
            dve.drain()
            V.scalar_tensor_tensor(s.tmp, s.lf, -1.0, s.lf, ALU.mult, ALU.max).then_inc(m.dve_a.sem, 1)
            dve.wait_ge(m.act_a.sem, m.act_a.at(1))
            V.tensor_scalar(s.tmp, s.tmp, 1.0, None, ALU.add).then_inc(m.dve_b.sem, 1)
            dve.wait_ge(m.act_b.sem, m.act_b.at(1))
            V.scalar_tensor_tensor(s.lf, s.lf, 0.0, s.tmp, ALU.min, ALU.subtract)
            dve.drain()
            dve.wait_ge(m.pool_a.sem, m.pool_a.at(1))
            V.tensor_tensor_scan(s.b[:, 0:T], s.mask[:, 0:T], s.lf[:, 0:T], 0.0, ALU.mult, ALU.add)
            V.tensor_tensor_scan(s.mx[:, 0:T], s.lf[:, 0:T], s.ig[:, 0:T], 0.0, ALU.add, ALU.max)
            V.tensor_tensor(s.tmp[:, 0:B], s.lf[:, T:N], s.m0, ALU.add)
            dve.drain()
            V.tensor_tensor(s.m_s, s.tmp[:, 0:B], s.ig[:, T:N], ALU.max)
            V.memset(s.m_prev[:, 0:1], 0.0)
            V.tensor_copy(s.m_prev[:, 1:], s.mx[:, MC - 1:T - 1:MC])
            V.tensor_tensor(s.gap, s.b[:, MC - 1:T:MC], s.mx[:, MC - 1:T:MC], ALU.subtract)
            dve.drain()
            V.tensor_tensor(s.rows_s[:, 0], s.tmp[:, 0:B], s.m_s, ALU.subtract)
            V.tensor_tensor(s.rows_s[:, 1], s.ig[:, T:N], s.m_s, ALU.subtract)
            V.tensor_scalar(s.rows_s[:, 2], s.m_s, -1.0, None, ALU.mult)
            V.tensor_tensor(s.decay_row, s.gap, s.m_prev, ALU.add)
            V.tensor_tensor(s.a[:, 0:T], s.b[:, 0:T], s.mx[:, 0:T], ALU.subtract)
            V.tensor_tensor(s.ig[:, 0:T], s.ig[:, 0:T], s.b[:, 0:T], ALU.subtract)
            dve.drain()
            chunks = lambda x: x[:, 0:T].rearrange("p (c t) -> p c t", c=NMC)
            V.tensor_tensor(chunks(s.tmp), chunks(s.a), s.m_prev.unsqueeze(2).to_broadcast([MH, NMC, MC]), ALU.add)
            dve.wait_ge(m.pool_b.sem, m.pool_b.at(1))
            V.tensor_tensor(chunks(s.mask), chunks(s.ig), s.gap.unsqueeze(2).to_broadcast([MH, NMC, MC]),
                            ALU.add).then_inc(m.dve_c.sem, 1)
            dve.drain()
            V.memset(s.bias[:, 0:1], 0.0).then_inc(m.dve_d.sem, 1)
            dve.wait_ge(m.pe_a.sem, m.pe_a.at(1))
            for half in range(2):
                V.tensor_copy(s.cols[:, 4 * half:4 * half + 4].rearrange("p c q h -> p (c q) h"),
                              m.ps[half][:].rearrange("p (x w) -> p x w", w=32)[:, :, 0:MH])
            V.tensor_copy(s.decay, m.ps[2][:, 0:MH * NMC].rearrange("p (h c) -> p h c", h=MH))
            V.tensor_copy(s.bc_s.rearrange("p q h b -> p h q b"),
                          m.ps[3][:, 0:MH * 3 * B].rearrange("p (h q b) -> p h q b", h=MH, q=3))

        @block.tensor
        def _(pe):
            pe.wait_ge(m.act_c.sem, m.act_c.at(1))
            for c in range(NMC):
                nc.tensor.transpose(m.ps[c // 4][:, (c % 4) * P:(c % 4) * P + P], s.pack[:, c * MC:(c + 1) * MC], m.ident[:])
            for h in range(MH):
                nc.tensor.matmul(m.ps[2][:, NMC * h:NMC * h + NMC], s.sel[:, h], s.decay_row, start=True, stop=True)
                last = nc.tensor.matmul(m.ps[3][:, 3 * B * h:3 * B * h + 3 * B], s.sel[:, h],
                                        s.rows_s.rearrange("p q b -> p (q b)"), start=True, stop=True)
            last.then_inc(m.pe_a.sem, 1)

    m.dma_a.passed(48)
    m.stored.passed(32)
    for x in (m.pool_a, m.pool_b, m.act_a, m.act_b, m.act_c, m.dve_a, m.dve_b, m.dve_c, m.dve_d, m.pe_a):
        x.passed(1)


def phase_ml_chunks(m):
    nc = m.nc
    s = m.ml
    scale = DH ** -0.5
    ps_a, ps_s, ps_k, ps_v = m.ps[0], m.ps[1], m.ps[2], m.ps[3]
    W = DH + 1
    heads = lambda bank: bank[:].rearrange("p (h t) -> p h t", h=MH)
    with nc.Block() as block:

        @block.sync
        def _(sp):
            def stage(c, slot, first):
                if not first:
                    sp.wait_ge(m.pe_b.sem, m.pe_b.at(c - 1))
                load = m.dma_b if slot else m.dma_a
                sp.dma_start(s.stage[slot], m.proj[:, 4:16, bass.ds(c * MC, MC)]).then_inc(load.sem, 16)

            for c in range(2):
                stage(c, c, True)
            with sp.Fori(1, NMC // 2) as i:
                for slot in range(2):
                    stage(i * 2 + slot, slot, False)
            sp.wait_ge(m.dve_d.sem, m.dve_d.at(NMC))
            sp.dma_start(m.outs["p_c"].rearrange("b h k v -> k (b h) v"), s.c_state[:, :, 0:DH]).then_inc(m.stored.sem, 16)
            sp.wait_ge(m.act_d.sem, m.act_d.at(1))
            sp.dma_start(m.outs["p_n"].rearrange("b h k -> (b h) k"), s.n_rows[0:MH, 0]).then_inc(m.stored.sem, 16)
            sp.wait_ge(m.stored.sem, m.stored.at(32))

        @block.tensor
        def _(pe):
            def scores(c, slot, first):
                load = m.dma_b if slot else m.dma_a
                pe.wait_ge(load.sem, load.at((c - slot) * 8 + 16))
                if not first:
                    pe.wait_ge(m.act_a.sem, m.act_a.at(c))
                    pe.wait_ge(m.dve_a.sem, m.dve_a.at(c))
                    pe.wait_ge(m.act_b.sem, m.act_b.at(c))
                x = s.stage[slot]
                for h in range(MH):
                    nc.tensor.matmul(heads(ps_a)[:, h], s.sel[:, h], s.a[:, bass.ds(c * MC, MC)], start=True, stop=True)
                for h in range(MH):
                    nc.tensor.matmul(heads(ps_s)[:, h], x[:, 4 + h], x[:, h], start=True, stop=True)
                for h in range(MH):
                    nc.tensor.transpose(heads(ps_k)[:, h], x[:, 4 + h], m.ident[:])
                    last = nc.tensor.transpose(heads(ps_v)[:, h], x[:, 8 + h], m.ident[:])
                last.then_inc(m.pe_a.sem, 1)

            def combine(c, slot, first):
                pe.wait_ge(m.dve_a.sem, m.dve_a.at(c + 1))
                pe.wait_ge(m.act_b.sem, m.act_b.at(c + 1))
                if not first:
                    pe.wait_ge(m.dve_d.sem, m.dve_d.at(c))
                    pe.wait_ge(m.dve_e.sem, m.dve_e.at(c))
                x = s.stage[slot]
                for h in range(MH):
                    bank = m.ps[4 + h]
                    nc.tensor.matmul(bank[:, 0:W], s.probs[:, h], s.v_ext[:, h], start=True, stop=True)
                    nc.tensor.matmul(bank[:, W:2 * W], x[:, h], s.c_state[:, h], start=True, stop=True)
                    last = nc.tensor.matmul(bank[:, 2 * W:3 * W], s.k_tok[:, h], s.v_ext[:, h], start=True, stop=True)
                last.then_inc(m.pe_b.sem, 1)

            def turn(c):
                pe.wait_ge(m.dve_c.sem, m.dve_c.at(c + 1))
                for h in range(MH):
                    last = nc.tensor.transpose(m.ps[4 + h][:, W:W + DH], s.h_tok[:, h], m.ident[:])
                last.then_inc(m.pe_c.sem, 1)

            def chunk(c, slot, first, last=False):
                combine(c, slot, first)
                if not last:
                    scores(c + 1, 1 - slot, False)
                turn(c)

            scores(0, 0, True)
            pe.wait_ge(m.pool_b.sem, m.pool_b.at(1))
            chunk(0, 0, True)
            with pe.Fori(0, NMC // 2 - 1) as i:
                for slot in (1, 0):
                    chunk(i * 2 + 2 - slot, slot, False)
            chunk(NMC - 1, 1, False, last=True)
            pe.wait_ge(m.dve_d.sem, m.dve_d.at(NMC))
            pe.wait_ge(m.dve_e.sem, m.dve_e.at(NMC))
            nc.tensor.transpose(ps_a[0:MH, 0:P], s.c_state[:, :, DH], m.ident[:]).then_inc(m.pe_d.sem, 1)

        @block.scalar
        def _(act):
            def chunk(c, first):
                cols = lambda q, h: s.cols[:, bass.ds(c, 1), q, h:h + 1].rearrange("p a b -> p (a b)")
                act.wait_ge(m.pe_a.sem, m.pe_a.at(c + 1))
                if not first:
                    act.wait_ge(m.dve_a.sem, m.dve_a.at(c))
                    act.wait_ge(m.pool_a.sem, m.pool_a.at(c))
                for h in range(MH):
                    last = nc.scalar.activation(s.decays[:, h], heads(ps_a)[:, h], ACT.Exp, bias=cols(0, h))
                last.then_inc(m.act_a.sem, 1)
                if not first:
                    act.wait_ge(m.pe_b.sem, m.pe_b.at(c))
                if first:
                    act.wait_ge(m.pool_b.sem, m.pool_b.at(1))
                nc.scalar.copy(s.v_ext[:, :, 0:DH], heads(ps_v))
                for h in range(MH):
                    last = nc.scalar.mul(s.k_tok[:, h], heads(ps_k)[:, h], cols(2, h))
                last.then_inc(m.act_b.sem, 1)
                act.wait_ge(m.pe_b.sem, m.pe_b.at(c + 1))
                if not first:
                    act.wait_ge(m.dve_b.sem, m.dve_b.at(c))
                for h in range(MH):
                    last = nc.scalar.mul(s.inter[:, h], m.ps[4 + h][:, W:2 * W], cols(1, h))
                last.then_inc(m.act_c.sem, 1)

            chunk(0, True)
            with act.Fori(1, NMC) as c:
                chunk(c, False)
            act.wait_ge(m.pe_d.sem, m.pe_d.at(1))
            nc.scalar.copy(s.n_rows[0:MH, 0], ps_a[0:MH, 0:P]).then_inc(m.act_d.sem, 1)

        @block.gpsimd
        def _(pool):
            nc.gpsimd.memset(s.c_state, 0.0)
            nc.gpsimd.memset(s.v_ext, 1.0).then_inc(m.pool_b.sem, 1)
            for c in range(NMC):
                pool.wait_ge(m.act_a.sem, m.act_a.at(c + 1))
                nc.gpsimd.affine_select(out=s.decays, in_=s.decays, compare_op=ALU.is_ge, fill=0.0, base=0,
                                        pattern=[[0, MH], [1, MC]], channel_multiplier=-1).then_inc(m.pool_a.sem, 1)

        @block.vector
        def _(dve):
            V = nc.vector

            def chunk(c, first):
                dve.wait_ge(m.pe_a.sem, m.pe_a.at(c + 1))
                dve.wait_ge(m.pool_a.sem, m.pool_a.at(c + 1))
                if not first:
                    dve.wait_ge(m.pe_b.sem, m.pe_b.at(c))
                V.scalar_tensor_tensor(s.probs, heads(ps_s), scale, s.decays, ALU.mult, ALU.mult).then_inc(m.dve_a.sem, 1)
                dve.wait_ge(m.act_c.sem, m.act_c.at(c + 1))
                for h in range(MH):
                    last = V.tensor_tensor(s.num[:, h], m.ps[4 + h][:, 0:W], s.inter[:, h], ALU.add)
                last.then_inc(m.dve_b.sem, 1)
                for h in range(MH):
                    decay = s.decay[:, h, bass.ds(c, 1)]
                    V.tensor_scalar(s.c_state[:, h], s.c_state[:, h], decay, None, ALU.mult)
                V.drain()
                for h in range(MH):
                    last = V.scalar_tensor_tensor(s.c_state[:, h], m.ps[4 + h][:, 2 * W:3 * W], scale,
                                                  s.c_state[:, h], ALU.mult, ALU.add)
                last.then_inc(m.dve_d.sem, 1)
                den = s.num[:, :, DH]
                V.scalar_tensor_tensor(s.den[:, 0], den, -1.0, den, ALU.mult, ALU.max)
                V.drain()
                V.tensor_tensor(s.den[:, 1], s.den[:, 0], s.cols[:, bass.ds(c, 1), 3, :].rearrange("p a h -> p (a h)"), ALU.max)
                V.drain()
                V.reciprocal(s.den[:, 0], s.den[:, 1])
                V.drain()
                if not first:
                    dve.wait_ge(m.pe_c.sem, m.pe_c.at(c))
                V.tensor_tensor(s.h_tok, s.num[:, :, 0:DH], s.den[:, 0].unsqueeze(2).to_broadcast([P, MH, DH]),
                                ALU.mult).then_inc(m.dve_c.sem, 1)
                dve.wait_ge(m.pe_c.sem, m.pe_c.at(c + 1))
                for half in range(2):
                    turned = m.ps_pair[2 + half][:].rearrange("p (h w) -> p h w", h=2)[:, :, W:W + DH]
                    last = V.tensor_tensor(m.normed[:, 4 + 2 * half:6 + 2 * half, bass.ds(c * MC, MC)], turned,
                                           m.proj[:, 16 + 2 * half:18 + 2 * half, bass.ds(c * MC, MC)], ALU.mult)
                last.then_inc(m.dve_e.sem, 1)

            chunk(0, True)
            with dve.Fori(1, NMC) as c:
                chunk(c, False)

    m.dma_a.passed(16 * NMC // 2)
    m.dma_b.passed(16 * NMC // 2)
    m.stored.passed(32)
    for x in (m.pe_a, m.pe_b, m.pe_c, m.act_a, m.act_b, m.act_c, m.pool_a, m.dve_a, m.dve_b, m.dve_c, m.dve_d, m.dve_e):
        x.passed(NMC)
    for x in (m.pe_d, m.act_d, m.pool_b):
        x.passed(1)


def phase_ml_samples(m):
    nc = m.nc
    s = m.ml
    scale = DH ** -0.5
    c = Carver(m.hidden[:])
    c_old = [c.take(MH, DH) for _ in range(2)]
    c_new = [c.take(MH, DH) for _ in range(2)]
    v_tok = c.take(MH, DH, parts=B)
    v_one = [c.take(MH, DH, parts=B) for _ in range(2)]
    q, k, v, o = (m.proj[:, 4 * i:4 * i + 4, T:N] for i in range(1, 5))
    flat = lambda x: x.rearrange("p h v -> p (h v)")
    with nc.Block() as block:

        @block.sync
        def _(sp):
            sp.dma_start(s.n_rows[0:B * MH, 0], m.ins["state_mlstm_n"].rearrange("b h k -> (b h) k")).then_inc(m.dma_c.sem, 16)

            def load(b, slot, first):
                if not first:
                    sp.wait_ge(m.act_a.sem, m.act_a.at(b - 1))
                sem = m.dma_b if slot else m.dma_a
                sp.dma_start(c_old[slot], m.ins["state_mlstm_c"][bass.ds(b, 1)].rearrange("b h k v -> k (b h) v")
                             ).then_inc(sem.sem, 16)

            for b in range(2):
                load(b, b, True)
            with sp.Fori(1, B // 2) as i:
                for slot in range(2):
                    load(i * 2 + slot, slot, False)
            sp.wait_ge(m.act_b.sem, m.act_b.at(1))
            sp.dma_start(m.outs["s_n"].rearrange("b h k -> (b h) k"), s.n_rows[0:B * MH, 1]).then_inc(m.stored.sem, 16)
            sp.wait_ge(m.stored.sem, m.stored.at(16))

        @block.tensor
        def _(pe):
            for h in range(MH):
                last = nc.tensor.transpose(m.ps[0][0:B, h * DH:(h + 1) * DH], v[:, h], m.ident[:])
            last.then_inc(m.pe_a.sem, 1)
            pe.wait_ge(m.dma_c.sem, m.dma_c.at(16))
            nc.tensor.transpose(m.ps[1][:, 0:B * MH], s.n_rows[0:B * MH, 0], m.ident[0:B * MH, 0:B * MH]).then_inc(m.pe_a.sem, 1)
            pe.wait_ge(m.dve_b.sem, m.dve_b.at(1))
            nc.tensor.transpose(m.ps[2][0:B * MH, 0:P], s.nt.rearrange("p b h -> p (b h)"), m.ident[:])
            nc.tensor.matmul(m.ps[3][:, 0:MH * B], m.ones[:], s.prod.rearrange("p h b -> p (h b)"),
                             start=True, stop=True).then_inc(m.pe_b.sem, 1)

            def spread(b, slot, first):
                pe.wait_ge(m.dve_a.sem, m.dve_a.at(b + 1))
                if not first:
                    pe.wait_ge(m.dve_c.sem, m.dve_c.at(b - 1))
                nc.tensor.matmul(m.ps[4 + slot][:], m.ones[0:B, :], flat(v_one[slot]), start=True, stop=True
                                 ).then_inc(m.pe_c.sem, 1)

            def apply(b, slot):
                pe.wait_ge(m.dve_c.sem, m.dve_c.at(b + 1))
                for h in range(MH):
                    last = nc.tensor.matmul(m.ps[6][:, bass.ds(b + h * B, 1)], c_new[slot][:, h], q[:, h, bass.ds(b, 1)],
                                            start=True, stop=True)
                last.then_inc(m.pe_d.sem, 1)

            for b in range(2):
                spread(b, b, True)
            with pe.Fori(0, B // 2 - 1) as i:
                for slot in range(2):
                    apply(i * 2 + slot, slot)
                for slot in range(2):
                    spread(i * 2 + slot + 2, slot, False)
            for slot in range(2):
                apply(B - 2 + slot, slot)

        @block.scalar
        def _(act):
            def decayed(b, slot):
                sem = m.dma_b if slot else m.dma_a
                act.wait_ge(sem.sem, sem.at((b - slot) * 8 + 16))
                act.wait_ge(m.dve_d.sem, m.dve_d.at(b + 1))
                for h in range(MH):
                    last = nc.scalar.mul(c_new[slot][:, h], c_old[slot][:, h], s.bc_s[:, 0, h, bass.ds(b, 1)])
                last.then_inc(m.act_a.sem, 1)
                act.wait_ge(m.dve_c.sem, m.dve_c.at(b + 1))
                out = m.dma_h if slot else m.dma_g
                act.dma_start(m.outs["s_c"][bass.ds(b, 1)].rearrange("b h k v -> k (b h) v"), c_new[slot]).then_inc(out.sem, 16)

            with act.Fori(0, B // 2) as i:
                for slot in range(2):
                    decayed(i * 2 + slot, slot)
            act.wait_ge(m.dma_g.sem, m.dma_g.at(16 * B // 2))
            act.wait_ge(m.dma_h.sem, m.dma_h.at(16 * B // 2))
            act.wait_ge(m.pe_b.sem, m.pe_b.at(1))
            nc.scalar.copy(s.n_rows[0:B * MH, 1], m.ps[2][0:B * MH, 0:P]).then_inc(m.act_b.sem, 1)

        @block.vector
        def _(dve):
            V = nc.vector
            by_head = lambda x: x.rearrange("p b h -> p h b")
            dve.wait_ge(m.pe_a.sem, m.pe_a.at(2))
            V.tensor_copy(flat(v_tok), m.ps[0][0:B, :])
            V.scalar_tensor_tensor(s.kw, k, scale, s.bc_s[:, 1], ALU.mult, ALU.mult)
            V.tensor_tensor(s.dn[:, 0], by_head(m.ps[1][:, 0:B * MH].rearrange("p (b h) -> p b h", h=MH)),
                            s.bc_s[:, 0], ALU.mult)
            V.drain()
            V.tensor_tensor(by_head(s.nt), s.dn[:, 0], s.kw, ALU.add)
            V.drain()
            V.tensor_tensor(s.prod, by_head(s.nt), q, ALU.mult).then_inc(m.dve_b.sem, 1)
            dve.wait_ge(m.pe_b.sem, m.pe_b.at(1))
            V.tensor_copy(s.dn[:, 0], m.ps[3][:, 0:MH * B].rearrange("p (h b) -> p h b", h=MH))
            V.drain()
            V.scalar_tensor_tensor(s.dn[:, 1], s.dn[:, 0], -1.0, s.dn[:, 0], ALU.mult, ALU.max)
            V.drain()
            V.tensor_tensor(s.dn[:, 1], s.dn[:, 1], s.bc_s[:, 2], ALU.max)
            V.drain()
            V.reciprocal(s.dn[:, 2], s.dn[:, 1])
            V.memset(s.dn[:, 0], 0.0).then_inc(m.dve_d.sem, 2)

            def alone(b, slot):
                V.tensor_scalar(v_one[slot], v_tok, m.ident[0:B, bass.ds(b, 1)], None, ALU.mult).then_inc(m.dve_a.sem, 1)

            def update(b, slot, last_pair):
                dve.wait_ge(m.pe_c.sem, m.pe_c.at(b + 1))
                dve.wait_ge(m.act_a.sem, m.act_a.at(b + 1))
                for h in range(MH):
                    last = V.scalar_tensor_tensor(c_new[slot][:, h], m.ps[4 + slot][:, h * DH:(h + 1) * DH],
                                                  s.kw[:, h, bass.ds(b, 1)], c_new[slot][:, h], ALU.mult, ALU.add)
                last.then_inc(m.dve_c.sem, 1)
                if not last_pair:
                    alone(b + 2, slot)
                    out = m.dma_h if slot else m.dma_g
                    dve.wait_ge(m.pe_d.sem, m.pe_d.at(b + 1))
                    dve.wait_ge(out.sem, out.at((b - slot) * 8 + 16))
                    V.memset(s.dn[:, 0, 0, 0:1], 0.0).then_inc(m.dve_d.sem, 1)

            for b in range(2):
                alone(b, b)
            with dve.Fori(0, B // 2 - 1) as i:
                for slot in range(2):
                    update(i * 2 + slot, slot, False)
            for slot in range(2):
                update(B - 2 + slot, slot, True)
            dve.wait_ge(m.pe_d.sem, m.pe_d.at(B))
            V.tensor_tensor(s.num_s, m.ps[6][:, 0:MH * B].rearrange("p (h b) -> p h b", h=MH), s.dn[:, 2], ALU.mult)
            V.drain()
            V.tensor_tensor(m.normed[:, 4:8, T:N], s.num_s, o, ALU.mult)

    m.dma_c.passed(16)
    m.stored.passed(16)
    for x in (m.dma_a, m.dma_b, m.dma_g, m.dma_h):
        x.passed(16 * B // 2)
    for x in (m.pe_c, m.pe_d, m.act_a, m.dve_a, m.dve_c, m.dve_d):
        x.passed(B)
    m.pe_a.passed(2)
    for x in (m.pe_b, m.act_b, m.dve_b):
        x.passed(1)


def phase_out(m, w_name):
    nc = m.nc
    w = m.ins[w_name].rearrange("(k p) n -> p k n", p=P)
    place_out(m)
    x_hi, x_lo = m.x_hi, m.x_lo
    with nc.Block() as block:

        @block.scalar
        def _(act):
            for k in range(KT):
                nc.scalar.copy(parts(x_hi[:, k]), m.normed[:, k]).then_inc(m.tiles_ready.sem, 1)

        @block.sync
        def _(sp):
            for slot in range(2):
                load_unit(sp, m, slot, 0, w[:, :, slot * P:slot * P + P])
            sp.wait_ge(m.w_loaded0.sem, m.w_loaded0.at(16))
            sp.dma_start(m.resid[:, 0:KT // 2], m.spill[:, 0:KT // 2]).then_inc(m.x_back.sem, 16)
            sp.dma_start(m.resid[:, KT // 2:], m.spill[:, KT // 2:]).then_inc(m.dma_a.sem, 16)
            with sp.Fori(1, KT // 2) as j:
                for slot in range(2):
                    load_unit(sp, m, slot, j, w[:, :, bass.ds((j * 2 + slot) * P, P)])

        @block.gpsimd
        def _(pool):
            with pool.Fori(0, KT // 2) as j:
                for slot in range(2):
                    split_unit(pool, m, slot, j)

        @block.tensor
        def _(pe):
            unit_matmuls(pe, m, 0, 0, x_hi, x_lo, ready=norm_ready(pe, m))
            unit_matmuls(pe, m, 1, 0, x_hi, x_lo)
            with pe.Fori(1, KT // 2) as j:
                for slot in range(2):
                    unit_matmuls(pe, m, slot, j, x_hi, x_lo)

        @block.vector
        def _(dve):
            for k in range(KT):
                dve.wait_ge(m.tiles_ready.sem, m.tiles_ready.at(k + 1))
                nc.vector.tensor_tensor(parts(x_lo[:, k]), m.normed[:, k], x_hi[:, k], ALU.subtract
                                        ).then_inc(m.lo_ready.sem, 1)
            for half, back in enumerate((m.x_back, m.dma_a)):
                dve.wait_ge(back.sem, back.at(16))
                with dve.Fori(half * KT // 4, (half + 1) * KT // 4) as j:
                    for slot in range(2):
                        add_unit(dve, m, slot, j * 2 + slot, j * 2 + slot)

    m.x_back.passed(16)
    m.dma_a.passed(16)
    m.tiles_ready.passed(KT)
    m.lo_ready.passed(KT)
    units_passed(m, KT)


def add_unit(dve, m, slot, u, tile):
    nc = m.nc
    dve.wait_ge(m.unit_done.sem, m.unit_done.at(u + 1))
    for c in range(CHUNKS):
        x = m.resid[:, bass.ds(tile, 1), token_cols(c)].rearrange("p a n -> p (a n)")
        last = nc.vector.tensor_tensor(x, m.ps[3 * slot + c][:, 0:CH], x, ALU.add)
    last.then_inc(m.set_free.sem, 1)


def phase_mlp(m, layer):
    nc = m.nc
    w_up = m.ins["w_up"][layer].rearrange("(k p) n -> p k n", p=P)
    w_down = m.ins["w_down"][layer].rearrange("(q k p) n -> p q k n", p=P, k=KT)
    per_group = 2 * KT
    place_mlp(m)
    with nc.Block() as block:

        @block.gpsimd
        def _(pool):
            with pool.Fori(0, FF_GROUPS * KT) as j:
                for slot in range(2):
                    split_unit(pool, m, slot, j)

        @block.sync
        def _(sp):
            with sp.Fori(0, FF_GROUPS) as g:
                with sp.Fori(0, KT // 2) as j:
                    for slot in range(2):
                        load_unit(sp, m, slot, g * KT + j, w_up[:, :, bass.ds(g * D + (j * 2 + slot) * P, P)])
                with sp.Fori(0, KT // 2) as j:
                    for slot in range(2):
                        load_unit(sp, m, slot, g * KT + KT // 2 + j,
                                  w_down[:, bass.ds(g, 1), :, bass.ds((j * 2 + slot) * P, P)].rearrange("p a k n -> p (a k) n"))

        @block.tensor
        def _(pe):
            def up(g, j):
                for slot in range(2):
                    unit_matmuls(pe, m, slot, g * KT + j, m.x_hi, m.x_lo)

            def down(g, j, slot, first):
                def hidden_tile(k):
                    pe.wait_ge(m.act_a.sem, m.act_a.at(g * KT + k + 1))
                    pe.wait_ge(m.dve_b.sem, m.dve_b.at(g * KT + k + 1))
                unit_matmuls(pe, m, slot, g * KT + KT // 2 + j, m.h_hi, m.h_lo, ready=hidden_tile if first else None)

            def rest(g):
                with pe.Fori(1, KT // 2) as j:
                    up(g, j)
                down(g, 0, 0, True)
                down(g, 0, 1, False)
                with pe.Fori(1, KT // 2) as j:
                    for slot in range(2):
                        down(g, j, slot, False)

            norm_first_units(pe, m)
            rest(0)
            with pe.Fori(1, FF_GROUPS) as g:
                up(g, 0)
                rest(g)

        @block.scalar
        def _(act):
            norm_act(act, m, m.g_mlp[layer])
            norm_root(act, m)
            with act.Fori(0, FF_GROUPS * KT // 2) as i:
                for slot in range(2):
                    u = i * 2 + slot
                    act.wait_ge(m.dve_a.sem, m.dve_a.at(u + 1))
                    x = m.h_hi[:, bass.ds((i % (KT // 2)) * 2 + slot, 1), :].rearrange("p a n -> p (a n)")
                    nc.scalar.activation(m.relu[slot], m.relu[slot], ACT.Square)
                    act.drain()
                    nc.scalar.copy(parts(x), m.relu[slot]).then_inc(m.act_a.sem, 1)

        @block.vector
        def _(dve):
            norm_dve(dve, m, m.g_mlp[layer])
            dve.wait_ge(m.inv_done.sem, m.inv_done.at(1))

            def low_part(g, j, slot):
                u = j * 2 + slot
                dve.wait_ge(m.act_a.sem, m.act_a.at(g * KT + u + 1))
                nc.vector.tensor_tensor(flat(parts(m.h_lo[:, bass.ds(u, 1), :])), m.relu[slot],
                                        flat(m.h_hi[:, bass.ds(u, 1), :]), ALU.subtract).then_inc(m.dve_b.sem, 1)

            def rectify(g, j, slot, first=False):
                u = j * 2 + slot
                dve.wait_ge(m.unit_done.sem, m.unit_done.at(g * per_group + u + 1))
                if not first:
                    dve.wait_ge(m.dve_b.sem, m.dve_b.at(g * KT + u - 1))
                for c in range(CHUNKS):
                    last = nc.vector.scalar_tensor_tensor(m.relu[slot][:, token_cols(c)], m.ps[3 * slot + c][:, 0:CH], 0.0,
                                                          m.inv_rms[:, token_cols(c)], ALU.max, ALU.mult)
                last.then_inc(m.dve_a.sem, 1)
                dve.wait_ge(m.dve_a.sem, m.dve_a.at(g * KT + u + 1))
                nc.vector.memset(m.mark[:], 0.0).then_inc(m.set_free.sem, 1)

            def group(g, first):
                for slot in range(2):
                    rectify(g, 0, slot, first)
                with dve.Fori(1, KT // 2) as j:
                    for slot in range(2):
                        low_part(g, j - 1, slot)
                        rectify(g, j, slot)
                for slot in range(2):
                    low_part(g, KT // 2 - 1, slot)
                with dve.Fori(0, KT // 2) as j:
                    for slot in range(2):
                        add_unit(dve, m, slot, g * per_group + KT + j * 2 + slot, j * 2 + slot)

            group(0, True)
            with dve.Fori(1, FF_GROUPS) as g:
                group(g, False)

    norm_passed(m)
    units_passed(m, FF_GROUPS * per_group)
    m.act_a.passed(FF_GROUPS * KT)
    m.dve_a.passed(FF_GROUPS * KT)
    m.dve_b.passed(FF_GROUPS * KT)


def phase_final(m):
    nc = m.nc
    m.left.close()
    place_wide(m, "y_rows")
    g_row = m.proj[:, 0, 0:D]
    y = [m.proj[:, 2 + i, 0:D] for i in range(2)]
    sq = m.proj[:, 4, 0:D]
    st = m.proj[:, 5, 0:4]
    n_out = TB + 1
    with nc.Block() as block:

        @block.sync
        def _(sp):
            sp.dma_start(g_row, m.ins["norm_final"].partition_broadcast(P)).then_inc(m.dma_a.sem, 16)
            for t in range(n_out):
                sp.wait_ge(m.dve_b.sem, m.dve_b.at(t + 1))
                out = m.dma_c if t % 2 else m.dma_b
                if t < TB:
                    sp.dma_start(m.outs["y_prompt"][0, t * P:(t + 1) * P, :], y[t % 2]).then_inc(out.sem, 16)
                else:
                    sp.dma_start(m.outs["y_sample"].rearrange("b o f -> (b o) f"), y[t % 2][0:B]).then_inc(out.sem, 16)
            sp.wait_ge(m.dma_b.sem, m.dma_b.at(16 * 5))
            sp.wait_ge(m.dma_c.sem, m.dma_c.at(16 * 4))

        @block.tensor
        def _(pe):
            for t in range(n_out):
                n = P if t < TB else B
                if t >= 2:
                    pe.wait_ge(m.dve_b.sem, m.dve_b.at(t - 1))
                for k in range(KT):
                    last = nc.tensor.transpose(m.ps[2 * (t % 2) + k // 4][0:n, (k % 4) * P:(k % 4 + 1) * P],
                                               m.resid[:, k, t * P:t * P + n], m.ident[:])
                last.then_inc(m.pe_a.sem, 1)

        @block.scalar
        def _(act):
            for t in range(n_out):
                n = P if t < TB else B
                act.wait_ge(m.pe_a.sem, m.pe_a.at(t + 1))
                if t >= 1:
                    act.wait_ge(m.dve_a.sem, m.dve_a.at(t))
                act.drain()
                for half in range(2):
                    last = nc.scalar.activation(sq[0:n, 512 * half:512 * half + 512], m.ps[2 * (t % 2) + half][0:n, :],
                                                ACT.Square, accum_out=st[0:n, half:half + 1])
                last.then_inc(m.act_a.sem, 1)
                act.wait_ge(m.dve_a.sem, m.dve_a.at(t + 1))
                nc.scalar.activation(st[0:n, 3:4], st[0:n, 2:3], ACT.Sqrt).then_inc(m.act_b.sem, 1)

        @block.vector
        def _(dve):
            V = nc.vector
            for t in range(n_out):
                n = P if t < TB else B
                dve.wait_ge(m.act_a.sem, m.act_a.at(t + 1))
                V.tensor_tensor(st[0:n, 2:3], st[0:n, 0:1], st[0:n, 1:2], ALU.add)
                V.drain()
                V.tensor_scalar(st[0:n, 2:3], st[0:n, 2:3], 1.0 / D, EPS, ALU.mult, ALU.add)
                V.drain()
                V.reciprocal(st[0:n, 2:3], st[0:n, 2:3]).then_inc(m.dve_a.sem, 1)
                if t == 0:
                    dve.wait_ge(m.dma_a.sem, m.dma_a.at(16))
                if t >= 2:
                    out = m.dma_c if t % 2 else m.dma_b
                    dve.wait_ge(out.sem, out.at(16 * (t // 2)))
                dve.wait_ge(m.act_b.sem, m.act_b.at(t + 1))
                for half in range(2):
                    h = slice(512 * half, 512 * half + 512)
                    last = V.scalar_tensor_tensor(y[t % 2][0:n, h], m.ps[2 * (t % 2) + half][0:n, :], st[0:n, 3:4],
                                                  g_row[0:n, h], ALU.mult, ALU.mult)
                last.then_inc(m.dve_b.sem, 1)

    m.dma_a.passed(16)
    m.dma_b.passed(16 * 5)
    m.dma_c.passed(16 * 4)
    for x in (m.pe_a, m.act_a, m.act_b, m.dve_a, m.dve_b):
        x.passed(n_out)


QT, KT1, VT1, QIT, KI, KI2 = 0, 8, 10, 12, 16, 17


def score_width(i):
    return P * (i + 1)


def l1_tiles(m):
    s = m.l1 = Tiles()
    c = Carver(m.hidden[:])
    s.v_tok = c.take(TB, KVH * DH)
    s.score = [c.take(score_width(i)) for i in range(TB)]
    s.samples = m.proj[0:B, 18, :]
    s.new = m.proj[0:B, 19, 0:1]
    x = Carver(m.s5_small[:])
    s.w_tok = x.take(TB, IH)
    s.qi_s = x.take(B, IH, parts=IDIM)
    s.w_s = x.take(B, parts=IH)
    s.table = x.take(B * PAGES, parts=1).bitcast(I32)
    s.q_s = x.take(B, AH)
    s.cand = x.take(TB)
    s.cnt = x.take(TB)
    s.prefix = x.take(TB).bitcast(I32)
    s.key = x.take(TB).bitcast(I32)
    s.flip = x.take(TB).bitcast(I32)
    s.bit = x.take(TB).bitcast(I32)
    s.tau = x.take(TB)
    s.need = x.take(TB)
    s.limit = x.take(TB)
    s.sel = x.take(B, 36, parts=B)
    s.stat = x.take(16)
    return s


def phase_in1(m):
    nc = m.nc
    w_in = m.ins["w_in1"].rearrange("(k p) n -> p k n", p=P)
    units = 16
    M = IDIM + IH
    place_in(m, 1)
    with nc.Block() as block:

        @block.gpsimd
        def _(pool):
            for slot in range(2):
                split_unit(pool, m, slot, 0, m.raw_first)
            pool.wait_ge(m.dma_a.sem, m.dma_a.at(16))
            split(pool, m, m.last_raw, m.last_hi[:], m.last_lo[:]).then_inc(m.pool_a.sem, 1)
            with pool.Fori(1, units // 2) as j:
                for slot in range(2):
                    split_unit(pool, m, slot, j)

        @block.sync
        def _(sp):
            for slot in range(2):
                load_unit(sp, m, slot, 0, w_in[:, :, slot * P:slot * P + P], m.raw_first)
            sp.dma_start(m.last_raw, w_in[:, :, units * P:units * P + M]).then_inc(m.dma_a.sem, 16)
            sp.wait_ge(m.w_loaded0.sem, m.w_loaded0.at(16))
            sp.dma_start(m.spill, m.resid[:]).then_inc(m.x_stored.sem, 16)
            sp.wait_ge(m.x_stored.sem, m.x_stored.at(16))
            sp.wait_ge(m.sq_done.sem, m.sq_done.at(KT))
            sp.wait_ge(m.lo_ready.sem, m.lo_ready.at(KT))
            with sp.Fori(1, units // 2) as j:
                for slot in range(2):
                    load_unit(sp, m, slot, j, w_in[:, :, bass.ds((j * 2 + slot) * P, P)])
            sp.wait_ge(m.x_stored.sem, m.x_stored.at(16))

        @block.tensor
        def _(pe):
            norm_first_units(pe, m)
            with pe.Fori(1, units // 2) as j:
                for slot in range(2):
                    unit_matmuls(pe, m, slot, j, m.x_hi, m.x_lo)
            pe.wait_ge(m.pool_a.sem, m.pool_a.at(1))
            pe.wait_ge(m.set_free.sem, m.set_free.at(units + 1))
            for k in range(KT):
                last = product_parts(nc, [m.ps[c][0:M, 0:CH] for c in range(CHUNKS)], m.last_hi[:, k], m.last_lo[:, k],
                                     m.x_hi[:, k], m.x_lo[:, k], k == 0, k == KT - 1)
            last.then_inc(m.pe_a.sem, 1)

        @block.scalar
        def _(act):
            norm_act(act, m, m.g_mix[1])
            norm_root(act, m)

        @block.vector
        def _(dve):
            norm_dve(dve, m, m.g_mix[1])
            dve.wait_ge(m.inv_done.sem, m.inv_done.at(1))
            with dve.Fori(0, units // 2) as j:
                for slot in range(2):
                    u = j * 2 + slot
                    dve.wait_ge(m.unit_done.sem, m.unit_done.at(u + 1))
                    for c in range(CHUNKS):
                        last = nc.vector.tensor_tensor(
                            m.proj[:, bass.ds(u, 1), token_cols(c)].rearrange("p a n -> p (a n)"),
                            m.ps[3 * slot + c][:, 0:CH], m.inv_rms[:, token_cols(c)], ALU.mult)
                    last.then_inc(m.set_free.sem, 1)
            dve.wait_ge(m.pe_a.sem, m.pe_a.at(1))
            for c in range(CHUNKS):
                nc.vector.tensor_tensor(m.proj[0:M, KI, token_cols(c)], m.ps[c][0:M, 0:CH],
                                        m.inv_rms[0:M, token_cols(c)], ALU.mult)

    m.pe_a.passed(1)
    m.dma_a.passed(16)
    m.x_stored.passed(16)
    norm_passed(m)
    units_passed(m, units)


def phase_rows(m):
    nc = m.nc
    place_mixer(m)
    s = l1_tiles(m)
    r = Carver(m.resid[:])
    k_rows = r.take(TB, KVH * DH)
    ki_rows = r.take(TB, IDIM)
    smp = r.take(2 * KVH * DH + IDIM, parts=B)
    x = m.proj
    n_blocks = TB + 1
    with nc.Block() as block:

        @block.tensor
        def _(pe):
            for t in range(n_blocks):
                n = P if t < TB else B
                cols = slice(t * P, t * P + n)
                if t >= 2:
                    pe.wait_ge(m.dve_a.sem, m.dve_a.at(t - 1))
                    pe.wait_ge(m.act_a.sem, m.act_a.at(t - 1))
                for i, tile in enumerate((KT1, KT1 + 1, VT1, VT1 + 1)):
                    nc.tensor.transpose(m.ps[2 * (t % 2) + i // 2][0:n, (i % 2) * P:(i % 2 + 1) * P], x[:, tile, cols], m.ident[:])
                nc.tensor.transpose(m.ps[4 + t % 2][0:n, 0:IDIM + IH], x[0:IDIM + IH, KI, cols],
                                    m.ident[0:IDIM + IH, 0:IDIM + IH]).then_inc(m.pe_a.sem, 1)

        @block.vector
        def _(dve):
            V = nc.vector
            for t in range(TB):
                dve.wait_ge(m.pe_a.sem, m.pe_a.at(t + 1))
                V.tensor_copy(k_rows[:, t], m.ps[2 * (t % 2)][:, 0:KVH * DH])
                V.tensor_copy(ki_rows[:, t], m.ps[4 + t % 2][:, 0:IDIM])
                V.tensor_scalar(s.w_tok[:, t], m.ps[4 + t % 2][:, IDIM:IDIM + IH], (IDIM * IH) ** -0.5, None,
                                ALU.mult).then_inc(m.dve_a.sem, 1)
            dve.wait_ge(m.pe_a.sem, m.pe_a.at(n_blocks))
            V.tensor_copy(smp[:, 0:KVH * DH], m.ps[0][0:B, 0:KVH * DH])
            V.tensor_copy(smp[:, 2 * KVH * DH:], m.ps[4][0:B, 0:IDIM]).then_inc(m.dve_b.sem, 1)
            V.tensor_copy(x[IDIM:P, KI2, 0:T], x[0:IDIM, KI, 0:T])
            V.tensor_scalar(s.w_s, x[IDIM:IDIM + IH, KI, T:N], (IDIM * IH) ** -0.5, None, ALU.mult)
            for half in range(2):
                V.tensor_copy(s.qi_s[:, :, half::2].rearrange("p b t -> p t b"),
                              x[IDIM * half:IDIM * half + IDIM, QIT:QIT + 4, T:N])
            V.tensor_copy(s.q_s.rearrange("p b h -> p h b"), x[:, QT:QT + AH, T:N])

        @block.scalar
        def _(act):
            for t in range(TB):
                act.wait_ge(m.pe_a.sem, m.pe_a.at(t + 1))
                nc.scalar.copy(s.v_tok[:, t], m.ps[2 * (t % 2) + 1][:, 0:KVH * DH]).then_inc(m.act_a.sem, 1)
            act.wait_ge(m.pe_a.sem, m.pe_a.at(n_blocks))
            nc.scalar.copy(smp[:, KVH * DH:2 * KVH * DH], m.ps[1][0:B, 0:KVH * DH]).then_inc(m.act_b.sem, 1)

        @block.gpsimd
        def _(pool):
            for i in range(2):
                nc.gpsimd.memset(s.score[i], 0.0)
            nc.gpsimd.memset(s.sel, 1.0)
            pool.drain()
            for i in range(2):
                nc.gpsimd.affine_select(out=s.score[i], in_=s.score[i], compare_op=ALU.is_ge, fill=NEG, base=P * i,
                                        pattern=[[-1, score_width(i)]], channel_multiplier=1)
            nc.gpsimd.affine_select(out=s.sel, in_=s.sel, compare_op=ALU.is_equal, fill=0.0, base=0,
                                    pattern=[[-1, B], [0, 36]], channel_multiplier=1)

        @block.sync
        def _(sp):
            sp.dma_start(s.table, m.ins["page_table"].rearrange("(a b) j -> a (b j)", a=1)).then_inc(m.dma_a.sem, 16)
            sp.wait_ge(m.dve_a.sem, m.dve_a.at(TB))
            sp.dma_start(m.outs["p_k"].rearrange("b (t p) h d -> p (b t) (h d)", p=P), k_rows).then_inc(m.stored.sem, 16)
            sp.dma_start(m.outs["p_kidx"].rearrange("b (t p) d -> p (b t) d", p=P), ki_rows).then_inc(m.stored.sem, 16)
            sp.wait_ge(m.act_a.sem, m.act_a.at(TB))
            sp.dma_start(m.outs["p_v"].rearrange("b (t p) h d -> p (b t) (h d)", p=P), s.v_tok).then_inc(m.stored.sem, 16)
            sp.wait_ge(m.dve_b.sem, m.dve_b.at(1))
            sp.wait_ge(m.act_b.sem, m.act_b.at(1))
            for i, name in enumerate(("s_k", "s_v")):
                sp.dma_start(m.outs[name].rearrange("b a h d -> (b a) (h d)"), smp[:, KVH * DH * i:KVH * DH * (i + 1)]
                             ).then_inc(m.stored.sem, 16)
            sp.dma_start(m.outs["s_kidx"].rearrange("b a d -> (b a) d"), smp[:, 2 * KVH * DH:]).then_inc(m.stored.sem, 16)
            sp.wait_ge(m.stored.sem, m.stored.at(6 * 16))
            sp.wait_ge(m.dma_a.sem, m.dma_a.at(16))

    m.pe_a.passed(n_blocks)
    m.dve_a.passed(TB)
    m.act_a.passed(TB)
    m.dve_b.passed(1)
    m.act_b.passed(1)
    m.dma_a.passed(16)
    m.stored.passed(6 * 16)


def phase_index(m):
    nc = m.nc
    s = m.l1
    x = m.proj
    r = Carver(m.resid[:])
    rect = [r.take(1024) for _ in range(2)]
    steps = [(i, h) for i in range(2, TB) for h in range(IH)]
    with nc.Block() as block:

        @block.tensor
        def _(pe):
            for n, (i, h) in enumerate(steps):
                if n >= 4:
                    pe.wait_ge(m.act_a.sem, m.act_a.at(n - 3))
                half, w = h % 2, score_width(i)
                rows = slice(IDIM * half, IDIM * half + IDIM)
                for c in range(0, w, 512):
                    e = min(w, c + 512)
                    last = nc.tensor.matmul(m.ps[2 * (n % 4) + c // 512][:, 0:e - c], x[rows, QIT + h // 2, i * P:(i + 1) * P],
                                            x[rows, KI2 if half else KI, c:e], start=True, stop=True)
                last.then_inc(m.pe_a.sem, 1)

        @block.scalar
        def _(act):
            for n, (i, h) in enumerate(steps):
                act.wait_ge(m.pe_a.sem, m.pe_a.at(n + 1))
                if n >= 2:
                    act.wait_ge(m.dve_a.sem, m.dve_a.at(n - 1))
                w = score_width(i)
                for c in range(0, w, 512):
                    e = min(w, c + 512)
                    last = nc.scalar.activation(rect[n % 2][:, c:e], m.ps[2 * (n % 4) + c // 512][:, 0:e - c], ACT.Relu)
                last.then_inc(m.act_a.sem, 1)

        @block.vector
        def _(dve):
            V = nc.vector
            for n, (i, h) in enumerate(steps):
                dve.wait_ge(m.act_a.sem, m.act_a.at(n + 1))
                V.drain()
                w = score_width(i)
                if h == 0:
                    ins = V.tensor_scalar(s.score[i], rect[n % 2][:, 0:w], s.w_tok[:, i, h:h + 1], None, ALU.mult)
                else:
                    ins = V.scalar_tensor_tensor(s.score[i], rect[n % 2][:, 0:w], s.w_tok[:, i, h:h + 1], s.score[i],
                                                 ALU.mult, ALU.add)
                ins.then_inc(m.dve_a.sem, 1)

        @block.gpsimd
        def _(pool):
            for i in range(2, TB):
                pool.wait_ge(m.dve_a.sem, m.dve_a.at(IH * (i - 1)))
                diag = s.score[i][:, i * P:(i + 1) * P]
                nc.gpsimd.affine_select(out=diag, in_=diag, compare_op=ALU.is_ge, fill=NEG, base=0,
                                        pattern=[[-1, P]], channel_multiplier=1)

    m.pe_a.passed(len(steps))
    m.act_a.passed(len(steps))
    m.dve_a.passed(len(steps))


def phase_index_samples(m):
    nc = m.nc
    s = m.l1
    r = Carver(m.resid[:])
    pages = [r.take(PAGES, IDIM) for _ in range(2)]
    keys = r.take(PAST + 1, parts=IDIM)
    rect = r.take(PAST + 1, parts=IH)
    row = r.take(PAST + 1, parts=1)
    qi = r.take(IH, parts=IDIM)
    pieces = ((0, 512), (512, 1024), (1024, 1025))
    last_page = m.ins["cache_kidx"].shape[0] - 1
    with nc.Block() as block:

        @block.sync
        def _(sp):
            def load(b, slot, first):
                sem = m.dma_b if slot else m.dma_a
                if not first:
                    sp.wait_ge(m.pe_a.sem, m.pe_a.at(b - 1))
                for j in range(PAGES):
                    page = sp.value_load(s.table[0:1, b * PAGES + j:b * PAGES + j + 1], min_val=0, max_val=last_page)
                    sp.dma_start(pages[slot][:, j], m.ins["cache_kidx"][bass.ds(page, 1)].rearrange("a p d -> p (a d)")
                                 ).then_inc(sem.sem, 16)

            for b in range(B):
                load(b, b % 2, b < 2)
            sp.wait_ge(m.dma_c.sem, m.dma_c.at(16 * B))
            sp.dma_start(s.samples[:, 0:PAST + 1], m.score_dram).then_inc(m.dma_d.sem, 16)
            sp.wait_ge(m.dma_d.sem, m.dma_d.at(16))

        @block.tensor
        def _(pe):
            def sample(b, slot, first):
                sem = m.dma_b if slot else m.dma_a
                pe.wait_ge(sem.sem, sem.at((b - slot) * (8 * PAGES) + 16 * PAGES))
                if not first:
                    pe.wait_ge(m.act_a.sem, m.act_a.at(b))
                for j in range(PAGES):
                    last = nc.tensor.transpose(m.ps[j // 4][0:IDIM, (j % 4) * PAGE:(j % 4 + 1) * PAGE], pages[slot][:, j], m.ident[:])
                last.then_inc(m.pe_a.sem, 1)
                pe.wait_ge(m.act_a.sem, m.act_a.at(b + 1))
                pe.wait_ge(m.dve_a.sem, m.dve_a.at(b + 1))
                for n, (c, e) in enumerate(pieces):
                    last = nc.tensor.matmul(m.ps[2 + n][0:IH, 0:e - c], qi, keys[:, c:e], start=True, stop=True)
                last.then_inc(m.pe_b.sem, 1)
                pe.wait_ge(m.dve_b.sem, m.dve_b.at(b + 1))
                if not first:
                    pe.wait_ge(m.act_b.sem, m.act_b.at(b))
                for n, (c, e) in enumerate(pieces):
                    last = nc.tensor.matmul(m.ps[5 + n][0:1, 0:e - c], m.ones[0:IH, 0:1], rect[:, c:e], start=True, stop=True)
                last.then_inc(m.pe_c.sem, 1)

            for b in range(B):
                sample(b, b % 2, b == 0)

        @block.scalar
        def _(act):
            def sample(b, first):
                act.wait_ge(m.pe_a.sem, m.pe_a.at(b + 1))
                if not first:
                    act.wait_ge(m.pe_b.sem, m.pe_b.at(b))
                for half in range(2):
                    last = nc.scalar.copy(keys[:, 512 * half:512 * half + 512], m.ps[half][0:IDIM, :])
                last.then_inc(m.act_a.sem, 1)
                act.wait_ge(m.pe_c.sem, m.pe_c.at(b + 1))
                if not first:
                    act.wait_ge(m.dma_c.sem, m.dma_c.at(b * 16))
                for n, (c, e) in enumerate(pieces):
                    last = nc.scalar.copy(row[:, c:e], m.ps[5 + n][0:1, 0:e - c])
                last.then_inc(m.act_b.sem, 1)
                act.wait_ge(m.act_b.sem, m.act_b.at(b + 1))
                act.dma_start(m.score_dram[bass.ds(b, 1)], row).then_inc(m.dma_c.sem, 16)

            sample(0, True)
            with act.Fori(1, B) as b:
                sample(b, False)

        @block.vector
        def _(dve):
            V = nc.vector

            def sample(b, first):
                if not first:
                    dve.wait_ge(m.pe_b.sem, m.pe_b.at(b))
                V.tensor_copy(keys[:, PAST:PAST + 1], m.proj[0:IDIM, KI, bass.ds(b + T, 1)])
                V.tensor_copy(qi, s.qi_s[:, bass.ds(b, 1), :].rearrange("p a h -> p (a h)")).then_inc(m.dve_a.sem, 1)
                dve.wait_ge(m.pe_b.sem, m.pe_b.at(b + 1))
                if not first:
                    dve.wait_ge(m.pe_c.sem, m.pe_c.at(b))
                for n, (c, e) in enumerate(pieces):
                    last = V.tensor_scalar(rect[:, c:e], m.ps[2 + n][0:IH, 0:e - c], 0.0, s.w_s[:, bass.ds(b, 1)],
                                           ALU.max, ALU.mult)
                last.then_inc(m.dve_b.sem, 1)

            sample(0, True)
            with dve.Fori(1, B) as b:
                sample(b, False)

    m.dma_a.passed(16 * PAGES * B // 2)
    m.dma_b.passed(16 * PAGES * B // 2)
    m.dma_c.passed(16 * B)
    m.dma_d.passed(16)
    for q in (m.pe_a, m.pe_b, m.pe_c, m.act_a, m.act_b, m.dve_a, m.dve_b):
        q.passed(B)


def phase_topk(m):
    nc = m.nc
    s = m.l1
    r = Carver(m.resid[:])
    sets = [(0, s.samples[:, 0:PAST + 1], B)] + [(i, s.score[i], P) for i in range(2, TB)]
    by_act = (2, 3, 5, 7)
    marks = [r.take(x.shape[1]) for _, x, _ in sets]
    junk = r.take(PAST + 1)
    equal = r.take(PAST + 1)
    rank = marks[0]
    SIGN = -2 ** 31
    with nc.Block() as block:

        @block.scalar
        def _(act):
            with act.Fori(0, 32) as step:
                act.wait_ge(m.dve_a.sem, m.dve_a.at(step + 1))
                for mark, (i, x, n) in zip(marks, sets):
                    if i in by_act:
                        last = nc.scalar.activation(mark, x, ACT.Sign, bias=s.cand[:, i:i + 1], scale=-1.0,
                                                    accum_out=s.cnt[:, i:i + 1])
                last.then_inc(m.act_a.sem, 1)

        @block.vector
        def _(dve):
            V = nc.vector
            V.memset(s.prefix, 0)
            V.memset(s.bit, SIGN)
            V.memset(s.cnt, 0.0)
            V.memset(s.limit, 0.0)
            V.drain()
            for i, x, n in sets:
                w = x.shape[1]
                V.memset(s.limit[:, i:i + 1], w - 2 * TOPK + 0.5 if i in by_act else w - TOPK + 0.5)
            V.drain()
            with dve.Fori(0, 32) as step:
                V.tensor_tensor(s.key, s.prefix, s.bit, ALU.bitwise_or)
                V.drain()
                V.tensor_scalar(s.flip, s.key, 31, -1, ALU.arith_shift_right, ALU.bitwise_xor)
                V.drain()
                V.tensor_scalar(s.flip, s.flip, SIGN, None, ALU.bitwise_or)
                V.drain()
                V.tensor_tensor(s.cand.bitcast(I32), s.key, s.flip, ALU.bitwise_xor).then_inc(m.dve_a.sem, 1)
                V.drain()
                for mark, (i, x, n) in zip(marks, sets):
                    if i not in by_act:
                        V.tensor_scalar(mark[0:n], x, s.cand[0:n, i:i + 1], 0.0, ALU.is_lt, ALU.add,
                                        accum_out=s.cnt[0:n, i:i + 1])
                V.drain()
                dve.wait_ge(m.act_a.sem, m.act_a.at(step + 1))
                V.tensor_tensor(s.need, s.cnt, s.limit, ALU.subtract)
                V.drain()
                V.tensor_scalar(s.flip, s.need, 0.0, -1.0, ALU.is_le, ALU.mult)
                V.drain()
                V.tensor_tensor(s.key, s.flip, s.bit, ALU.bitwise_and)
                V.drain()
                V.tensor_tensor(s.prefix, s.prefix, s.key, ALU.bitwise_or)
                V.tensor_scalar(s.flip, s.bit, 1, None, ALU.logical_shift_right)
                V.drain()
                V.tensor_copy(s.bit, s.flip)
                V.drain()
            V.tensor_scalar(s.flip, s.prefix, 31, -1, ALU.arith_shift_right, ALU.bitwise_xor)
            V.drain()
            V.tensor_scalar(s.flip, s.flip, SIGN, None, ALU.bitwise_or)
            V.drain()
            V.tensor_tensor(s.tau.bitcast(I32), s.prefix, s.flip, ALU.bitwise_xor)
            V.memset(s.cnt, 0.0)
            V.memset(s.cand, 0.0)
            V.drain()
            for mark, (i, x, n) in zip(marks, sets):
                if i in by_act:
                    w = x.shape[1]
                    tau = s.tau[:, i:i + 1]
                    V.tensor_scalar(mark, x, tau, 0.0, ALU.is_gt, ALU.add, accum_out=s.cnt[:, i:i + 1])
                    V.tensor_scalar(junk[:, 0:w], x, tau, -3e38, ALU.is_le, ALU.mult)
                    V.drain()
                    V.scalar_tensor_tensor(junk[:, 0:w], x, -1.0, junk[:, 0:w], ALU.mult, ALU.add)
                    V.drain()
                    V.reduce_max(s.cand[:, i:i + 1], junk[:, 0:w], AX_X)
                    V.drain()
            V.tensor_scalar(s.need, s.cand, -1.0, None, ALU.mult)
            V.tensor_scalar(s.flip, s.cnt, TOPK - 0.5, -1.0, ALU.is_ge, ALU.mult)
            V.drain()
            V.tensor_tensor(s.key, s.tau.bitcast(I32), s.need.bitcast(I32), ALU.bitwise_xor)
            V.drain()
            V.tensor_tensor(s.key, s.key, s.flip, ALU.bitwise_and)
            V.drain()
            V.tensor_tensor(s.tau.bitcast(I32), s.tau.bitcast(I32), s.key, ALU.bitwise_xor)
            V.drain()
            for i, x, n in sets:
                w = x.shape[1]
                tau, cnt, need = s.tau[0:n, i:i + 1], s.cnt[0:n, i:i + 1], s.need[0:n, i:i + 1]
                V.tensor_scalar(junk[0:n, 0:w], x, tau, 0.0, ALU.is_gt, ALU.add, accum_out=cnt)
                V.tensor_scalar(equal[0:n, 0:w], x, tau, None, ALU.is_equal)
                V.drain()
                V.tensor_scalar(need, cnt, -1.0, float(TOPK), ALU.mult, ALU.add)
                V.tensor_tensor_scan(rank[0:n, 0:w], equal[0:n, 0:w], equal[0:n, 0:w], 0.0, ALU.add, ALU.max)
                V.drain()
                V.scalar_tensor_tensor(rank[0:n, 0:w], rank[0:n, 0:w], need, equal[0:n, 0:w], ALU.is_le, ALU.mult)
                V.drain()
                V.tensor_tensor(rank[0:n, 0:w], rank[0:n, 0:w], junk[0:n, 0:w], ALU.add)
                V.drain()
                V.tensor_scalar(x, rank[0:n, 0:w], -NEG, NEG, ALU.mult, ALU.add)
                V.drain()

    m.dve_a.passed(32)
    m.act_a.passed(32)


def phase_attend(m):
    nc = m.nc
    s = m.l1
    scale = DH ** -0.5
    r = Carver(m.resid[:])
    q = [r.take(P) for _ in range(2)]
    masked = [r.take(T) for _ in range(2)]
    probs_t = r.take(TB, P)
    o_tok = [r.take(DH) for _ in range(2)]
    ps_s = [m.ps_pair[0], m.ps_pair[1]]
    ps_t = m.ps_pair[2]
    ps_o, ps_ot = m.ps[6], m.ps[7]
    st = s.stat
    k_t = m.proj
    with nc.Block() as block:
        n_units = TB * AH

        @block.sync
        def _(sp):
            def load(n, h, slot, i, first):
                if not first:
                    sp.wait_ge(m.pe_a.sem, m.pe_a.at(n - 1))
                sem = m.dma_b if slot else m.dma_a
                sp.dma_start(q[slot], flat(m.proj[:, bass.ds(h, 1), i * P:(i + 1) * P])).then_inc(sem.sem, 16)

            for i in range(TB):
                if i == 0:
                    load(0, 0, 0, 0, True)
                    load(1, 1, 1, 0, True)
                with sp.Fori(1 if i == 0 else 0, AH // 2) as j:
                    for slot in range(2):
                        load(i * AH + j * 2 + slot, j * 2 + slot, slot, i, False)

        @block.tensor
        def _(pe):
            def scores(n, g, slot, i, first):
                sem = m.dma_b if slot else m.dma_a
                pe.wait_ge(sem.sem, sem.at((n - slot) * 8 + 16))
                if not first:
                    pe.wait_ge(m.dve_a.sem, m.dve_a.at(n - 1))
                w = score_width(i)
                for c in range(0, w, 512):
                    e = min(w, c + 512)
                    last = nc.tensor.matmul(ps_s[slot][:, c:e], q[slot], flat(k_t[:, bass.ds(g + KT1, 1), c:e]),
                                            start=True, stop=True)
                last.then_inc(m.pe_a.sem, 1)

            def turn_probs(n, slot, i, first):
                pe.wait_ge(m.act_a.sem, m.act_a.at(n + 1))
                if not first:
                    pe.wait_ge(m.act_b.sem, m.act_b.at(n))
                    pe.wait_ge(m.dve_b.sem, m.dve_b.at(n))
                for b in range(i + 1):
                    last = nc.tensor.transpose(ps_t[:, b * P:(b + 1) * P], masked[slot][:, b * P:(b + 1) * P], m.ident[:])
                last.then_inc(m.pe_b.sem, 1)

            def values(n, g, i, first):
                pe.wait_ge(m.act_b.sem, m.act_b.at(n + 1))
                pe.wait_ge(m.dve_b.sem, m.dve_b.at(n + 1))
                if not first:
                    pe.wait_ge(m.dve_c.sem, m.dve_c.at(n))
                for b in range(i + 1):
                    last = nc.tensor.matmul(ps_o[:, 0:DH], probs_t[:, b], s.v_tok[:, b, bass.ds(g * DH, DH)],
                                            start=(b == 0), stop=(b == i))
                last.then_inc(m.pe_c.sem, 1)

            def turn(n, slot, first):
                pe.wait_ge(m.dve_c.sem, m.dve_c.at(n + 1))
                if not first:
                    pe.wait_ge(m.act_c.sem, m.act_c.at(n))
                nc.tensor.transpose(ps_ot[:, 0:P], o_tok[slot], m.ident[:]).then_inc(m.pe_d.sem, 1)

            for i in range(TB):
                n0 = i * AH
                scores(n0, 0, 0, i, i == 0)
                scores(n0 + 1, 0, 1, i, i == 0)
                turn_probs(n0, 0, i, i == 0)
                scores(n0 + 2, 0, 0, i, False)
                values(n0, 0, i, i == 0)
                turn(n0, 0, i == 0)
                turn_probs(n0 + 1, 1, i, False)
                scores(n0 + 3, 0, 1, i, False)
                values(n0 + 1, 0, i, False)
                turn(n0 + 1, 1, False)
                with pe.Fori(1, AH // 2 - 1) as j:
                    for slot in range(2):
                        n = n0 + j * 2 + slot
                        turn_probs(n, slot, i, False)
                        scores(n + 2, (j + 1) // 2, slot, i, False)
                        values(n, j // 2, i, False)
                        turn(n, slot, False)
                for slot in range(2):
                    n = n0 + AH - 2 + slot
                    turn_probs(n, slot, i, False)
                    values(n, KVH - 1, i, False)
                    turn(n, slot, False)

        @block.vector
        def _(dve):
            V = nc.vector

            def mask(n, slot, i, first):
                w = score_width(i)
                a = 4 * slot
                dve.wait_ge(m.pe_a.sem, m.pe_a.at(n + 1))
                V.memset(m.mark[:, 0:1], 0.0)
                if not first:
                    dve.wait_ge(m.pe_b.sem, m.pe_b.at(n - 1))
                V.memset(m.mark[:, 1:2], 0.0)
                V.tensor_tensor_reduce(masked[slot][:, 0:w], ps_s[slot][:, 0:w], s.score[i], 1.0, -3e38, ALU.add, ALU.max,
                                       st[:, a:a + 1])
                V.drain()
                V.tensor_scalar(st[:, a + 1:a + 2], st[:, a:a + 1], -scale, None, ALU.mult).then_inc(m.dve_a.sem, 1)

            def copy_t(n, slot, i):
                half = (i + 1) // 2
                dve.wait_ge(m.pe_b.sem, m.pe_b.at(n + 1))
                V.memset(m.mark[:, 2:3], 0.0)
                ins = V.tensor_copy(probs_t[:, 0:half].rearrange("p a n -> p (a n)"), ps_t[:, 0:half * P]) if half else \
                    V.memset(m.mark[:, 3:4], 0.0)
                ins.then_inc(m.dve_b.sem, 1)

            def norm(n, slot):
                a = 4 * slot
                V.reciprocal(st[:, a + 3:a + 4], st[:, a + 2:a + 3])
                V.drain()
                dve.wait_ge(m.pe_c.sem, m.pe_c.at(n + 1))
                V.tensor_scalar(o_tok[slot], ps_o[:, 0:DH], st[:, a + 3:a + 4], None, ALU.mult).then_inc(m.dve_c.sem, 1)

            for i in range(TB):
                n0 = i * AH
                mask(n0, 0, i, i == 0)
                mask(n0 + 1, 1, i, i == 0)
                with dve.Fori(0, AH // 2 - 1) as j:
                    for slot in range(2):
                        n = n0 + j * 2 + slot
                        copy_t(n, slot, i)
                        norm(n, slot)
                        mask(n + 2, slot, i, False)
                for slot in range(2):
                    n = n0 + AH - 2 + slot
                    copy_t(n, slot, i)
                    norm(n, slot)

        @block.scalar
        def _(act):
            def exps(n, slot, i):
                a = 4 * slot
                w = score_width(i)
                act.wait_ge(m.dve_a.sem, m.dve_a.at(n + 1))
                nc.scalar.activation(masked[slot][:, 0:w], masked[slot][:, 0:w], ACT.Exp, bias=st[:, a + 1:a + 2],
                                     scale=scale, accum_out=st[:, a + 2:a + 3]).then_inc(m.act_a.sem, 1)

            def rest(n, h, slot, i):
                half = (i + 1) // 2
                act.wait_ge(m.pe_b.sem, m.pe_b.at(n + 1))
                act.wait_ge(m.dve_b.sem, m.dve_b.at(n + 1))
                nc.scalar.copy(probs_t[:, half:i + 1].rearrange("p a n -> p (a n)"), ps_t[:, half * P:(i + 1) * P]
                               ).then_inc(m.act_b.sem, 1)
                act.wait_ge(m.pe_d.sem, m.pe_d.at(n + 1))
                nc.scalar.copy(flat(m.normed[:, bass.ds(h, 1), i * P:(i + 1) * P]), ps_ot[:, 0:P]).then_inc(m.act_c.sem, 1)

            for i in range(TB):
                n0 = i * AH
                exps(n0, 0, i)
                exps(n0 + 1, 1, i)
                with act.Fori(0, AH // 2 - 1) as j:
                    for slot in range(2):
                        h = j * 2 + slot
                        rest(n0 + h, h, slot, i)
                        exps(n0 + h + 2, slot, i)
                for slot in range(2):
                    rest(n0 + AH - 2 + slot, AH - 2 + slot, slot, i)

    m.dma_a.passed(16 * n_units // 2)
    m.dma_b.passed(16 * n_units // 2)
    for x in (m.pe_a, m.pe_b, m.pe_c, m.pe_d, m.act_a, m.act_b, m.act_c, m.dve_a, m.dve_b, m.dve_c):
        x.passed(n_units)


def phase_attend_samples(m):
    nc = m.nc
    s = m.l1
    scale = DH ** -0.5
    R = 36
    r = Carver(m.resid[:])
    k_pages = [r.take(PAGES, KVH * DH) for _ in range(2)]
    v_pages = [r.take(PAGES, KVH * DH) for _ in range(2)]
    c = Carver(m.hidden[:])
    key_slots = [c.take(KVH, PAST + 1) for _ in range(2)]
    masked = c.take(PAST + 1, parts=R)
    probs_t = c.take(PAGES, R)
    new_t = c.take(R, parts=1)
    v_news = [c.take(KVH * DH, parts=1) for _ in range(2)]
    q_slots = [c.take(AH) for _ in range(2)]
    sel_slots = [c.take(R, parts=B) for _ in range(2)]
    pieces = ((0, 512), (512, 1024), (1024, 1025))
    n_pages = m.ins["cache_k"].shape[0]
    st = s.stat
    with nc.Block() as block:

        @block.sync
        def _(sp):
            def load(b, first):
                slot = b % 2
                k_page, v_page, v_new = k_pages[slot], v_pages[slot], v_news[slot]
                k_sem, v_sem = (m.dma_c, m.dma_d) if slot else (m.dma_a, m.dma_b)
                for j in range(PAGES):
                    page = sp.value_load(s.table[0:1, b * PAGES + j:b * PAGES + j + 1], min_val=0, max_val=n_pages - 1)
                    if j == 0 and not first:
                        sp.wait_ge(m.pe_a.sem, m.pe_a.at(b - 1))
                        sp.wait_ge(m.pe_d.sem, m.pe_d.at(b - 1))
                    sp.dma_start(k_page[:, j], m.ins["cache_k"][bass.ds(page, 1)].rearrange("a p h d -> p (a h d)")
                                 ).then_inc(k_sem.sem, 16)
                    sp.dma_start(v_page[:, j], m.ins["cache_v"][bass.ds(page, 1)].rearrange("a p h d -> p (a h d)")
                                 ).then_inc(v_sem.sem, 16)
                sp.dma_start(v_new, m.outs["s_v"][bass.ds(b, 1)].rearrange("b a h d -> (b a) (h d)")).then_inc(v_sem.sem, 16)

            for b in range(B):
                load(b, b < 2)

        @block.tensor
        def _(pe):
            def turn_keys(b):
                k_page, k_sem = k_pages[b % 2], m.dma_c if b % 2 else m.dma_a
                pe.wait_ge(k_sem.sem, k_sem.at((b // 2 + 1) * 16 * PAGES))
                if b > 0:
                    pe.wait_ge(m.act_a.sem, m.act_a.at(b))
                for g in range(KVH):
                    for j in range(PAGES):
                        last = nc.tensor.transpose(m.ps_pair[g][:, j * PAGE:(j + 1) * PAGE],
                                                   k_page[:, j, g * DH:(g + 1) * DH], m.ident[:])
                last.then_inc(m.pe_a.sem, 1)

            def sample(b, first):
                slot = b % 2
                v_page, v_new, v_sem = v_pages[slot], v_news[slot], m.dma_d if slot else m.dma_b
                keys, q, sel = key_slots[slot], q_slots[slot], sel_slots[slot]
                pe.wait_ge(m.act_a.sem, m.act_a.at(b + 1))
                pe.wait_ge(m.dve_a.sem, m.dve_a.at(b + 1))
                if not first:
                    pe.wait_ge(m.dve_c.sem, m.dve_c.at(b))
                for n, (c0, e) in enumerate(pieces):
                    ps = m.ps[4 + n][:, 0:e - c0]
                    nc.tensor.matmul(ps[0:R], sel, s.samples[:, c0:e], start=True, stop=False, skip_group_check=True)
                    for g in range(KVH):
                        last = nc.tensor.matmul(ps[32 * g:32 * g + AG], q[:, g * AG:(g + 1) * AG], keys[:, g, c0:e],
                                                start=False, stop=True, skip_group_check=True)
                last.then_inc(m.pe_b.sem, 1)
                if b < B - 1:
                    turn_keys(b + 1)
                if not first:
                    pe.wait_ge(m.act_c.sem, m.act_c.at(b))
                pe.wait_ge(m.dve_b.sem, m.dve_b.at(b + 1))
                for j in range(PAGES):
                    nc.tensor.transpose(m.ps[7][:, j * R:(j + 1) * R], masked[:, j * PAGE:(j + 1) * PAGE], m.ident[0:R, 0:R])
                nc.tensor.transpose(m.ps[7][0:1, PAGES * R:(PAGES + 1) * R], masked[:, PAST:PAST + 1],
                                    m.ident[0:R, 0:R]).then_inc(m.pe_c.sem, 1)
                pe.wait_ge(m.dve_d.sem, m.dve_d.at(b + 1))
                pe.wait_ge(v_sem.sem, v_sem.at((b // 2 + 1) * 16 * (PAGES + 1)))
                for g in range(KVH):
                    rows = slice(32 * g, 32 * g + AG)
                    out = m.ps[7][:, 384 + AG * g:384 + AG * (g + 1)]
                    for j in range(PAGES):
                        nc.tensor.matmul(out, v_page[:, j, g * DH:(g + 1) * DH], probs_t[:, j, rows], start=(j == 0), stop=False)
                    last = nc.tensor.matmul(out, v_new[:, g * DH:(g + 1) * DH], new_t[:, rows], start=False, stop=True)
                last.then_inc(m.pe_d.sem, 1)

            turn_keys(0)
            for b in range(B):
                sample(b, b == 0)

        @block.scalar
        def _(act):
            def copy_keys(b, slot, first):
                act.wait_ge(m.pe_a.sem, m.pe_a.at(b + 1))
                if not first:
                    act.wait_ge(m.pe_b.sem, m.pe_b.at(b - 1))
                for g in range(KVH):
                    last = nc.scalar.copy(key_slots[slot][:, g, 0:PAST], m.ps_pair[g][:])
                last.then_inc(m.act_a.sem, 1)

            def sample(b, slot, first=False, last=False):
                act.wait_ge(m.dve_c.sem, m.dve_c.at(b + 1))
                nc.scalar.activation(masked, masked, ACT.Exp, bias=st[0:R, 1:2], scale=scale,
                                     accum_out=st[0:R, 2:3]).then_inc(m.act_b.sem, 1)
                if not last:
                    copy_keys(b + 1, 1 - slot, first)
                act.wait_ge(m.pe_d.sem, m.pe_d.at(b + 1))
                nc.scalar.copy(m.normed[:, :, bass.ds(b + T, 1)].rearrange("p h a -> p (h a)"), m.ps[7][:, 384:384 + AH]
                               ).then_inc(m.act_c.sem, 1)

            copy_keys(0, 0, True)
            sample(0, 0, first=True)
            with act.Fori(0, B // 2 - 1) as i:
                for slot in (1, 0):
                    sample(i * 2 + 2 - slot, slot)
            sample(B - 1, 1, last=True)

        @block.vector
        def _(dve):
            V = nc.vector

            def fill(b, slot, first):
                keys, q, sel = key_slots[slot], q_slots[slot], sel_slots[slot]
                if not first:
                    dve.wait_ge(m.pe_b.sem, m.pe_b.at(b - 1))
                V.tensor_copy(keys[:, :, PAST:PAST + 1], m.proj[:, KT1:KT1 + KVH, bass.ds(b + T, 1)])
                V.tensor_copy(q, s.q_s[:, bass.ds(b, 1), :].rearrange("p a h -> p (a h)"))
                V.tensor_copy(sel, s.sel[:, bass.ds(b, 1), :].rearrange("p a h -> p (a h)")).then_inc(m.dve_a.sem, 1)

            def sample(b, slot, first=False, last=False):
                if not last:
                    fill(b + 1, 1 - slot, first)
                dve.wait_ge(m.pe_b.sem, m.pe_b.at(b + 1))
                if not first:
                    dve.wait_ge(m.pe_c.sem, m.pe_c.at(b))
                for n, (c0, e) in enumerate(pieces):
                    V.tensor_copy(masked[:, c0:e], m.ps[4 + n][0:R, 0:e - c0])
                V.drain()
                V.reduce_max(st[0:R, 0:1], masked, AX_X)
                V.drain()
                V.tensor_scalar(st[0:R, 1:2], st[0:R, 0:1], -scale, None, ALU.mult).then_inc(m.dve_c.sem, 1)
                dve.wait_ge(m.act_b.sem, m.act_b.at(b + 1))
                V.reciprocal(st[0:R, 3:4], st[0:R, 2:3])
                V.drain()
                V.tensor_scalar(masked, masked, st[0:R, 3:4], None, ALU.mult).then_inc(m.dve_b.sem, 1)
                dve.wait_ge(m.pe_c.sem, m.pe_c.at(b + 1))
                if not first:
                    dve.wait_ge(m.pe_d.sem, m.pe_d.at(b))
                V.tensor_copy(new_t, m.ps[7][0:1, PAGES * R:(PAGES + 1) * R])
                V.tensor_copy(probs_t.rearrange("p j r -> p (j r)"), m.ps[7][:, 0:PAGES * R]).then_inc(m.dve_d.sem, 1)

            fill(0, 0, True)
            sample(0, 0, first=True)
            with dve.Fori(0, B // 2 - 1) as i:
                for slot in (1, 0):
                    sample(i * 2 + 2 - slot, slot)
            sample(B - 1, 1, last=True)

    for x in (m.dma_a, m.dma_c):
        x.passed(16 * PAGES * B // 2)
    for x in (m.dma_b, m.dma_d):
        x.passed(16 * (PAGES + 1) * B // 2)
    for x in (m.pe_a, m.pe_b, m.pe_c, m.pe_d, m.act_a, m.act_b, m.act_c, m.dve_a, m.dve_b, m.dve_c, m.dve_d):
        x.passed(B)


PHASES = [phase_load_x, phase_in0, phase_s5_params, phase_s5_states, phase_s5_outputs, phase_s5_glu,
          phase_ml_gates, phase_ml_chunks, phase_ml_samples,
          lambda m: phase_out(m, "w_out0"), lambda m: phase_mlp(m, 0),
          phase_in1, phase_rows, phase_index, phase_index_samples, phase_topk, phase_attend, phase_attend_samples,
          lambda m: phase_out(m, "w_out1"), lambda m: phase_mlp(m, 1), phase_final]


def program(nc, ins, outs):
    with ExitStack() as ctx:
        m = Machine(ctx, nc, ins, outs)
        m.spill = nc.dram_tensor("resid_spill", [P, KT, N], F32).ap()
        m.s5_dram = nc.dram_tensor("s5_by_channel", [S5_W, N], F32).ap()
        m.score_dram = nc.dram_tensor("sample_scores", [B, PAST + 1], F32).ap()
        for phase in PHASES:
            phase(m)
        for stack in (m.left, m.mixed, m.right):
            stack.close()


_INS = ["x_prompt", "x_sample", "state_s5_re", "state_s5_im", "state_mlstm_c", "state_mlstm_n", "state_mlstm_m",
        "cache_k", "cache_v", "cache_kidx", "page_table", "norm_mix", "norm_mlp", "norm_final", "w_in0",
        "s5_lam_re", "s5_lam_im", "s5_log_dt", "s5_b_re", "s5_b_im", "s5_c_re", "s5_c_im", "s5_d", "w_glu",
        "b_glu", "b_igate", "b_fgate", "w_out0", "w_in1", "w_out1", "w_up", "w_down"]
_OUTS = [("y_prompt", (1, 1024, 1024)), ("y_sample", (8, 1, 1024)),
         ("p_s5_re", (1, 32, 64)), ("p_s5_im", (1, 32, 64)), ("p_c", (1, 4, 128, 128)), ("p_n", (1, 4, 128)),
         ("p_m", (1, 4)), ("p_k", (1, 1024, 2, 128)), ("p_v", (1, 1024, 2, 128)), ("p_kidx", (1, 1024, 64)),
         ("s_s5_re", (8, 32, 64)), ("s_s5_im", (8, 32, 64)), ("s_c", (8, 4, 128, 128)), ("s_n", (8, 4, 128)),
         ("s_m", (8, 4)), ("s_k", (8, 1, 2, 128)), ("s_v", (8, 1, 2, 128)), ("s_kidx", (8, 1, 64))]


def kernel(**inputs):
    import numpy as _np
    import concourse.bacc as _bacc
    from concourse import mybir as _mybir
    from concourse.bass_utils import run_bass_kernel_spmd as _run

    nc = _bacc.Bacc("TRN2", target_bir_lowering=False, num_devices=1)
    arrays, ins, outs = {}, {}, {}
    for name in _INS:
        a = _np.ascontiguousarray(inputs[name])
        arrays[f"in_{name}"] = a
        ins[name] = nc.dram_tensor(f"in_{name}", a.shape, _mybir.dt.from_np(a.dtype), kind="ExternalInput").ap()
    for name, shape in _OUTS:
        outs[name] = nc.dram_tensor(f"out_{name}", shape, _mybir.dt.float32, kind="ExternalOutput").ap()
    program(nc, ins, outs)
    r = _run(nc, [arrays], core_ids=[0])
    return tuple(r.results[0][f"out_{name}"] for name, _ in _OUTS)
```
